# Optimizing a Trainium2 kernel written in Bass

```python
import math
import jax, jax.numpy as jnp
from jax import lax
import numpy as np

D_MODEL = 1024
BATCH = 1
SEQ = 1024
DEPTH = 1

CHUNK = 64
POOL_WIDTH = 512
POOL_WINDOWS = (2, 4, 8, 16)
POOL_GROUPS = len(POOL_WINDOWS)
POOL_GROUP_DIM = POOL_WIDTH // POOL_GROUPS
HEAD_DIM = 64
N_Q_HEADS = 8
N_KV_HEADS = 2
GQA_GROUP = N_Q_HEADS // N_KV_HEADS
WINDOW = 128
WINDOW_CHUNKS = WINDOW // CHUNK
ROPE_THETA = 500000.0
ROT_DIM = HEAD_DIM // 4
Q_WIDTH = N_Q_HEADS * HEAD_DIM
KV_WIDTH = N_KV_HEADS * HEAD_DIM
IN_WIDTH = POOL_WIDTH + Q_WIDTH + 2 * KV_WIDTH + 2 * D_MODEL
SPLITS = (POOL_WIDTH,
          POOL_WIDTH + Q_WIDTH,
          POOL_WIDTH + Q_WIDTH + KV_WIDTH,
          POOL_WIDTH + Q_WIDTH + 2 * KV_WIDTH,
          POOL_WIDTH + Q_WIDTH + 2 * KV_WIDTH + D_MODEL)
PEER_HEADS = 8
PEER_QDIM = 256
PEER_HALF = PEER_QDIM // 2
N_KEYS = 128
N_EXPERTS = N_KEYS * N_KEYS
PEER_TOPK = 16
PEER_BLOCK = 128
EPS = 1e-6

kernel_name = "chunk_causal_pool_swa_peer_hybrid"

def rms_norm(x, g):
    xf = x.astype(jnp.float32)
    r = lax.rsqrt(jnp.mean(xf * xf, axis=-1, keepdims=True) + EPS)
    return (xf * r * g.astype(jnp.float32)).astype(x.dtype)

def rope_tables(seq):
    pos = jnp.arange(seq, dtype=jnp.float32)
    inv = ROPE_THETA ** (-jnp.arange(0, ROT_DIM, 2, dtype=jnp.float32) / ROT_DIM)
    ang = pos[:, None] * inv[None, :]
    return jnp.cos(ang)[:, None, :], jnp.sin(ang)[:, None, :]

def apply_partial_rope(t, cos, sin):
    tf = t.astype(jnp.float32)
    half = ROT_DIM // 2
    r1, r2, rest = tf[..., :half], tf[..., half:ROT_DIM], tf[..., ROT_DIM:]
    out = jnp.concatenate([r1 * cos - r2 * sin, r2 * cos + r1 * sin, rest], axis=-1)
    return out.astype(t.dtype)

def pool_mixer(p, w_grp, scale):
    B, S, _ = p.shape
    pf = p.astype(jnp.float32)
    cs = jnp.concatenate([jnp.zeros((B, 1, POOL_WIDTH), jnp.float32),
                          jnp.cumsum(pf, axis=1)], axis=1)
    t = jnp.arange(S)
    outs = []
    for g, w in enumerate(POOL_WINDOWS):
        sl = slice(g * POOL_GROUP_DIM, (g + 1) * POOL_GROUP_DIM)
        c = cs[..., sl]
        lo = jnp.maximum(t + 1 - w, 0)
        cnt = (t + 1 - lo).astype(jnp.float32)[None, :, None]
        mean = (c[:, t + 1] - c[:, lo]) / cnt
        pooled = (mean - pf[..., sl]).astype(p.dtype)
        outs.append(jnp.einsum('bsc,cd->bsd', pooled, w_grp[g]))
    return jnp.concatenate(outs, axis=-1) * scale

def window_attention(q, k, v, sinks):
    B, S = q.shape[:2]
    n_c = S // CHUNK
    qc = q.reshape(B, n_c, CHUNK, N_KV_HEADS, GQA_GROUP, HEAD_DIM)
    kc = k.reshape(B, n_c, CHUNK, N_KV_HEADS, HEAD_DIM)
    vc = v.reshape(B, n_c, CHUNK, N_KV_HEADS, HEAD_DIM)
    pad = ((0, 0), (1, 0), (0, 0), (0, 0), (0, 0))
    kb = jnp.concatenate([jnp.pad(kc[:, :-1], pad), kc], axis=2)
    vb = jnp.concatenate([jnp.pad(vc[:, :-1], pad), vc], axis=2)
    scores = jnp.einsum('bcqhgd,bckhd->bchgqk', qc, kb).astype(jnp.float32)
    scores = scores * (1.0 / math.sqrt(HEAD_DIM))
    key_slot = jnp.arange(WINDOW_CHUNKS * CHUNK)
    valid = (key_slot[None, :] >= CHUNK) | (jnp.arange(n_c)[:, None] > 0)
    scores = jnp.where(valid[None, :, None, None, None, :], scores, -1e30)
    sink = sinks.astype(jnp.float32).reshape(N_KV_HEADS, GQA_GROUP)
    sink = jnp.broadcast_to(sink[None, None, :, :, None, None], scores.shape[:-1] + (1,))
    probs = jax.nn.softmax(jnp.concatenate([scores, sink], axis=-1), axis=-1)[..., :-1]
    out = jnp.einsum('bchgqk,bckhd->bcqhgd', probs.astype(v.dtype), vb)
    return out.reshape(B, S, Q_WIDTH)

def peer_layer(h, w_q, keys_1, keys_2, expert_down, expert_up):
    B, S, D = h.shape
    T = B * S
    ht = h.reshape(T, D)
    q = (ht @ w_q).reshape(T, PEER_HEADS, PEER_QDIM)
    s1 = jnp.einsum('thd,kd->thk', q[..., :PEER_HALF], keys_1).astype(jnp.float32)
    s2 = jnp.einsum('thd,kd->thk', q[..., PEER_HALF:], keys_2).astype(jnp.float32)
    v1, i1 = lax.top_k(s1, PEER_TOPK)
    v2, i2 = lax.top_k(s2, PEER_TOPK)
    cand = (v1[..., :, None] + v2[..., None, :]).reshape(T, PEER_HEADS, PEER_TOPK * PEER_TOPK)
    vals, ci = lax.top_k(cand, PEER_TOPK)
    e_idx = (jnp.take_along_axis(i1, ci // PEER_TOPK, axis=-1) * N_KEYS
             + jnp.take_along_axis(i2, ci % PEER_TOPK, axis=-1))
    gates = jax.nn.softmax(vals, axis=-1)
    n_blk = T // PEER_BLOCK

    def block(args):
        hb, eb, gb = args
        u = jnp.take(expert_down, eb, axis=0)
        act = jax.nn.gelu(jnp.einsum('td,thkd->thk', hb, u).astype(jnp.float32))
        wv = (gb * act).astype(expert_up.dtype)
        vv = jnp.take(expert_up, eb, axis=0)
        return jnp.einsum('thk,thkd->td', wv, vv)

    y = lax.map(block, (ht.reshape(n_blk, PEER_BLOCK, D),
                        e_idx.reshape(n_blk, PEER_BLOCK, PEER_HEADS, PEER_TOPK),
                        gates.reshape(n_blk, PEER_BLOCK, PEER_HEADS, PEER_TOPK)))
    return y.reshape(B, S, D).astype(h.dtype)

def setup_inputs(seed: int = 0) -> dict:
    key = jax.random.key(seed)
    ks = jax.random.split(key, 17)
    f32 = jnp.float32
    n = lambda k, shape: jax.random.normal(k, shape, f32)
    return {
        "x": n(ks[0], (BATCH, SEQ, D_MODEL)),
        "g_mix": 1.0 + 0.02 * n(ks[1], (DEPTH, D_MODEL)),
        "w_in": n(ks[2], (DEPTH, D_MODEL, IN_WIDTH)) * D_MODEL ** -0.5,
        "w_pool_grp": n(ks[3], (DEPTH, POOL_GROUPS, POOL_GROUP_DIM, POOL_GROUP_DIM)) * POOL_GROUP_DIM ** -0.5,
        "pool_scale": 1.0 + 0.02 * n(ks[4], (DEPTH, POOL_WIDTH)),
        "attn_sinks": 0.5 * n(ks[5], (DEPTH, N_Q_HEADS)),
        "w_branch_pool": n(ks[6], (DEPTH, POOL_WIDTH, D_MODEL)) * POOL_WIDTH ** -0.5,
        "w_branch_attn": n(ks[7], (DEPTH, Q_WIDTH, D_MODEL)) * Q_WIDTH ** -0.5,
        "w_out": n(ks[8], (DEPTH, D_MODEL, D_MODEL)) * D_MODEL ** -0.5,
        "g_ffn": 1.0 + 0.02 * n(ks[9], (DEPTH, D_MODEL)),
        "w_peer_q": n(ks[10], (DEPTH, D_MODEL, PEER_HEADS * PEER_QDIM)) * D_MODEL ** -0.5,
        "peer_keys_1": n(ks[11], (DEPTH, N_KEYS, PEER_HALF)) * PEER_HALF ** -0.5,
        "peer_keys_2": n(ks[12], (DEPTH, N_KEYS, PEER_HALF)) * PEER_HALF ** -0.5,
        "expert_down": n(ks[13], (DEPTH, N_EXPERTS, D_MODEL)) * D_MODEL ** -0.5,
        "expert_up": n(ks[14], (DEPTH, N_EXPERTS, D_MODEL)) * PEER_HEADS ** -0.5,
        "g_final": 1.0 + 0.02 * n(ks[15], (D_MODEL,)),
    }

def reference(x, g_mix, w_in, w_pool_grp, pool_scale, attn_sinks, w_branch_pool,
              w_branch_attn, w_out, g_ffn, w_peer_q, peer_keys_1, peer_keys_2,
              expert_down, expert_up, g_final):
    B, S, _ = x.shape
    cos, sin = rope_tables(S)
    for l in range(DEPTH):
        h = rms_norm(x, g_mix[l])
        z = h @ w_in[l]
        p, q, k, v, gate_pool, gate_attn = jnp.split(z, SPLITS, axis=-1)
        q = apply_partial_rope(q.reshape(B, S, N_Q_HEADS, HEAD_DIM), cos, sin)
        k = apply_partial_rope(k.reshape(B, S, N_KV_HEADS, HEAD_DIM), cos, sin)
        v = v.reshape(B, S, N_KV_HEADS, HEAD_DIM)
        y_pool = pool_mixer(p, w_pool_grp[l], pool_scale[l]) @ w_branch_pool[l]
        y_attn = window_attention(q, k, v, attn_sinks[l]) @ w_branch_attn[l]
        merged = jax.nn.sigmoid(gate_pool) * y_pool + jax.nn.sigmoid(gate_attn) * y_attn
        x = x + merged @ w_out[l]
        x = x + peer_layer(rms_norm(x, g_ffn[l]), w_peer_q[l], peer_keys_1[l],
                           peer_keys_2[l], expert_down[l], expert_up[l])
    return rms_norm(x, g_final)


_drawn_inputs = setup_inputs


def setup_inputs(seed=0):
    import zlib

    import numpy as np

    out = dict(_drawn_inputs(seed))
    spreads = {}
    factors = {'g_mix': 2.83, 'pool_scale': 9.47, 'attn_sinks': 64.0, 'g_final': 23.536, 'g_ffn': 22.391}
    for name, (base, spread) in spreads.items():
        noise = np.random.default_rng([zlib.crc32(name.encode()), seed]).standard_normal(out[name].shape)
        drawn = base * np.exp(spread * noise) if base else spread * noise
        out[name] = __import__('jax').numpy.asarray(drawn.astype(out[name].dtype))
    for name, factor in factors.items():
        out[name] = (out[name] * factor).astype(out[name].dtype)
    return out
```

```python
from contextlib import ExitStack

import concourse.bass as bass
from concourse import mybir
import numpy as np

P = 128
D = 1024
KD = D // P
T = 1024
TG = 512
NG = T // TG
TT = TG // P
NBLK = T // P
POOL_W = 512
NPOOL = 4
PAD = 16
NH = 8
HD = 64
CH = 64
WK = CH + P
PH = 8
NK = 128
TOPK = 16
NSEL = PH * TOPK
NEXP = NK * NK
EPS = 1e-6
STAGES = 2
NEG_BIG = -3.4028234e38
NBANK = 8
RING = 8

F32 = mybir.dt.float32
U32 = mybir.dt.uint32
I32 = mybir.dt.int32
ALU = mybir.AluOpType
ACT = mybir.ActivationFunctionType
AX = mybir.AxisListType

SLOT_P, SLOT_K, SLOT_V, SLOT_Q = 0, 4, 5, 6
SLOT_MERGE = 10
SLOT_OUT = SLOT_MERGE + 3 * KD
SLOT_PQ = SLOT_OUT + KD
NSLOT = SLOT_PQ + 2 * PH

C_IDENT = 0
C_PERM = C_IDENT + P
C_ROWS = C_PERM + P
C_MASK = C_ROWS + P
C_IOTA = C_MASK + 4 * WK
NCONST = C_IOTA + TOPK
V_GMIX, V_GFFN, V_PSCALE = 0, KD, 2 * KD
V_SINK = V_PSCALE + NPOOL
NVEC = V_SINK + NH
R_COS, R_SIN, R_CNT = 0, TG, 2 * TG
NROPE = R_CNT + NPOOL * PAD


def mixer_jobs():
    jobs = [("xT", k) for k in range(KD)]
    jobs += [("p", j) for j in range(NPOOL)] + [("k",), ("v",), ("rot", 0)]
    for j in range(4):
        jobs += [("q", j)]
        if j:
            jobs += [("rot", j)]
    jobs += [("grp", 0), ("rot", 4)] + [("grp", j) for j in range(1, NPOOL)]
    jobs += [("sc", 0, i) for i in range(4)]
    for t in range(TT):
        jobs += [("pT", t, i) for i in range(4)]
        if t + 1 < TT:
            jobs += [("sc", t + 1, i) for i in range(4)]
        jobs += [("pv", t), ("yaT", t)]
    for m in range(KD):
        jobs += [("gp", m), ("ga", m), ("bp", m), ("ba", m)]
    jobs += [("xo", t, n) for t in range(TT) for n in range(2)]
    jobs += [("xT2", k) for k in range(KD)]
    jobs += [("pq", 0, 0), ("pq", 0, 1)]
    for h in range(PH):
        for i in range(2):
            if h + 1 < PH:
                jobs += [("pq", h + 1, i)]
            jobs += [("ss", h, i)]
    return {job: n for n, job in enumerate(jobs)}


JOBS = mixer_jobs()
NJ = len(JOBS)
NJ += -NJ % NBANK
SLOT_READER = ([("p", j) for j in range(NPOOL)] + [("k",), ("v",)] + [("q", j) for j in range(4)]
               + [(n, m) for m in range(KD) for n in ("gp", "ga", "ba")]
               + [("xo", TT - 1, 1)] * KD + [("pq", h, i) for h in range(PH) for i in range(2)])


def mixer(nc, io, scr):
    with ExitStack() as ctx:
        def sb(name, shape, dt=F32):
            return ctx.enter_context(nc.sbuf_tensor(name, shape, dt))

        def sem(name):
            return ctx.enter_context(nc.semaphore(name))

        banks = [ctx.enter_context(nc.psum_tensor(f"bank{i}", [P, 512], F32)) for i in range(NBANK)]

        const = sb("const", [P, NCONST])
        vecs = sb("vecs", [P, NVEC])
        keys = sb("keys", [P, 2, NK])
        wgrp = sb("wgrp", [P, NPOOL, P])
        gffn = sb("gffn", [P, D])
        rope = sb("rope", [P, NROPE])
        ring = sb("ring", [P, RING, D])
        x = sb("x", [P, TT, D])
        h = sb("h", [P, TT, D])
        hT = sb("hT", [P, KD, TG])
        pT = sb("pT", [P, NPOOL, PAD + TG])
        sums = sb("sums", [P, 2, PAD + TG])
        pooled = sb("pooled", [P, NPOOL, TG])
        ypT = sb("ypT", [P, NPOOL, TG])
        raw = sb("raw", [P, 2, TG])
        rot = sb("rot", [P, 2, TG])
        qz = sb("qz", [P, NH, TG])
        kT = sb("kT", [P, CH + TG])
        v = sb("v", [P, 1 + TT, P])
        pr = sb("pr", [P, NH, 2 * P])
        prT = sb("prT", [P, 2 * NH, P])
        ya = sb("ya", [P, NH * HD])
        yaT = sb("yaT", [P, 4, TG])
        sg = sb("sg", [P, 2, 2, TG])
        smask = sb("smask", [P, 2 * NK])
        small = sb("small", [P, 72])
        vtop = sb("vtop", [P, 2, TOPK])
        itop = sb("itop", [P, 2, TT, TOPK], U32)
        itopf = sb("itopf", [P, 2, TT, TOPK])
        cand = sb("cand", [P, TOPK, TOPK])
        cmask = sb("cmask", [P, TOPK * TOPK])
        ctop = sb("ctop", [P, TT, TOPK], U32)
        cij = sb("cij", [P, 2, TT, TOPK], U32)
        cijf = sb("cijf", [P, 2, TT, TOPK])
        sel = sb("sel", [P, 2, TT * TOPK])
        vals = sb("vals", [P, TT, TOPK])
        gsm = sb("gsm", [P, 2, TT])
        eidx = sb("eidx", [P, TT, NSEL], I32)
        gate = sb("gate", [P, TT, NSEL])

        mT = h[:].rearrange("p t d -> p (t d)").rearrange("p (k n) -> p k n", k=KD)
        qd = ypT
        s12 = pooled[:].rearrange("p a n -> p (a n)").rearrange("p (h i t c) -> p h i t c", h=2, i=2, t=TT)
        hit = sums[:].rearrange("p a n -> p (a n)")[:, 0:TT * TOPK * TOPK].rearrange("p (n j) -> p n j", j=TOPK)
        ident = const[:, C_IDENT:C_IDENT + P]
        ssq, var, std, rinv, tmp = (small[:, 4 * i:4 * i + 4] for i in range(5))
        mx, negm, sarg, es, rs, den = (small[:, 24 + 8 * i:32 + 8 * i] for i in range(6))

        consts_in = sem("consts_in")
        x_in = sem("x_in")
        rope_in = sem("rope_in")
        slot_in = [sem(f"slot_in{i}") for i in range(RING)]
        job_full = sem("job_full")
        ssq_ready = sem("ssq_ready")
        var_ready = sem("var_ready")
        std_ready = sem("std_ready")
        rinv_ready = sem("rinv_ready")
        h_ready = sem("h_ready")
        hT_ready = sem("hT_ready")
        p_ready = sem("p_ready")
        raw_ready = sem("raw_ready")
        roped = sem("roped")
        v_ready = sem("v_ready")
        pooled_ready = sem("pooled_ready")
        yp_ready = sem("yp_ready")
        m_ready = sem("m_ready")
        exp_ready = sem("exp_ready")
        prT_ready = sem("prT_ready")
        ya_ready = sem("ya_ready")
        yaT_ready = sem("yaT_ready")
        sig_ready = sem("sig_ready")
        merged = sem("merged")
        x2_ready = sem("x2_ready")
        x2_out = sem("x2_out")
        h2_ready = sem("h2_ready")
        h2_out = sem("h2_out")
        qd_ready = sem("qd_ready")
        ss_ready = sem("ss_ready")
        garg_ready = sem("garg_ready")
        gexp_ready = sem("gexp_ready")
        topk_done = sem("topk_done")
        choice_out = sem("choice_out")
        zeroed = sem("zeroed")
        carried = sem("carried")
        dve_own = sem("dve_own")
        pool_own = sem("pool_own")

        frees = {}
        for k in range(KD):
            frees["xT", k] = (hT_ready, k + 1, 2 * KD)
            frees["xT2", k] = (hT_ready, KD + k + 1, 2 * KD)
        for j in range(NPOOL):
            frees["p", j] = (p_ready, j + 1, NPOOL)
            frees["grp", j] = (yp_ready, j + 1, NPOOL)
            frees["q", j] = (raw_ready, j + 2, 5)
        frees["k",] = (raw_ready, 1, 5)
        frees["v",] = (v_ready, 1, 1)
        for i in range(5):
            frees["rot", i] = (roped, i + 1, 5)
        for t in range(TT):
            for i in range(4):
                frees["sc", t, i] = (exp_ready, 9 * t + 2 * i + 2, 9 * TT)
                frees["pT", t, i] = (prT_ready, 4 * t + i + 1, 4 * TT)
            frees["pv", t] = (ya_ready, t + 1, TT)
            frees["yaT", t] = (yaT_ready, t + 1, TT)
            for n in range(2):
                frees["xo", t, n] = (x2_ready, 2 * t + n + 1, 2 * TT)
        for m in range(KD):
            frees["gp", m] = (sig_ready, 2 * m + 1, 2 * KD)
            frees["ga", m] = (sig_ready, 2 * m + 2, 2 * KD)
            frees["bp", m] = frees["ba", m] = (merged, m + 1, KD)
        for hd in range(PH):
            for i in range(2):
                frees["pq", hd, i] = (qd_ready, 2 * hd + i + 1, 2 * PH)
                frees["ss", hd, i] = (ss_ready, 2 * hd + i + 1, 2 * PH)
        by_number = {n: job for job, n in JOBS.items()}

        def bank(*job):
            return banks[JOBS[job] % NBANK]

        def wait_job(eng, g, *job):
            eng.wait_ge(job_full, (g + 1) * NJ + JOBS[job] + 1)

        block = ctx.enter_context(nc.Block())

        @block.sync
        def _(sp):
            for dst, src in ((const, io["const"]), (vecs, io["vecs"]), (keys, io["keys"]),
                             (wgrp, io["wgrp"]), (gffn, io["gffn"])):
                sp.dma_start(dst[:], src).then_inc(consts_in, 16)
            with sp.Fori(0, NG) as g:
                sp.wait_ge(carried, g + 1)
                sp.dma_start(x[:], io["x"][bass.ds(g, 1)].rearrange("a t p d -> p (a t) d")).then_inc(x_in, 16)
                sp.dma_start(rope[:], io["rope"][bass.ds(g, 1)].rearrange("a p n -> p (a n)")).then_inc(rope_in, 16)
                for s in range(NSLOT):
                    before = [r for r in range(s % RING, NSLOT, RING) if r < s] or [
                        r - NSLOT for r in range(s % RING, NSLOT, RING)]
                    r = before[-1]
                    sp.wait_ge(job_full, (g + (1 if r >= 0 else 0)) * NJ + JOBS[SLOT_READER[r % NSLOT]] + 1)
                    sp.dma_start(ring[:, s % RING], io["slots"][s]).then_inc(slot_in[s % RING], 16)
                    if s == SLOT_PQ + 5:
                        for t in range(TT):
                            sp.wait_ge(x2_ready, g * 2 * TT + 2 * t + 2)
                            sp.dma_start(scr["x2"][bass.ds(g * TT + t, 1)].rearrange("a p d -> p (a d)"),
                                         x[:, t]).then_inc(x2_out, 16)
                for t in range(TT):
                    sp.wait_ge(h2_ready, g * TT + t + 1)
                    sp.dma_start(scr["h2"][bass.ds(g * TT + t, 1)].rearrange("a p d -> p (a d)"),
                                 x[:, t]).then_inc(h2_out, 16)
                sp.wait_ge(topk_done, g * PH + PH)
                sp.dma_start(scr["eidx"][bass.ds(g * TT, TT)].rearrange("t p n -> p t n"), eidx[:]).then_inc(choice_out, 16)
                sp.dma_start(scr["gate"][bass.ds(g * TT, TT)].rearrange("t p n -> p t n"), gate[:]).then_inc(choice_out, 16)
            sp.wait_ge(x2_out, 16 * NBLK)
            sp.wait_ge(h2_out, 16 * NBLK)
            sp.wait_ge(choice_out, 32 * NG)

        def slot_uses(q):
            return len(range(q, NSLOT, RING))

        @block.tensor
        def _(pe):
            pe.sem_inc(job_full, NJ)
            pe.wait_ge(consts_in, 16 * 5)
            with pe.Fori(0, NG) as g:
                def begin(*job):
                    n = JOBS[job]
                    if n >= NBANK:
                        s, c, per = frees[by_number[n - NBANK]]
                        pe.wait_ge(s, g * per + c)
                    return banks[n % NBANK]

                def weights(s):
                    pe.wait_ge(slot_in[s % RING], 16 * (g * slot_uses(s % RING) + s // RING + 1))
                    return ring[:, s % RING]

                def product(out, w, act, ks):
                    for i, k in enumerate(ks):
                        ins = nc.tensor.matmul(out[:], w[:, k * P:(k + 1) * P], act[:, i],
                                               start=i == 0, stop=i == len(ks) - 1)
                    ins.then_inc(job_full, 1)

                def project(job, s, act=hT, ks=range(KD)):
                    out = begin(*job)
                    w = weights(s)
                    product(out, w, act, ks)

                def turn(job, src):
                    out = begin(*job)
                    for i, a in enumerate(src):
                        ins = nc.tensor.transpose(out[:, i * P:(i + 1) * P], a, ident)
                    ins.then_inc(job_full, 1)

                pe.wait_ge(h_ready, g * 2 * TT + TT)
                for k in range(KD):
                    turn(("xT", k), [h[:, t, k * P:(k + 1) * P] for t in range(TT)])
                pe.wait_ge(hT_ready, g * 2 * KD + KD)
                for j in range(NPOOL):
                    project(("p", j), SLOT_P + j)
                project(("k",), SLOT_K)
                out = begin("v")
                w = weights(SLOT_V)
                for t in range(TT):
                    for k in range(KD):
                        ins = nc.tensor.matmul(out[:, t * P:(t + 1) * P], hT[:, k, t * P:(t + 1) * P],
                                               w[:, k * P:(k + 1) * P], start=k == 0, stop=k == KD - 1)
                ins.then_inc(job_full, 1)

                def partner(i):
                    out = begin("rot", i)
                    pe.wait_ge(raw_ready, g * 5 + i + 1)
                    nc.tensor.matmul(out[:], const[:, C_PERM:C_PERM + P], raw[:, i % 2],
                                     start=True, stop=True).then_inc(job_full, 1)

                def group(j):
                    out = begin("grp", j)
                    pe.wait_ge(pooled_ready, g * NPOOL + j + 1)
                    nc.tensor.matmul(out[:], wgrp[:, j], pooled[:, j], start=True, stop=True).then_inc(job_full, 1)

                partner(0)
                for j in range(4):
                    project(("q", j), SLOT_Q + j)
                    if j:
                        partner(j)
                group(0)
                partner(4)
                for j in range(1, NPOOL):
                    group(j)

                def scores(t):
                    if t == 0:
                        pe.wait_ge(roped, g * 5 + 5)
                        pe.wait_ge(carried, g + 1)
                    mask = const[:, C_MASK:C_MASK + 2 * WK] if t == 0 else const[:, C_MASK + 2 * WK:C_MASK + 4 * WK]
                    for i in range(4):
                        out = begin("sc", t, i)
                        nc.tensor.matmul(out[:, 0:2 * WK], const[:, C_ROWS:C_ROWS + P], mask, start=True, stop=False)
                        for e in range(2):
                            ins = nc.tensor.matmul(out[:, e * WK:(e + 1) * WK], qz[:, 2 * i + e, t * P:(t + 1) * P],
                                                   kT[:, t * P:t * P + WK], start=False, stop=e == 1)
                        ins.then_inc(job_full, 1)

                scores(0)
                for t in range(TT):
                    for i in range(4):
                        pe.wait_ge(exp_ready, g * 9 * TT + 9 * t + 2 * i + 2)
                        turn(("pT", t, i), [pr[:, 2 * i + e // 2, (e % 2) * P:(e % 2 + 1) * P] for e in range(4)])
                    if t + 1 < TT:
                        scores(t + 1)
                    out = begin("pv", t)
                    pe.wait_ge(prT_ready, g * 4 * TT + 4 * t + 4)
                    if t == 0:
                        pe.wait_ge(v_ready, g + 1)
                    for hd in range(NH):
                        kv = slice(hd // 4 * HD, (hd // 4 + 1) * HD)
                        nc.tensor.matmul(out[:, hd * HD:(hd + 1) * HD], prT[:, 2 * hd], v[:, t, kv], start=True, stop=False)
                        ins = nc.tensor.matmul(out[:, hd * HD:(hd + 1) * HD], prT[:, 2 * hd + 1], v[:, t + 1, kv],
                                               start=False, stop=True)
                    ins.then_inc(job_full, 1)
                    pe.wait_ge(ya_ready, g * TT + t + 1)
                    turn(("yaT", t), [ya[:, j * P:(j + 1) * P] for j in range(4)])

                for m in range(KD):
                    s = SLOT_MERGE + 3 * m
                    project(("gp", m), s)
                    project(("ga", m), s + 1)
                    w = weights(s + 2)
                    if m == 0:
                        pe.wait_ge(yp_ready, g * NPOOL + NPOOL)
                        pe.wait_ge(yaT_ready, g * TT + TT)
                    product(begin("bp", m), w, ypT, range(4))
                    product(begin("ba", m), w, yaT, range(4, 8))

                wo = [weights(SLOT_OUT + k) for k in range(KD)]
                pe.wait_ge(merged, g * KD + KD)
                for t in range(TT):
                    for n in range(2):
                        out = begin("xo", t, n)
                        for k in range(KD):
                            ins = nc.tensor.matmul(out[:], mT[:, k, t * P:(t + 1) * P], wo[k][:, n * 512:(n + 1) * 512],
                                                   start=k == 0, stop=k == KD - 1)
                        ins.then_inc(job_full, 1)

                pe.wait_ge(h_ready, g * 2 * TT + 2 * TT)
                for k in range(KD):
                    turn(("xT2", k), [h[:, t, k * P:(k + 1) * P] for t in range(TT)])
                pe.wait_ge(hT_ready, g * 2 * KD + 2 * KD)
                project(("pq", 0, 0), SLOT_PQ)
                project(("pq", 0, 1), SLOT_PQ + 1)
                for hd in range(PH):
                    for i in range(2):
                        if hd + 1 < PH:
                            project(("pq", hd + 1, i), SLOT_PQ + 2 * hd + 2 + i)
                        out = begin("ss", hd, i)
                        pe.wait_ge(qd_ready, g * 2 * PH + 2 * hd + i + 1)
                        for t in range(TT):
                            ins = nc.tensor.matmul(out[:, t * P:(t + 1) * P], qd[:, (2 * hd + i) % 4, t * P:(t + 1) * P],
                                                   keys[:, i], start=True, stop=True)
                        ins.then_inc(job_full, 1)
                pe.wait_ge(ss_ready, g * 2 * PH + 2 * PH)
                pe.wait_ge(qd_ready, g * 2 * PH + 2 * PH)
                pe.sem_inc(job_full, NJ - len(JOBS))

        @block.scalar
        def _(act):
            act.wait_ge(consts_in, 16 * 5)
            with act.Fori(0, NG) as g:
                def norm(n):
                    if n == 1:
                        act.wait_ge(x2_ready, g * 2 * TT + 2 * TT)
                    for t in range(TT):
                        ins = nc.scalar.activation(h[:, t], x[:, t], ACT.Square, accum_out=ssq[:, t:t + 1])
                    ins.then_inc(ssq_ready, 1)
                    act.wait_ge(var_ready, 2 * g + n + 1)
                    nc.scalar.activation(std, var, ACT.Sqrt).then_inc(std_ready, 1)
                    act.wait_ge(rinv_ready, 2 * g + n + 1)
                    for t in range(TT):
                        nc.scalar.activation(h[:, t], x[:, t], ACT.Copy, scale=rinv[:, t:t + 1]).then_inc(h_ready, 1)
                    for k in range(KD):
                        job = ("xT2" if n else "xT", k)
                        wait_job(act, g, *job)
                        gain = vecs[:, (V_GFFN if n else V_GMIX) + k:(V_GFFN if n else V_GMIX) + k + 1]
                        nc.scalar.activation(hT[:, k], bank(*job)[:], ACT.Copy, scale=gain).then_inc(hT_ready, 1)

                act.wait_ge(x_in, 16 * (g + 1))
                act.wait_ge(carried, g + 1)
                norm(0)
                for j in range(NPOOL):
                    wait_job(act, g, "p", j)
                    nc.scalar.activation(pT[:, j, PAD:], bank("p", j)[:], ACT.Copy).then_inc(p_ready, 1)

                def keep_raw(i, *job):
                    wait_job(act, g, *job)
                    if i >= 2:
                        act.wait_ge(roped, g * 5 + i - 1)
                    nc.scalar.activation(raw[:, i % 2], bank(*job)[:], ACT.Copy).then_inc(raw_ready, 1)

                keep_raw(0, "k")
                wait_job(act, g, "v")
                nc.scalar.activation(v[:, 1:1 + TT].rearrange("p t c -> p (t c)"), bank("v")[:], ACT.Copy).then_inc(v_ready, 1)
                for j in range(4):
                    keep_raw(1 + j, "q", j)
                for j in range(NPOOL):
                    wait_job(act, g, "grp", j)
                    nc.scalar.activation(ypT[:, j], bank("grp", j)[:], ACT.Copy,
                                         scale=vecs[:, V_PSCALE + j:V_PSCALE + j + 1]).then_inc(yp_ready, 1)

                def expon(t):
                    act.wait_ge(m_ready, g * TT + t + 1)
                    if t:
                        wait_job(act, g, "pT", t - 1, 3)
                        act.wait_ge(ya_ready, g * TT + t)
                    for hd in range(NH):
                        src = bank("sc", t, hd // 2)[:, hd % 2 * WK:(hd % 2 + 1) * WK]
                        nc.scalar.activation(pr[:, hd, CH:], src, ACT.Exp, bias=negm[:, hd:hd + 1], scale=HD ** -0.5,
                                             accum_out=rs[:, hd:hd + 1]).then_inc(exp_ready, 1)
                    nc.scalar.activation(es, sarg, ACT.Exp).then_inc(exp_ready, 1)

                for t in range(TT):
                    expon(t)
                    wait_job(act, g, "yaT", t)
                    nc.scalar.activation(yaT[:, :, t * P:(t + 1) * P],
                                         bank("yaT", t)[:].rearrange("p (j c) -> p j c", j=4), ACT.Copy).then_inc(yaT_ready, 1)

                for m in range(KD):
                    if m >= 2:
                        act.wait_ge(merged, g * KD + m - 1)
                    for i, n in enumerate(("gp", "ga")):
                        wait_job(act, g, n, m)
                        nc.scalar.activation(sg[:, m % 2, i], bank(n, m)[:], ACT.Sigmoid).then_inc(sig_ready, 1)

                norm(1)

                def keep_q(hd, i):
                    n = 2 * hd + i
                    wait_job(act, g, "pq", hd, i)
                    if n >= 4:
                        wait_job(act, g, "ss", (n - 4) // 2, i)
                    nc.scalar.activation(qd[:, n % 4], bank("pq", hd, i)[:], ACT.Copy).then_inc(qd_ready, 1)

                keep_q(0, 0)
                keep_q(0, 1)
                for hd in range(PH):
                    for i in range(2):
                        if hd + 1 < PH:
                            keep_q(hd + 1, i)
                        wait_job(act, g, "ss", hd, i)
                        if hd >= 2:
                            act.wait_ge(topk_done, g * PH + hd - 1)
                        nc.scalar.activation(s12[:, hd % 2, i].rearrange("p t c -> p (t c)"), bank("ss", hd, i)[:],
                                             ACT.Copy).then_inc(ss_ready, 1)
                    if hd:
                        act.wait_ge(garg_ready, g * PH + hd)
                        nc.scalar.activation(vals[:], vals[:], ACT.Exp).then_inc(gexp_ready, 1)
                act.wait_ge(garg_ready, g * PH + PH)
                nc.scalar.activation(vals[:], vals[:], ACT.Exp).then_inc(gexp_ready, 1)

        @block.gpsimd
        def _(pool):
            nc.gpsimd.memset(qz[:], 0.0)
            nc.gpsimd.memset(pr[:], 0.0)
            nc.gpsimd.memset(pT[:, :, 0:PAD], 0.0)
            nc.gpsimd.memset(kT[:, 0:CH], 0.0)
            nc.gpsimd.memset(v[:, 0], 0.0).then_inc(carried, 1)
            pool.wait_ge(consts_in, 16 * 5)
            with pool.Fori(0, NG) as g:
                own = [0]

                def link(ins):
                    own[0] += 1
                    ins.then_inc(pool_own, 1)
                    pool.wait_ge(pool_own, own[0])

                pool.wait_ge(rope_in, 16 * (g + 1))
                for j in range(NPOOL):
                    pool.wait_ge(p_ready, g * NPOOL + j + 1)
                    src, lo = pT[:, j], 0
                    for i in range(j + 1):
                        lo += 1 << i
                        dst = sums[:, i % 2]
                        link(nc.gpsimd.tensor_tensor(dst[:, lo:], src[:, lo:], src[:, lo - (1 << i):PAD + TG - (1 << i)], ALU.add))
                        src = dst
                    head = src[:, PAD:2 * PAD]
                    link(nc.gpsimd.tensor_tensor(head, head, rope[:, R_CNT + j * PAD:R_CNT + (j + 1) * PAD], ALU.mult))
                    link(nc.gpsimd.tensor_scalar(src[:, PAD:], src[:, PAD:], 1.0 / (2 << j), None, ALU.mult))
                    nc.gpsimd.tensor_tensor(pooled[:, j], src[:, PAD:], pT[:, j, PAD:], ALU.subtract).then_inc(pooled_ready, 1)
                    pool.wait_ge(pooled_ready, g * NPOOL + j + 1)

                for t in range(TT):
                    pool.wait_ge(h_ready, g * 2 * TT + TT + t + 1)
                    pool.wait_ge(x2_out, 16 * (g * TT + TT))
                    nc.gpsimd.tensor_tensor(x[:, t], h[:, t], gffn[:], ALU.mult).then_inc(h2_ready, 1)

                pool.wait_ge(job_full, (g + 1) * NJ + NJ)
                own[0] += 1
                pool.sem_inc(pool_own, 1)
                link(nc.gpsimd.tensor_copy(pT[:, :, 0:PAD], pT[:, :, TG:TG + PAD]))
                link(nc.gpsimd.tensor_copy(kT[:, 0:CH], kT[:, TG:TG + CH]))
                link(nc.gpsimd.tensor_copy(v[:, 0], v[:, TT]))
                link(nc.gpsimd.tensor_copy(const[:, C_MASK:C_MASK + 2 * WK], const[:, C_MASK + 2 * WK:C_MASK + 4 * WK]))
                pool.wait_ge(choice_out, 32 * (g + 1))
                pool.wait_ge(h2_out, 16 * TT * (g + 1))
                pool.sem_inc(carried, 1)
                pool.sem_clear(pool_own)

        @block.vector
        def _(dve):
            dve.wait_ge(consts_in, 16 * 5)
            with dve.Fori(0, NG) as g:
                own = [0]

                def link(ins):
                    own[0] += 1
                    ins.then_inc(dve_own, 1)
                    dve.wait_ge(dve_own, own[0])

                def mark(ins):
                    own[0] += 1
                    ins.then_inc(dve_own, 1)

                def linked():
                    dve.wait_ge(dve_own, own[0])

                def norm(n):
                    dve.wait_ge(ssq_ready, 2 * g + n + 1)
                    nc.vector.tensor_scalar(var, ssq, 1.0 / D, EPS, ALU.mult, ALU.add).then_inc(var_ready, 1)
                    dve.wait_ge(std_ready, 2 * g + n + 1)
                    link(nc.vector.reciprocal(rinv, std))
                    link(nc.vector.tensor_tensor(tmp, rinv, rinv, ALU.mult))
                    link(nc.vector.tensor_tensor(tmp, tmp, var, ALU.mult))
                    link(nc.vector.tensor_scalar(tmp, tmp, -0.5, 1.5, ALU.mult, ALU.add))
                    nc.vector.tensor_tensor(rinv, rinv, tmp, ALU.mult).then_inc(rinv_ready, 1)

                norm(0)

                dve.wait_ge(rope_in, 16 * (g + 1))
                dve.wait_ge(carried, g + 1)
                for i in range(5):
                    dve.wait_ge(raw_ready, g * 5 + i + 1)
                    mark(nc.vector.tensor_tensor(rot[:, 0], raw[:, i % 2], rope[:, R_COS:R_COS + TG], ALU.mult))
                    wait_job(dve, g, "rot", i)
                    link(nc.vector.tensor_tensor(rot[:, 1], bank("rot", i)[:], rope[:, R_SIN:R_SIN + TG], ALU.mult))
                    if i == 0:
                        nc.vector.tensor_tensor(kT[:, CH:], rot[:, 0], rot[:, 1], ALU.add).then_inc(roped, 1)
                    else:
                        mark(nc.vector.tensor_tensor(qz[0:HD, i - 1], rot[0:HD, 0], rot[0:HD, 1], ALU.add))
                        nc.vector.tensor_tensor(qz[HD:P, i + 3], rot[HD:P, 0], rot[HD:P, 1], ALU.add).then_inc(roped, 1)
                    dve.wait_ge(roped, g * 5 + i + 1)

                sink = vecs[:, V_SINK:V_SINK + NH]

                def maxima(t):
                    for i in range(4):
                        wait_job(dve, g, "sc", t, i)
                        mark(nc.vector.tensor_reduce(mx[:, 2 * i:2 * i + 2],
                                                     bank("sc", t, i)[:, 0:2 * WK].rearrange("p (e c) -> p e c", e=2),
                                                     AX.X, ALU.max))
                    linked()
                    if t:
                        dve.wait_ge(exp_ready, g * 9 * TT + 9 * t)
                    link(nc.vector.scalar_tensor_tensor(out=mx, in0=mx, scalar=HD ** -0.5, in1=sink, op0=ALU.mult, op1=ALU.max))
                    mark(nc.vector.tensor_scalar(negm, mx, -1.0, None, ALU.mult))
                    nc.vector.tensor_tensor(sarg, sink, mx, ALU.subtract).then_inc(m_ready, 1)
                    dve.wait_ge(m_ready, g * TT + t + 1)

                for t in range(TT):
                    maxima(t)
                    for i in range(4):
                        wait_job(dve, g, "pT", t, i)
                        nc.vector.tensor_copy(prT[:, 4 * i:4 * i + 4].rearrange("p a c -> p (a c)"),
                                              bank("pT", t, i)[:]).then_inc(prT_ready, 1)
                    dve.wait_ge(exp_ready, g * 9 * TT + 9 * t + 9)
                    link(nc.vector.tensor_tensor(den, rs, es, ALU.add))
                    link(nc.vector.reciprocal(den, den))
                    wait_job(dve, g, "pv", t)
                    nc.vector.tensor_tensor(ya[:].rearrange("p (a c) -> p a c", a=NH),
                                            bank("pv", t)[:].rearrange("p (a c) -> p a c", a=NH),
                                            den.unsqueeze(2).to_broadcast([P, NH, HD]), ALU.mult).then_inc(ya_ready, 1)

                for m in range(KD):
                    for i, n in enumerate(("bp", "ba")):
                        wait_job(dve, g, n, m)
                        dve.wait_ge(sig_ready, g * 2 * KD + 2 * m + 1 + i)
                        mark(nc.vector.tensor_tensor(sg[:, m % 2, i], bank(n, m)[:], sg[:, m % 2, i], ALU.mult))
                    linked()
                    nc.vector.tensor_tensor(mT[:, m], sg[:, m % 2, 0], sg[:, m % 2, 1], ALU.add).then_inc(merged, 1)

                for t in range(TT):
                    for n in range(2):
                        wait_job(dve, g, "xo", t, n)
                        part = x[:, t, n * 512:(n + 1) * 512]
                        nc.vector.tensor_tensor(part, part, bank("xo", t, n)[:], ALU.add).then_inc(x2_ready, 1)

                norm(1)

                def top16(scores, masked, values, places):
                    link(nc.vector.max(values[:, 0:8], scores))
                    mark(nc.vector.max_index(places[:, 0:8], values[:, 0:8], scores))
                    link(nc.vector.match_replace(masked, values[:, 0:8], scores, NEG_BIG))
                    link(nc.vector.max(values[:, 8:16], masked))
                    mark(nc.vector.max_index(places[:, 8:16], values[:, 8:16], masked))

                iota = const[:, C_IOTA:C_IOTA + TOPK]
                for hd in range(PH):
                    dve.wait_ge(ss_ready, g * 2 * PH + 2 * hd + 2)
                    own[0] += 1
                    dve.sem_inc(dve_own, 1)
                    for t in range(TT):
                        for i in range(2):
                            top16(s12[:, hd % 2, i, t], smask[:, i * NK:(i + 1) * NK], vtop[:, i], itop[:, i, t])
                        linked()
                        link(nc.vector.tensor_tensor(cand[:], vtop[:, 0].unsqueeze(2).to_broadcast([P, TOPK, TOPK]),
                                                     vtop[:, 1].unsqueeze(1).to_broadcast([P, TOPK, TOPK]), ALU.add))
                        top16(cand[:].rearrange("p a b -> p (a b)"), cmask[:], vals[:, t], ctop[:, t])
                    linked()
                    mark(nc.vector.tensor_scalar(cij[:, 0], ctop[:], 4, None, ALU.logical_shift_right))
                    mark(nc.vector.tensor_scalar(cij[:, 1], ctop[:], TOPK - 1, None, ALU.bitwise_and))
                    mark(nc.vector.tensor_copy(itopf[:], itop[:]))
                    mark(nc.vector.tensor_copy(gsm[:, 0], vals[:, :, 0]))
                    linked()
                    mark(nc.vector.tensor_copy(cijf[:], cij[:]))
                    nc.vector.tensor_tensor(vals[:], vals[:], gsm[:, 0].unsqueeze(2).to_broadcast([P, TT, TOPK]),
                                            ALU.subtract).then_inc(garg_ready, 1)
                    linked()
                    for i in range(2):
                        link(nc.vector.tensor_tensor(hit, cijf[:, i].rearrange("p t k -> p (t k)").unsqueeze(2)
                                                     .to_broadcast([P, TT * TOPK, TOPK]),
                                                     iota.unsqueeze(1).to_broadcast([P, TT * TOPK, TOPK]), ALU.is_equal))
                        hit4 = hit.rearrange("p (t k) j -> p t k j", t=TT)
                        link(nc.vector.tensor_tensor(hit4, hit4, itopf[:, i].unsqueeze(2).to_broadcast([P, TT, TOPK, TOPK]),
                                                     ALU.mult))
                        link(nc.vector.tensor_reduce(sel[:, i], hit, AX.X, ALU.add))
                    cols = slice(hd * TOPK, (hd + 1) * TOPK)
                    link(nc.vector.scalar_tensor_tensor(out=eidx[:, :, cols], in0=sel[:, 0].rearrange("p (t k) -> p t k", t=TT),
                                                        scalar=float(NK), in1=sel[:, 1].rearrange("p (t k) -> p t k", t=TT),
                                                        op0=ALU.mult, op1=ALU.add))
                    dve.wait_ge(gexp_ready, g * PH + hd + 1)
                    link(nc.vector.tensor_reduce(gsm[:, 0], vals[:], AX.X, ALU.add))
                    link(nc.vector.reciprocal(gsm[:, 1], gsm[:, 0]))
                    nc.vector.tensor_tensor(gate[:, :, cols], vals[:], gsm[:, 1].unsqueeze(2).to_broadcast([P, TT, TOPK]),
                                            ALU.mult).then_inc(topk_done, 1)
                    dve.wait_ge(topk_done, g * PH + hd + 1)
                dve.sem_inc(dve_own, 1)
                dve.sem_clear(dve_own)
                dve.wait_ge(choice_out, 32 * (g + 1))


RD, RU, RDIAG = 16, 16, 4
CHUNK = 4


def peer(nc, io, scr):
    with ExitStack() as ctx:
        def sb(name, shape, dt=F32):
            return ctx.enter_context(nc.sbuf_tensor(name, shape, dt))

        def sem(name):
            return ctx.enter_context(nc.semaphore(name))

        ident = sb("p_ident", [P, P])
        gfin = sb("p_gfin", [P, D])
        next_h2, next_x2 = sb("next_h2", [P, D]), sb("next_x2", [P, D])
        next_gate, next_idx = sb("next_gate", [P, NSEL]), sb("next_idx", [P, NSEL], I32)
        h2, gate = sb("h2", [P, D]), sb("gate_now", [P, NSEL])
        idx_down, idx_up = sb("idx_down", [P, NSEL], I32), sb("idx_up", [P, NSEL], I32)
        down = sb("down", [P, RD, D])
        up = sb("up", [P, RU, D])
        diag = sb("diag", [P, RDIAG, P])
        acc = sb("acc", [P, D])
        fin = sb("fin", [P, D])
        junk = sb("junk", [P, D])
        dots = sb("dots", [P, TOPK])
        g1, g2, th = sb("g1", [P, TOPK]), sb("g2", [P, TOPK]), sb("th", [P, TOPK])
        wts = sb("wts", [P, 2, TOPK])
        stat = sb("stat", [P, 8])
        ysum = ctx.enter_context(nc.psum_tensor("ysum", [P, 2, D], F32))
        ssq, var, std, rinv, tmp = (stat[:, i:i + 1] for i in range(5))

        const_in = sem("p_const_in")
        idx_in, h2_in, gate_in, x2_in = sem("idx_in"), sem("h2_in"), sem("gate_in"), sem("x2_in")
        idx_taken = sem("idx_taken")
        h2_taken, x2_taken = sem("h2_taken"), sem("x2_taken")
        idx_copied = sem("idx_copied")
        pool_waits = sem("pool_waits")
        down_in = [sem(f"down_in{i}") for i in range(RD)]
        up_in = [sem(f"up_in{i}") for i in range(RU)]
        dot_done = sem("dot_done")
        up_used = sem("up_used")
        th_arg, th_ready, w_ready = sem("th_arg"), sem("th_ready"), sem("w_ready")
        diag_ready = sem("diag_ready")
        y_ready = sem("y_ready")
        y_taken = sem("y_taken")
        acc_ready, ssq_ready, var_ready, std_ready = sem("acc_ready"), sem("p_ssq_ready"), sem("p_var_ready"), sem("p_std_ready")
        fin_ready, out_stored = sem("fin_ready"), sem("out_stored")
        fin_free = sem("fin_free")
        dve_own = sem("p_dve_own")

        block = ctx.enter_context(nc.Block())

        def blocks(eng, one):
            one(0, True, False)
            with eng.Fori(1, NBLK - 1) as b:
                one(b, False, False)
            one(NBLK - 1, False, True)

        @block.sync
        def _(sp):
            sp.dma_start(ident[:], io["const"][:, C_IDENT:C_IDENT + P]).then_inc(const_in, 16)
            sp.dma_start(gfin[:], io["gfin"]).then_inc(const_in, 16)

            def rows(name, b):
                if isinstance(b, int):
                    return scr[name][b]
                return scr[name][bass.ds(b, 1)].rearrange("a p n -> p (a n)")

            def one(b, first, last):
                if first:
                    sp.dma_start(next_idx[:], rows("eidx", 0)).then_inc(idx_in, 16)
                sp.wait_ge(h2_taken, b + 1)
                sp.dma_start(next_h2[:], rows("h2", b)).then_inc(h2_in, 16)
                sp.dma_start(next_gate[:], rows("gate", b)).then_inc(gate_in, 16)
                if not last:
                    sp.wait_ge(idx_taken, b + 1)
                    sp.dma_start(next_idx[:], rows("eidx", b + 1)).then_inc(idx_in, 16)
                sp.wait_ge(x2_taken, b + 1)
                sp.dma_start(next_x2[:], rows("x2", b)).then_inc(x2_in, 16)
                if not first:
                    sp.wait_ge(fin_ready, b)
                    dst = io["out"][b - 1] if isinstance(b, int) else io["out"][bass.ds(b - 1, 1)].rearrange("a p n -> p (a n)")
                    sp.dma_start(dst, fin[:]).then_inc(out_stored, 16)
                    sp.wait_ge(out_stored, 16 * b)
                    sp.sem_inc(fin_free, 1)

            blocks(sp, one)
            sp.wait_ge(fin_ready, NBLK)
            sp.dma_start(io["out"][NBLK - 1], fin[:]).then_inc(out_stored, 16)
            sp.wait_ge(out_stored, 16 * NBLK)

        @block.gpsimd
        def _(pool):
            def gather(dst, table, idx, h, k, arrived):
                nc.gpsimd.indirect_dma_start(dst, None, table, bass.IndirectOffsetOnAxis(
                    idx[:, h * TOPK + k:h * TOPK + k + 1], 0)).then_inc(arrived, 16)

            def free(used, count):
                pool.wait_ge(used, count)
                pool.sem_inc(pool_waits, 1)

            def down_rows(n, h, ks):
                free(dot_done, 16 * n + ks[-1] + 1)
                for k in ks:
                    gather(down[:, k % RD], io["down"], idx_down, h, k, down_in[k % RD])

            pool.wait_ge(idx_in, 16)
            nc.gpsimd.tensor_copy(idx_down[:], next_idx[:]).then_inc(idx_copied, 1)
            pool.wait_ge(idx_copied, 1)
            pool.sem_inc(idx_taken, 1)
            down_rows(0, 0, range(TOPK))

            def one(b, first, last):
                for h in range(PH):
                    n = b * PH + h
                    cols = slice(h * TOPK, (h + 1) * TOPK)
                    nc.gpsimd.tensor_copy(idx_up[:, cols], idx_down[:, cols]).then_inc(idx_copied, 1)
                    free(idx_copied, 1 + 2 * n + 1)
                    for c in range(0, TOPK, CHUNK):
                        ks = range(c, c + CHUNK)
                        if not (last and h == PH - 1):
                            down_rows(n + 1, (h + 1) % PH, ks)
                        free(up_used, 16 * n + ks[-1] + 1)
                        for k in ks:
                            gather(up[:, k % RU], io["up"], idx_up, h, k, up_in[k % RU])
                    if h == 0 and not last:
                        pool.wait_ge(idx_in, 16 * (b + 2))
                    free(dot_done, 16 * (n + 1) + RD)
                    nc.gpsimd.tensor_copy(idx_down[:, cols], next_idx[:, cols]).then_inc(idx_copied, 1)
                    if h == PH - 1:
                        pool.wait_ge(idx_copied, 1 + 2 * n + 2)
                        pool.sem_inc(idx_taken, 1)
                pool.sem_clear(pool_waits)

            blocks(pool, one)

        @block.vector
        def _(dve):
            dve.sem_inc(h2_taken, 1)
            dve.sem_inc(x2_taken, 1)
            dve.sem_inc(dot_done, RD)
            dve.sem_inc(y_taken, 2)
            dve.sem_inc(fin_free, 1)
            own = [0]

            def link(ins):
                own[0] += 1
                ins.then_inc(dve_own, 1)
                dve.wait_ge(dve_own, own[0])

            def add_sum(n, h):
                dve.wait_ge(y_ready, n)
                if h == 1:
                    dve.wait_ge(x2_in, 16 * ((n - 1) // PH + 1) if isinstance(n, int) else 2 * n + 14)
                src = next_x2 if h == 1 else acc
                link(nc.vector.tensor_tensor(acc[:], src[:], ysum[:, (h - 1) % 2], ALU.add))
                dve.sem_inc(y_taken, 1)
                if h == 1:
                    dve.sem_inc(x2_taken, 1)

            def final_norm(b):
                dve.wait_ge(ssq_ready, b)
                nc.vector.tensor_scalar(var, ssq, 1.0 / D, EPS, ALU.mult, ALU.add).then_inc(var_ready, 1)
                dve.wait_ge(std_ready, b)
                link(nc.vector.reciprocal(rinv, std))
                link(nc.vector.tensor_tensor(tmp, rinv, rinv, ALU.mult))
                link(nc.vector.tensor_tensor(tmp, tmp, var, ALU.mult))
                link(nc.vector.tensor_scalar(tmp, tmp, -0.5, 1.5, ALU.mult, ALU.add))
                link(nc.vector.tensor_tensor(rinv, rinv, tmp, ALU.mult))
                dve.wait_ge(fin_free, b)
                nc.vector.scalar_tensor_tensor(out=fin[:], in0=acc[:], scalar=rinv, in1=gfin[:],
                                               op0=ALU.mult, op1=ALU.mult).then_inc(fin_ready, 1)
                dve.wait_ge(fin_ready, b)

            def one(b, first, last):
                dve.wait_ge(h2_in, 16 * (b + 1))
                dve.wait_ge(gate_in, 16 * (b + 1))
                nc.vector.tensor_copy(h2[:], next_h2[:])
                link(nc.vector.tensor_copy(gate[:], next_gate[:]))
                dve.sem_inc(h2_taken, 1)
                for h in range(PH):
                    n = b * PH + h
                    for k in range(TOPK):
                        dve.wait_ge(down_in[k % RD], 16 * (TOPK // RD * n + k // RD + 1))
                        row = down[:, k % RD]
                        ins = nc.vector.tensor_tensor_reduce(out=row, in0=row, in1=h2[:], scale=1.0, scalar=0.0, op0=ALU.mult,
                                                             op1=ALU.add, accum_out=dots[:, k:k + 1]).then_inc(dot_done, 1)
                    dve.wait_ge(dot_done, 16 * (n + 1) + RD)
                    link(nc.vector.tensor_tensor(g1[:], dots[:], dots[:], ALU.mult))
                    link(nc.vector.tensor_scalar(g1[:], g1[:], 0.044715, 1.0, ALU.mult, ALU.add))
                    nc.vector.tensor_tensor(g1[:], g1[:], dots[:], ALU.mult).then_inc(th_arg, 1)
                    link(nc.vector.scalar_tensor_tensor(out=g2[:], in0=dots[:], scalar=0.5, in1=gate[:, h * TOPK:(h + 1) * TOPK],
                                                        op0=ALU.mult, op1=ALU.mult))
                    if not (first and h == 0):
                        add_sum(n, h if h else PH)
                        if h == 0:
                            dve.sem_inc(acc_ready, 1)
                    dve.wait_ge(th_ready, n + 1)
                    nc.vector.scalar_tensor_tensor(out=wts[:, h % 2], in0=th[:], scalar=1.0, in1=g2[:],
                                                   op0=ALU.add, op1=ALU.mult).then_inc(w_ready, 1)
                    dve.wait_ge(w_ready, n + 1)
                    if h == 0 and not first:
                        final_norm(b)
                own[0] += 1
                dve.sem_inc(dve_own, 1)
                dve.sem_clear(dve_own)
                own[0] = 0

            dve.wait_ge(const_in, 32)
            blocks(dve, one)
            add_sum(NBLK * PH, PH)
            dve.sem_inc(acc_ready, 1)
            final_norm(NBLK)

        @block.scalar
        def _(act):
            def root(b):
                act.wait_ge(acc_ready, b)
                if not (isinstance(b, int) and b == 1):
                    act.wait_ge(fin_ready, b - 1)
                nc.scalar.activation(junk[:], acc[:], ACT.Square, accum_out=ssq).then_inc(ssq_ready, 1)
                act.wait_ge(var_ready, b)
                nc.scalar.activation(std, var, ACT.Sqrt).then_inc(std_ready, 1)

            def one(b, first, last):
                for h in range(PH):
                    n = b * PH + h
                    act.wait_ge(th_arg, n + 1)
                    nc.scalar.activation(th[:], g1[:], ACT.Tanh, scale=0.7978845608028654).then_inc(th_ready, 1)
                    if h == 0 and not first:
                        root(b)
                    act.wait_ge(w_ready, n + 1)
                    for k in range(TOPK):
                        act.wait_ge(up_used, 16 * n + k + 1 + RU - RDIAG)
                        nc.scalar.activation(diag[:, k % RDIAG], ident[:], ACT.Copy,
                                             scale=wts[:, h % 2, k:k + 1]).then_inc(diag_ready, 1)

            act.wait_ge(const_in, 32)
            blocks(act, one)
            root(NBLK)

        @block.tensor
        def _(pe):
            pe.sem_inc(up_used, RU)

            def one(b, first, last):
                for h in range(PH):
                    n = b * PH + h
                    pe.wait_ge(y_taken, n + 1)
                    for k in range(TOPK):
                        pe.wait_ge(diag_ready, 16 * n + k + 1)
                        pe.wait_ge(up_in[k % RU], 16 * (TOPK // RU * n + k // RU + 1))
                        for i in range(2):
                            cols = slice(i * 512, (i + 1) * 512)
                            ins = nc.tensor.matmul(ysum[:, h % 2, cols], diag[:, k % RDIAG], up[:, k % RU, cols],
                                                   start=k == 0, stop=k == TOPK - 1)
                        ins.then_inc(up_used, 1)
                    pe.wait_ge(up_used, 16 * (n + 1) + RU)
                    pe.sem_inc(y_ready, 1)

            blocks(pe, one)


def build(nc, io):
    scr = {n: nc.dram_tensor(f"all_{n}", shape, dt, kind="Internal").ap() for n, shape, dt in (
        ("x2", (NBLK, P, D), F32), ("h2", (NBLK, P, D), F32), ("eidx", (NBLK, P, NSEL), I32), ("gate", (NBLK, P, NSEL), F32))}
    mixer(nc, io, scr)
    if STAGES > 1:
        peer(nc, io, scr)


def slots_of(w_in, w_branch_pool, w_branch_attn, w_out, w_peer_q):
    def columns(w):
        k, n = w.shape[0] // P, w.shape[1] // P
        return w.reshape(k, P, n, P).transpose(2, 1, 0, 3).reshape(n, P, k * P)

    pool, q, k, v, gp, ga = np.split(w_in, np.cumsum([POOL_W, NH * HD, P, P, D]), axis=1)
    q = q.reshape(D, 2, 4, HD).transpose(0, 2, 1, 3).reshape(D, NH * HD)
    branches = np.concatenate([columns(w_branch_pool), columns(w_branch_attn)], axis=2)
    merge = np.stack([columns(gp), columns(ga), branches], axis=1).reshape(3 * KD, P, D)
    return np.concatenate([columns(pool), columns(k), columns(v), columns(q), merge,
                           w_out.reshape(KD, P, D), columns(w_peer_q)])


def constants():
    c = np.zeros((P, NCONST), np.float32)
    c[:, C_IDENT:C_IDENT + P] = np.eye(P)
    rot, half = HD // 4, HD // 8
    for base in (0, HD):
        for d in range(rot):
            c[base + (d + half) % rot, C_PERM + base + d] = 1
    c[0, C_ROWS:C_ROWS + CH] = 1
    c[1, C_ROWS + CH:C_ROWS + P] = 1
    mask = c[:, C_MASK:C_MASK + 4 * WK].reshape(P, 4, WK)
    mask[0, :, P:] = -1e30
    mask[1, :, 0:CH] = -1e30
    mask[0, 0:2, 0:CH] = -1e30
    c[:, C_IOTA:C_IOTA + TOPK] = np.arange(TOPK)

    pos = np.arange(T, dtype=np.float32)
    inv = np.float32(500000.0) ** (-np.arange(0, rot, 2, dtype=np.float32) / np.float32(rot))
    ang = pos[:, None] * inv[None, :]
    table = np.zeros((2, P, T), np.float32)
    table[0] = 1
    for base in (0, HD):
        table[0, base:base + rot] = np.tile(np.cos(ang).T, (2, 1))
        table[1, base:base + rot] = np.tile(np.sin(ang).T, (2, 1))
        table[1, base:base + half] *= -1
    r = np.ones((NG, P, NROPE), np.float32)
    r[:, :, R_COS:R_CNT] = table.reshape(2, P, NG, TG).transpose(2, 1, 0, 3).reshape(NG, P, 2 * TG)
    for j in range(NPOOL):
        w = 2 << j
        r[0, :, R_CNT + j * PAD:R_CNT + (j + 1) * PAD] = w / np.minimum(np.arange(PAD) + 1, w)
    return c, r


def arrays_of(x, g_mix, w_in, w_pool_grp, pool_scale, attn_sinks, w_branch_pool, w_branch_attn, w_out, g_ffn,
              w_peer_q, peer_keys_1, peer_keys_2, expert_down, expert_up, g_final):
    c, r = constants()
    vecs = np.concatenate([g_mix[0].reshape(KD, P).T, g_ffn[0].reshape(KD, P).T, pool_scale[0].reshape(NPOOL, P).T,
                           np.broadcast_to(attn_sinks[0], (P, NH))], axis=1)
    return {
        "x": x.reshape(NG, TT, P, D), "const": c, "rope": r, "vecs": vecs,
        "slots": slots_of(w_in[0], w_branch_pool[0], w_branch_attn[0], w_out[0], w_peer_q[0]),
        "keys": np.stack([peer_keys_1[0].T, peer_keys_2[0].T], axis=1),
        "wgrp": w_pool_grp[0].transpose(1, 0, 2),
        "gffn": np.broadcast_to(g_ffn[0], (P, D)), "gfin": np.broadcast_to(g_final, (P, D)),
        "down": expert_down[0], "up": expert_up[0],
    }


def kernel(**inputs):
    import concourse.bacc as bacc
    from concourse.bass_utils import run_bass_kernel_spmd

    nc = bacc.Bacc("TRN2", target_bir_lowering=False, num_devices=1)
    arrays = {n: np.ascontiguousarray(a) for n, a in arrays_of(**{k: np.asarray(a) for k, a in inputs.items()}).items()}
    io = {n: nc.dram_tensor(f"in_{n}", a.shape, F32, kind="ExternalInput").ap() for n, a in arrays.items()}
    io["out"] = nc.dram_tensor("out", (NBLK, P, D), F32, kind="ExternalOutput").ap()
    build(nc, io)
    r = run_bass_kernel_spmd(nc, [{f"in_{n}": a for n, a in arrays.items()}], core_ids=[0])
    return r.results[0]["out"].reshape(1, T, D)
```

```python
from contextlib import ExitStack

import concourse.bass as bass
from concourse import mybir
import numpy as np

P = 128
D = 1024
KD = D // P
T = 1024
TG = 512
NG = T // TG
TT = TG // P
NBLK = T // P
POOL_W = 512
NPOOL = 4
PAD = 16
NH = 8
HD = 64
CH = 64
WK = CH + P
PH = 8
NK = 128
TOPK = 16
NSEL = PH * TOPK
NEXP = NK * NK
EPS = 1e-6
STAGES = 2
NEG_BIG = -3.4028234e38
NBANK = 8
RING = 8

F32 = mybir.dt.float32
U32 = mybir.dt.uint32
I32 = mybir.dt.int32
ALU = mybir.AluOpType
ACT = mybir.ActivationFunctionType
AX = mybir.AxisListType

SLOT_P, SLOT_K, SLOT_V, SLOT_Q = 0, 4, 5, 6
SLOT_MERGE = 10
SLOT_OUT = SLOT_MERGE + 3 * KD
SLOT_PQ = SLOT_OUT + KD
NSLOT = SLOT_PQ + 2 * PH

C_IDENT = 0
C_PERM = C_IDENT + P
C_ROWS = C_PERM + P
C_MASK = C_ROWS + P
C_IOTA = C_MASK + 4 * WK
NCONST = C_IOTA + P
V_GMIX, V_GFFN, V_PSCALE = 0, KD, 2 * KD
V_SINK = V_PSCALE + NPOOL
NVEC = V_SINK + NH
R_COS, R_SIN, R_CNT = 0, TG, 2 * TG
NROPE = R_CNT + NPOOL * PAD


def mixer_jobs():
    jobs = [("xT", k) for k in range(KD)]
    jobs += [("p", j) for j in range(NPOOL)] + [("k",), ("v",), ("rot", 0)]
    for j in range(4):
        jobs += [("q", j)]
        if j:
            jobs += [("rot", j)]
    jobs += [("grp", 0), ("rot", 4)] + [("grp", j) for j in range(1, NPOOL)]
    jobs += [("sc", 0, i) for i in range(4)]
    for t in range(TT):
        jobs += [("pT", t, i) for i in range(4)]
        if t + 1 < TT:
            jobs += [("sc", t + 1, i) for i in range(4)]
        jobs += [("pv", t), ("yaT", t)]
    for m in range(KD):
        jobs += [("gp", m), ("ga", m), ("bp", m), ("ba", m)]
    jobs += [("xo", t, n) for t in range(TT) for n in range(2)]
    jobs += [("xT2", k) for k in range(KD)]
    jobs += [("pq", 0, 0), ("pq", 0, 1)]
    for h in range(PH):
        for i in range(2):
            if h + 1 < PH:
                jobs += [("pq", h + 1, i)]
            jobs += [("ss", h, i)]
    return {job: n for n, job in enumerate(jobs)}


JOBS = mixer_jobs()
NJ = len(JOBS)
NJ += -NJ % NBANK
SLOT_READER = ([("p", j) for j in range(NPOOL)] + [("k",), ("v",)] + [("q", j) for j in range(4)]
               + [(n, m) for m in range(KD) for n in ("gp", "ga", "ba")]
               + [("xo", TT - 1, 1)] * KD + [("pq", h, i) for h in range(PH) for i in range(2)])


def mixer(nc, io, scr):
    with ExitStack() as ctx:
        def sb(name, shape, dt=F32):
            return ctx.enter_context(nc.sbuf_tensor(name, shape, dt))

        def sem(name):
            return ctx.enter_context(nc.semaphore(name))

        banks = [ctx.enter_context(nc.psum_tensor(f"bank{i}", [P, 512], F32)) for i in range(NBANK)]

        const = sb("const", [P, NCONST])
        vecs = sb("vecs", [P, NVEC])
        keys = sb("keys", [P, 2, NK])
        wgrp = sb("wgrp", [P, NPOOL, P])
        gffn = sb("gffn", [P, D])
        rope = sb("rope", [P, NROPE])
        ring = sb("ring", [P, RING, D])
        x = sb("x", [P, TT, D])
        h = sb("h", [P, TT, D])
        hT = sb("hT", [P, KD, TG])
        pT = sb("pT", [P, NPOOL, PAD + TG])
        sums = sb("sums", [P, 2, PAD + TG])
        pooled = sb("pooled", [P, NPOOL, TG])
        ypT = sb("ypT", [P, NPOOL, TG])
        raw = sb("raw", [P, 2, TG])
        rot = sb("rot", [P, 2, TG])
        qz = sb("qz", [P, NH, TG])
        kT = sb("kT", [P, CH + TG])
        v = sb("v", [P, 1 + TT, P])
        pr = sb("pr", [P, NH, 2 * P])
        prT = sb("prT", [P, 2 * NH, P])
        ya = sb("ya", [P, NH * HD])
        yaT = sb("yaT", [P, 4, TG])
        sg = sb("sg", [P, 2, 2, TG])
        smask = sb("smask", [P, 2 * NK])
        small = sb("small", [P, 72])
        vtop = sb("vtop", [P, 2, TOPK])
        itop = sb("itop", [P, 2, TT, TOPK], U32)
        itopf = sb("itopf", [P, 2, TT, TOPK])
        cand = sb("cand", [P, TOPK, TOPK])
        cmask = sb("cmask", [P, TOPK * TOPK])
        ctop = sb("ctop", [P, TT, TOPK], U32)
        cij = sb("cij", [P, 2, TT, TOPK], U32)
        cijf = sb("cijf", [P, 2, TT, TOPK])
        sel = sb("sel", [P, 2, TT, NSEL])
        vals = sb("vals", [P, TT, TOPK])
        gsm = sb("gsm", [P, 2, TT])
        eidx = sb("eidx", [P, TT, NSEL], I32)
        gate = sb("gate", [P, TT, NSEL])

        mT = h[:].rearrange("p t d -> p (t d)").rearrange("p (k n) -> p k n", k=KD)
        qd = ypT
        s12 = pooled[:].rearrange("p a n -> p (a n)").rearrange("p (h i t c) -> p h i t c", h=2, i=2, t=TT)
        hit = sums[:].rearrange("p a n -> p (a n)")[:, 0:TT * TOPK * TOPK].rearrange("p (n j) -> p n j", j=TOPK)
        ident = const[:, C_IDENT:C_IDENT + P]
        ssq, var, std, rinv, tmp = (small[:, 4 * i:4 * i + 4] for i in range(5))
        mx, negm, sarg, es, rs, den = (small[:, 24 + 8 * i:32 + 8 * i] for i in range(6))

        consts_in = sem("consts_in")
        x_in = sem("x_in")
        rope_in = sem("rope_in")
        slot_in = [sem(f"slot_in{i}") for i in range(RING)]
        job_full = sem("job_full")
        ssq_ready = sem("ssq_ready")
        var_ready = sem("var_ready")
        std_ready = sem("std_ready")
        rinv_ready = sem("rinv_ready")
        h_ready = sem("h_ready")
        hT_ready = sem("hT_ready")
        p_ready = sem("p_ready")
        raw_ready = sem("raw_ready")
        roped = sem("roped")
        v_ready = sem("v_ready")
        pooled_ready = sem("pooled_ready")
        yp_ready = sem("yp_ready")
        m_ready = sem("m_ready")
        exp_ready = sem("exp_ready")
        prT_ready = sem("prT_ready")
        ya_ready = sem("ya_ready")
        yaT_ready = sem("yaT_ready")
        sig_ready = sem("sig_ready")
        merged = sem("merged")
        x2_ready = sem("x2_ready")
        x2_out = sem("x2_out")
        h2_ready = sem("h2_ready")
        h2_out = sem("h2_out")
        h2T_out = sem("h2T_out")
        qd_ready = sem("qd_ready")
        ss_ready = sem("ss_ready")
        garg_ready = sem("garg_ready")
        gexp_ready = sem("gexp_ready")
        topk_done = sem("topk_done")
        choice_out = sem("choice_out")
        zeroed = sem("zeroed")
        carried = sem("carried")
        dve_own = sem("dve_own")
        pool_own = sem("pool_own")

        frees = {}
        for k in range(KD):
            frees["xT", k] = (hT_ready, k + 1, 2 * KD)
            frees["xT2", k] = (hT_ready, KD + k + 1, 2 * KD)
        for j in range(NPOOL):
            frees["p", j] = (p_ready, j + 1, NPOOL)
            frees["grp", j] = (yp_ready, j + 1, NPOOL)
            frees["q", j] = (raw_ready, j + 2, 5)
        frees["k",] = (raw_ready, 1, 5)
        frees["v",] = (v_ready, 1, 1)
        for i in range(5):
            frees["rot", i] = (roped, i + 1, 5)
        for t in range(TT):
            for i in range(4):
                frees["sc", t, i] = (exp_ready, 9 * t + 2 * i + 2, 9 * TT)
                frees["pT", t, i] = (prT_ready, 4 * t + i + 1, 4 * TT)
            frees["pv", t] = (ya_ready, t + 1, TT)
            frees["yaT", t] = (yaT_ready, t + 1, TT)
            for n in range(2):
                frees["xo", t, n] = (x2_ready, 2 * t + n + 1, 2 * TT)
        for m in range(KD):
            frees["gp", m] = (sig_ready, 2 * m + 1, 2 * KD)
            frees["ga", m] = (sig_ready, 2 * m + 2, 2 * KD)
            frees["bp", m] = frees["ba", m] = (merged, m + 1, KD)
        for hd in range(PH):
            for i in range(2):
                frees["pq", hd, i] = (qd_ready, 2 * hd + i + 1, 2 * PH)
                frees["ss", hd, i] = (ss_ready, 2 * hd + i + 1, 2 * PH)
        by_number = {n: job for job, n in JOBS.items()}

        def bank(*job):
            return banks[JOBS[job] % NBANK]

        def wait_job(eng, g, *job):
            eng.wait_ge(job_full, (g + 1) * NJ + JOBS[job] + 1)

        block = ctx.enter_context(nc.Block())

        @block.sync
        def _(sp):
            for dst, src in ((const, io["const"]), (vecs, io["vecs"]), (keys, io["keys"]),
                             (wgrp, io["wgrp"]), (gffn, io["gffn"])):
                sp.dma_start(dst[:], src).then_inc(consts_in, 16)
            with sp.Fori(0, NG) as g:
                sp.wait_ge(carried, g + 1)
                sp.dma_start(x[:], io["x"][bass.ds(g, 1)].rearrange("a t p d -> p (a t) d")).then_inc(x_in, 16)
                sp.dma_start(rope[:], io["rope"][bass.ds(g, 1)].rearrange("a p n -> p (a n)")).then_inc(rope_in, 16)
                for s in range(NSLOT):
                    before = [r for r in range(s % RING, NSLOT, RING) if r < s] or [
                        r - NSLOT for r in range(s % RING, NSLOT, RING)]
                    r = before[-1]
                    sp.wait_ge(job_full, (g + (1 if r >= 0 else 0)) * NJ + JOBS[SLOT_READER[r % NSLOT]] + 1)
                    sp.dma_start(ring[:, s % RING], io["slots"][s]).then_inc(slot_in[s % RING], 16)
                    if s == SLOT_PQ + 5:
                        for t in range(TT):
                            sp.wait_ge(x2_ready, g * 2 * TT + 2 * t + 2)
                            sp.dma_start(scr["x2"][bass.ds(g * TT + t, 1)].rearrange("a p d -> p (a d)"),
                                         x[:, t]).then_inc(x2_out, 16)
                for t in range(TT):
                    sp.wait_ge(h2_ready, g * TT + t + 1)
                    sp.dma_start(scr["h2"][bass.ds(g * TT + t, 1)].rearrange("a p d -> p (a d)"),
                                 x[:, t]).then_inc(h2_out, 16)
                sp.wait_ge(hT_ready, g * 2 * KD + 2 * KD)
                sp.dma_start(scr["h2T"][bass.ds(g, 1)].rearrange("a p n -> p (a n)"),
                             hT[:].rearrange("p k n -> p (k n)")).then_inc(h2T_out, 16)
                sp.wait_ge(topk_done, g * PH + PH)
                for i, name in enumerate(("sel1", "sel2")):
                    sp.dma_start(scr[name][bass.ds(g * TT, TT)].rearrange("t p n -> p t n"), sel[:, i]).then_inc(choice_out, 16)
                sp.dma_start(scr["eidx"][bass.ds(g * TT, TT)].rearrange("t p n -> p t n"), eidx[:]).then_inc(choice_out, 16)
                sp.dma_start(scr["gate"][bass.ds(g * TT, TT)].rearrange("t p n -> p t n"), gate[:]).then_inc(choice_out, 16)
            sp.wait_ge(x2_out, 16 * NBLK)
            sp.wait_ge(h2_out, 16 * NBLK)
            sp.wait_ge(choice_out, 64 * NG)
            sp.wait_ge(h2T_out, 16 * NG)

        def slot_uses(q):
            return len(range(q, NSLOT, RING))

        @block.tensor
        def _(pe):
            pe.sem_inc(job_full, NJ)
            pe.wait_ge(consts_in, 16 * 5)
            with pe.Fori(0, NG) as g:
                def begin(*job):
                    n = JOBS[job]
                    if n >= NBANK:
                        s, c, per = frees[by_number[n - NBANK]]
                        pe.wait_ge(s, g * per + c)
                    return banks[n % NBANK]

                def weights(s):
                    pe.wait_ge(slot_in[s % RING], 16 * (g * slot_uses(s % RING) + s // RING + 1))
                    return ring[:, s % RING]

                def product(out, w, act, ks):
                    for i, k in enumerate(ks):
                        ins = nc.tensor.matmul(out[:], w[:, k * P:(k + 1) * P], act[:, i],
                                               start=i == 0, stop=i == len(ks) - 1)
                    ins.then_inc(job_full, 1)

                def project(job, s, act=hT, ks=range(KD)):
                    out = begin(*job)
                    w = weights(s)
                    product(out, w, act, ks)

                def turn(job, src):
                    out = begin(*job)
                    for i, a in enumerate(src):
                        ins = nc.tensor.transpose(out[:, i * P:(i + 1) * P], a, ident)
                    ins.then_inc(job_full, 1)

                pe.wait_ge(h_ready, g * 2 * TT + TT)
                for k in range(KD):
                    turn(("xT", k), [h[:, t, k * P:(k + 1) * P] for t in range(TT)])
                pe.wait_ge(hT_ready, g * 2 * KD + KD)
                for j in range(NPOOL):
                    project(("p", j), SLOT_P + j)
                project(("k",), SLOT_K)
                out = begin("v")
                w = weights(SLOT_V)
                for t in range(TT):
                    for k in range(KD):
                        ins = nc.tensor.matmul(out[:, t * P:(t + 1) * P], hT[:, k, t * P:(t + 1) * P],
                                               w[:, k * P:(k + 1) * P], start=k == 0, stop=k == KD - 1)
                ins.then_inc(job_full, 1)

                def partner(i):
                    out = begin("rot", i)
                    pe.wait_ge(raw_ready, g * 5 + i + 1)
                    nc.tensor.matmul(out[:], const[:, C_PERM:C_PERM + P], raw[:, i % 2],
                                     start=True, stop=True).then_inc(job_full, 1)

                def group(j):
                    out = begin("grp", j)
                    pe.wait_ge(pooled_ready, g * NPOOL + j + 1)
                    nc.tensor.matmul(out[:], wgrp[:, j], pooled[:, j], start=True, stop=True).then_inc(job_full, 1)

                partner(0)
                for j in range(4):
                    project(("q", j), SLOT_Q + j)
                    if j:
                        partner(j)
                group(0)
                partner(4)
                for j in range(1, NPOOL):
                    group(j)

                def scores(t):
                    if t == 0:
                        pe.wait_ge(roped, g * 5 + 5)
                        pe.wait_ge(carried, g + 1)
                    mask = const[:, C_MASK:C_MASK + 2 * WK] if t == 0 else const[:, C_MASK + 2 * WK:C_MASK + 4 * WK]
                    for i in range(4):
                        out = begin("sc", t, i)
                        nc.tensor.matmul(out[:, 0:2 * WK], const[:, C_ROWS:C_ROWS + P], mask, start=True, stop=False)
                        for e in range(2):
                            ins = nc.tensor.matmul(out[:, e * WK:(e + 1) * WK], qz[:, 2 * i + e, t * P:(t + 1) * P],
                                                   kT[:, t * P:t * P + WK], start=False, stop=e == 1)
                        ins.then_inc(job_full, 1)

                scores(0)
                for t in range(TT):
                    for i in range(4):
                        pe.wait_ge(exp_ready, g * 9 * TT + 9 * t + 2 * i + 2)
                        turn(("pT", t, i), [pr[:, 2 * i + e // 2, (e % 2) * P:(e % 2 + 1) * P] for e in range(4)])
                    if t + 1 < TT:
                        scores(t + 1)
                    out = begin("pv", t)
                    pe.wait_ge(prT_ready, g * 4 * TT + 4 * t + 4)
                    if t == 0:
                        pe.wait_ge(v_ready, g + 1)
                    for hd in range(NH):
                        kv = slice(hd // 4 * HD, (hd // 4 + 1) * HD)
                        nc.tensor.matmul(out[:, hd * HD:(hd + 1) * HD], prT[:, 2 * hd], v[:, t, kv], start=True, stop=False)
                        ins = nc.tensor.matmul(out[:, hd * HD:(hd + 1) * HD], prT[:, 2 * hd + 1], v[:, t + 1, kv],
                                               start=False, stop=True)
                    ins.then_inc(job_full, 1)
                    pe.wait_ge(ya_ready, g * TT + t + 1)
                    turn(("yaT", t), [ya[:, j * P:(j + 1) * P] for j in range(4)])

                for m in range(KD):
                    s = SLOT_MERGE + 3 * m
                    project(("gp", m), s)
                    project(("ga", m), s + 1)
                    w = weights(s + 2)
                    if m == 0:
                        pe.wait_ge(yp_ready, g * NPOOL + NPOOL)
                        pe.wait_ge(yaT_ready, g * TT + TT)
                    product(begin("bp", m), w, ypT, range(4))
                    product(begin("ba", m), w, yaT, range(4, 8))

                wo = [weights(SLOT_OUT + k) for k in range(KD)]
                pe.wait_ge(merged, g * KD + KD)
                for t in range(TT):
                    for n in range(2):
                        out = begin("xo", t, n)
                        for k in range(KD):
                            ins = nc.tensor.matmul(out[:], mT[:, k, t * P:(t + 1) * P], wo[k][:, n * 512:(n + 1) * 512],
                                                   start=k == 0, stop=k == KD - 1)
                        ins.then_inc(job_full, 1)

                pe.wait_ge(h_ready, g * 2 * TT + 2 * TT)
                for k in range(KD):
                    turn(("xT2", k), [h[:, t, k * P:(k + 1) * P] for t in range(TT)])
                pe.wait_ge(hT_ready, g * 2 * KD + 2 * KD)
                project(("pq", 0, 0), SLOT_PQ)
                project(("pq", 0, 1), SLOT_PQ + 1)
                for hd in range(PH):
                    for i in range(2):
                        if hd + 1 < PH:
                            project(("pq", hd + 1, i), SLOT_PQ + 2 * hd + 2 + i)
                        out = begin("ss", hd, i)
                        pe.wait_ge(qd_ready, g * 2 * PH + 2 * hd + i + 1)
                        for t in range(TT):
                            ins = nc.tensor.matmul(out[:, t * P:(t + 1) * P], qd[:, (2 * hd + i) % 4, t * P:(t + 1) * P],
                                                   keys[:, i], start=True, stop=True)
                        ins.then_inc(job_full, 1)
                pe.wait_ge(ss_ready, g * 2 * PH + 2 * PH)
                pe.wait_ge(qd_ready, g * 2 * PH + 2 * PH)
                pe.sem_inc(job_full, NJ - len(JOBS))

        @block.scalar
        def _(act):
            act.wait_ge(consts_in, 16 * 5)
            with act.Fori(0, NG) as g:
                def norm(n):
                    if n == 1:
                        act.wait_ge(x2_ready, g * 2 * TT + 2 * TT)
                    for t in range(TT):
                        ins = nc.scalar.activation(h[:, t], x[:, t], ACT.Square, accum_out=ssq[:, t:t + 1])
                    ins.then_inc(ssq_ready, 1)
                    act.wait_ge(var_ready, 2 * g + n + 1)
                    nc.scalar.activation(std, var, ACT.Sqrt).then_inc(std_ready, 1)
                    act.wait_ge(rinv_ready, 2 * g + n + 1)
                    for t in range(TT):
                        nc.scalar.activation(h[:, t], x[:, t], ACT.Copy, scale=rinv[:, t:t + 1]).then_inc(h_ready, 1)
                    for k in range(KD):
                        job = ("xT2" if n else "xT", k)
                        wait_job(act, g, *job)
                        gain = vecs[:, (V_GFFN if n else V_GMIX) + k:(V_GFFN if n else V_GMIX) + k + 1]
                        nc.scalar.activation(hT[:, k], bank(*job)[:], ACT.Copy, scale=gain).then_inc(hT_ready, 1)

                act.wait_ge(x_in, 16 * (g + 1))
                act.wait_ge(carried, g + 1)
                norm(0)
                for j in range(NPOOL):
                    wait_job(act, g, "p", j)
                    nc.scalar.activation(pT[:, j, PAD:], bank("p", j)[:], ACT.Copy).then_inc(p_ready, 1)

                def keep_raw(i, *job):
                    wait_job(act, g, *job)
                    if i >= 2:
                        act.wait_ge(roped, g * 5 + i - 1)
                    nc.scalar.activation(raw[:, i % 2], bank(*job)[:], ACT.Copy).then_inc(raw_ready, 1)

                keep_raw(0, "k")
                wait_job(act, g, "v")
                nc.scalar.activation(v[:, 1:1 + TT].rearrange("p t c -> p (t c)"), bank("v")[:], ACT.Copy).then_inc(v_ready, 1)
                for j in range(4):
                    keep_raw(1 + j, "q", j)
                for j in range(NPOOL):
                    wait_job(act, g, "grp", j)
                    nc.scalar.activation(ypT[:, j], bank("grp", j)[:], ACT.Copy,
                                         scale=vecs[:, V_PSCALE + j:V_PSCALE + j + 1]).then_inc(yp_ready, 1)

                def expon(t):
                    act.wait_ge(m_ready, g * TT + t + 1)
                    if t:
                        wait_job(act, g, "pT", t - 1, 3)
                        act.wait_ge(ya_ready, g * TT + t)
                    for hd in range(NH):
                        src = bank("sc", t, hd // 2)[:, hd % 2 * WK:(hd % 2 + 1) * WK]
                        nc.scalar.activation(pr[:, hd, CH:], src, ACT.Exp, bias=negm[:, hd:hd + 1], scale=HD ** -0.5,
                                             accum_out=rs[:, hd:hd + 1]).then_inc(exp_ready, 1)
                    nc.scalar.activation(es, sarg, ACT.Exp).then_inc(exp_ready, 1)

                for t in range(TT):
                    expon(t)
                    wait_job(act, g, "yaT", t)
                    nc.scalar.activation(yaT[:, :, t * P:(t + 1) * P],
                                         bank("yaT", t)[:].rearrange("p (j c) -> p j c", j=4), ACT.Copy).then_inc(yaT_ready, 1)

                for m in range(KD):
                    if m >= 2:
                        act.wait_ge(merged, g * KD + m - 1)
                    for i, n in enumerate(("gp", "ga")):
                        wait_job(act, g, n, m)
                        nc.scalar.activation(sg[:, m % 2, i], bank(n, m)[:], ACT.Sigmoid).then_inc(sig_ready, 1)

                norm(1)

                def keep_q(hd, i):
                    n = 2 * hd + i
                    wait_job(act, g, "pq", hd, i)
                    if n >= 4:
                        wait_job(act, g, "ss", (n - 4) // 2, i)
                    nc.scalar.activation(qd[:, n % 4], bank("pq", hd, i)[:], ACT.Copy).then_inc(qd_ready, 1)

                keep_q(0, 0)
                keep_q(0, 1)
                for hd in range(PH):
                    for i in range(2):
                        if hd + 1 < PH:
                            keep_q(hd + 1, i)
                        wait_job(act, g, "ss", hd, i)
                        if hd >= 2:
                            act.wait_ge(topk_done, g * PH + hd - 1)
                        nc.scalar.activation(s12[:, hd % 2, i].rearrange("p t c -> p (t c)"), bank("ss", hd, i)[:],
                                             ACT.Copy).then_inc(ss_ready, 1)
                    if hd:
                        act.wait_ge(garg_ready, g * PH + hd)
                        nc.scalar.activation(vals[:], vals[:], ACT.Exp).then_inc(gexp_ready, 1)
                act.wait_ge(garg_ready, g * PH + PH)
                nc.scalar.activation(vals[:], vals[:], ACT.Exp).then_inc(gexp_ready, 1)

        @block.gpsimd
        def _(pool):
            nc.gpsimd.memset(qz[:], 0.0)
            nc.gpsimd.memset(pr[:], 0.0)
            nc.gpsimd.memset(pT[:, :, 0:PAD], 0.0)
            nc.gpsimd.memset(kT[:, 0:CH], 0.0)
            nc.gpsimd.memset(v[:, 0], 0.0).then_inc(carried, 1)
            pool.wait_ge(consts_in, 16 * 5)
            with pool.Fori(0, NG) as g:
                own = [0]

                def link(ins):
                    own[0] += 1
                    ins.then_inc(pool_own, 1)
                    pool.wait_ge(pool_own, own[0])

                pool.wait_ge(rope_in, 16 * (g + 1))
                for j in range(NPOOL):
                    pool.wait_ge(p_ready, g * NPOOL + j + 1)
                    src, lo = pT[:, j], 0
                    for i in range(j + 1):
                        lo += 1 << i
                        dst = sums[:, i % 2]
                        link(nc.gpsimd.tensor_tensor(dst[:, lo:], src[:, lo:], src[:, lo - (1 << i):PAD + TG - (1 << i)], ALU.add))
                        src = dst
                    head = src[:, PAD:2 * PAD]
                    link(nc.gpsimd.tensor_tensor(head, head, rope[:, R_CNT + j * PAD:R_CNT + (j + 1) * PAD], ALU.mult))
                    link(nc.gpsimd.tensor_scalar(src[:, PAD:], src[:, PAD:], 1.0 / (2 << j), None, ALU.mult))
                    nc.gpsimd.tensor_tensor(pooled[:, j], src[:, PAD:], pT[:, j, PAD:], ALU.subtract).then_inc(pooled_ready, 1)
                    pool.wait_ge(pooled_ready, g * NPOOL + j + 1)

                for t in range(TT):
                    pool.wait_ge(h_ready, g * 2 * TT + TT + t + 1)
                    pool.wait_ge(x2_out, 16 * (g * TT + TT))
                    nc.gpsimd.tensor_tensor(x[:, t], h[:, t], gffn[:], ALU.mult).then_inc(h2_ready, 1)

                pool.wait_ge(job_full, (g + 1) * NJ + NJ)
                own[0] += 1
                pool.sem_inc(pool_own, 1)
                link(nc.gpsimd.tensor_copy(pT[:, :, 0:PAD], pT[:, :, TG:TG + PAD]))
                link(nc.gpsimd.tensor_copy(kT[:, 0:CH], kT[:, TG:TG + CH]))
                link(nc.gpsimd.tensor_copy(v[:, 0], v[:, TT]))
                link(nc.gpsimd.tensor_copy(const[:, C_MASK:C_MASK + 2 * WK], const[:, C_MASK + 2 * WK:C_MASK + 4 * WK]))
                pool.wait_ge(choice_out, 64 * (g + 1))
                pool.wait_ge(h2T_out, 16 * (g + 1))
                pool.wait_ge(h2_out, 16 * TT * (g + 1))
                pool.sem_inc(carried, 1)
                pool.sem_clear(pool_own)

        @block.vector
        def _(dve):
            dve.wait_ge(consts_in, 16 * 5)
            with dve.Fori(0, NG) as g:
                own = [0]

                def link(ins):
                    own[0] += 1
                    ins.then_inc(dve_own, 1)
                    dve.wait_ge(dve_own, own[0])

                def mark(ins):
                    own[0] += 1
                    ins.then_inc(dve_own, 1)

                def linked():
                    dve.wait_ge(dve_own, own[0])

                def norm(n):
                    dve.wait_ge(ssq_ready, 2 * g + n + 1)
                    nc.vector.tensor_scalar(var, ssq, 1.0 / D, EPS, ALU.mult, ALU.add).then_inc(var_ready, 1)
                    dve.wait_ge(std_ready, 2 * g + n + 1)
                    link(nc.vector.reciprocal(rinv, std))
                    link(nc.vector.tensor_tensor(tmp, rinv, rinv, ALU.mult))
                    link(nc.vector.tensor_tensor(tmp, tmp, var, ALU.mult))
                    link(nc.vector.tensor_scalar(tmp, tmp, -0.5, 1.5, ALU.mult, ALU.add))
                    nc.vector.tensor_tensor(rinv, rinv, tmp, ALU.mult).then_inc(rinv_ready, 1)

                norm(0)

                dve.wait_ge(rope_in, 16 * (g + 1))
                dve.wait_ge(carried, g + 1)
                for i in range(5):
                    dve.wait_ge(raw_ready, g * 5 + i + 1)
                    mark(nc.vector.tensor_tensor(rot[:, 0], raw[:, i % 2], rope[:, R_COS:R_COS + TG], ALU.mult))
                    wait_job(dve, g, "rot", i)
                    link(nc.vector.tensor_tensor(rot[:, 1], bank("rot", i)[:], rope[:, R_SIN:R_SIN + TG], ALU.mult))
                    if i == 0:
                        nc.vector.tensor_tensor(kT[:, CH:], rot[:, 0], rot[:, 1], ALU.add).then_inc(roped, 1)
                    else:
                        mark(nc.vector.tensor_tensor(qz[0:HD, i - 1], rot[0:HD, 0], rot[0:HD, 1], ALU.add))
                        nc.vector.tensor_tensor(qz[HD:P, i + 3], rot[HD:P, 0], rot[HD:P, 1], ALU.add).then_inc(roped, 1)
                    dve.wait_ge(roped, g * 5 + i + 1)

                sink = vecs[:, V_SINK:V_SINK + NH]

                def maxima(t):
                    for i in range(4):
                        wait_job(dve, g, "sc", t, i)
                        mark(nc.vector.tensor_reduce(mx[:, 2 * i:2 * i + 2],
                                                     bank("sc", t, i)[:, 0:2 * WK].rearrange("p (e c) -> p e c", e=2),
                                                     AX.X, ALU.max))
                    linked()
                    if t:
                        dve.wait_ge(exp_ready, g * 9 * TT + 9 * t)
                    link(nc.vector.scalar_tensor_tensor(out=mx, in0=mx, scalar=HD ** -0.5, in1=sink, op0=ALU.mult, op1=ALU.max))
                    mark(nc.vector.tensor_scalar(negm, mx, -1.0, None, ALU.mult))
                    nc.vector.tensor_tensor(sarg, sink, mx, ALU.subtract).then_inc(m_ready, 1)
                    dve.wait_ge(m_ready, g * TT + t + 1)

                for t in range(TT):
                    maxima(t)
                    for i in range(4):
                        wait_job(dve, g, "pT", t, i)
                        nc.vector.tensor_copy(prT[:, 4 * i:4 * i + 4].rearrange("p a c -> p (a c)"),
                                              bank("pT", t, i)[:]).then_inc(prT_ready, 1)
                    dve.wait_ge(exp_ready, g * 9 * TT + 9 * t + 9)
                    link(nc.vector.tensor_tensor(den, rs, es, ALU.add))
                    link(nc.vector.reciprocal(den, den))
                    wait_job(dve, g, "pv", t)
                    nc.vector.tensor_tensor(ya[:].rearrange("p (a c) -> p a c", a=NH),
                                            bank("pv", t)[:].rearrange("p (a c) -> p a c", a=NH),
                                            den.unsqueeze(2).to_broadcast([P, NH, HD]), ALU.mult).then_inc(ya_ready, 1)

                for m in range(KD):
                    for i, n in enumerate(("bp", "ba")):
                        wait_job(dve, g, n, m)
                        dve.wait_ge(sig_ready, g * 2 * KD + 2 * m + 1 + i)
                        mark(nc.vector.tensor_tensor(sg[:, m % 2, i], bank(n, m)[:], sg[:, m % 2, i], ALU.mult))
                    linked()
                    nc.vector.tensor_tensor(mT[:, m], sg[:, m % 2, 0], sg[:, m % 2, 1], ALU.add).then_inc(merged, 1)

                for t in range(TT):
                    for n in range(2):
                        wait_job(dve, g, "xo", t, n)
                        part = x[:, t, n * 512:(n + 1) * 512]
                        nc.vector.tensor_tensor(part, part, bank("xo", t, n)[:], ALU.add).then_inc(x2_ready, 1)

                norm(1)

                def top16(scores, masked, values, places):
                    link(nc.vector.max(values[:, 0:8], scores))
                    mark(nc.vector.max_index(places[:, 0:8], values[:, 0:8], scores))
                    link(nc.vector.match_replace(masked, values[:, 0:8], scores, NEG_BIG))
                    link(nc.vector.max(values[:, 8:16], masked))
                    mark(nc.vector.max_index(places[:, 8:16], values[:, 8:16], masked))

                iota = const[:, C_IOTA:C_IOTA + TOPK]
                for hd in range(PH):
                    dve.wait_ge(ss_ready, g * 2 * PH + 2 * hd + 2)
                    own[0] += 1
                    dve.sem_inc(dve_own, 1)
                    for t in range(TT):
                        for i in range(2):
                            top16(s12[:, hd % 2, i, t], smask[:, i * NK:(i + 1) * NK], vtop[:, i], itop[:, i, t])
                        linked()
                        link(nc.vector.tensor_tensor(cand[:], vtop[:, 0].unsqueeze(2).to_broadcast([P, TOPK, TOPK]),
                                                     vtop[:, 1].unsqueeze(1).to_broadcast([P, TOPK, TOPK]), ALU.add))
                        top16(cand[:].rearrange("p a b -> p (a b)"), cmask[:], vals[:, t], ctop[:, t])
                    linked()
                    mark(nc.vector.tensor_scalar(cij[:, 0], ctop[:], 4, None, ALU.logical_shift_right))
                    mark(nc.vector.tensor_scalar(cij[:, 1], ctop[:], TOPK - 1, None, ALU.bitwise_and))
                    mark(nc.vector.tensor_copy(itopf[:], itop[:]))
                    mark(nc.vector.tensor_copy(gsm[:, 0], vals[:, :, 0]))
                    linked()
                    mark(nc.vector.tensor_copy(cijf[:], cij[:]))
                    nc.vector.tensor_tensor(vals[:], vals[:], gsm[:, 0].unsqueeze(2).to_broadcast([P, TT, TOPK]),
                                            ALU.subtract).then_inc(garg_ready, 1)
                    linked()
                    cols = slice(hd * TOPK, (hd + 1) * TOPK)
                    for i in range(2):
                        link(nc.vector.tensor_tensor(hit, cijf[:, i].rearrange("p t k -> p (t k)").unsqueeze(2)
                                                     .to_broadcast([P, TT * TOPK, TOPK]),
                                                     iota.unsqueeze(1).to_broadcast([P, TT * TOPK, TOPK]), ALU.is_equal))
                        hit4 = hit.rearrange("p (t k) j -> p t k j", t=TT)
                        link(nc.vector.tensor_tensor(hit4, hit4, itopf[:, i].unsqueeze(2).to_broadcast([P, TT, TOPK, TOPK]),
                                                     ALU.mult))
                        link(nc.vector.tensor_reduce(sel[:, i, :, cols], hit4, AX.X, ALU.add))
                    link(nc.vector.scalar_tensor_tensor(out=eidx[:, :, cols], in0=sel[:, 0, :, cols], scalar=float(NK),
                                                        in1=sel[:, 1, :, cols], op0=ALU.mult, op1=ALU.add))
                    dve.wait_ge(gexp_ready, g * PH + hd + 1)
                    link(nc.vector.tensor_reduce(gsm[:, 0], vals[:], AX.X, ALU.add))
                    link(nc.vector.reciprocal(gsm[:, 1], gsm[:, 0]))
                    nc.vector.tensor_tensor(gate[:, :, cols], vals[:], gsm[:, 1].unsqueeze(2).to_broadcast([P, TT, TOPK]),
                                            ALU.mult).then_inc(topk_done, 1)
                    dve.wait_ge(topk_done, g * PH + hd + 1)
                dve.sem_inc(dve_own, 1)
                dve.sem_clear(dve_own)
                dve.wait_ge(choice_out, 64 * (g + 1))


NQ = NK // 4
QT = 4
TC = 32
NTC = TG // TC


def gate_table(nc, io, scr):
    QUADS = 2 * TC // 4
    ROH = 4
    with ExitStack() as ctx:
        def sb(name, shape, dt=F32):
            return ctx.enter_context(nc.sbuf_tensor(name, shape, dt))

        def sem(name):
            return ctx.enter_context(nc.semaphore(name))

        const = sb("t_const", [P, NCONST])
        rows = sb("t_rows", [P, 3, TT, NSEL])
        cols = sb("t_cols", [P, 3, TG])
        hot = sb("hot", [P, ROH, 2, 4, P])
        out = sb("t_out", [P, 2, NQ, QT, TC])
        banks = [ctx.enter_context(nc.psum_tensor(f"tbank{i}", [P, 512], F32)) for i in range(ROH)]
        tbank = [ctx.enter_context(nc.psum_tensor(f"tturn{i}", [P, TG], F32)) for i in range(3)]

        rows_in, turned, cols_ready = sem("rows_in"), sem("turned"), sem("cols_ready")
        hot_ready = sem("hot_ready")
        quad_done = sem("quad_done")
        quad_kept = sem("quad_kept")
        chunk_out = [sem(f"chunk_out{i}") for i in range(2)]
        sp_waits = sem("t_sp_waits")
        chunk_free = [sem(f"chunk_free{i}") for i in range(2)]

        block = ctx.enter_context(nc.Block())
        iota = const[:, C_IOTA:C_IOTA + P]

        @block.sync
        def _(sp):
            sp.dma_start(const[:], io["const"]).then_inc(rows_in, 16)
            for i, name in enumerate(("sel1", "sel2", "gate")):
                sp.dma_start(rows[:, i], scr[name][TT:2 * TT].rearrange("t p n -> p t n")).then_inc(rows_in, 16)
            with sp.Fori(0, NTC // 2) as m:
                for i in range(2):
                    sp.wait_ge(quad_kept, QUADS * m + (i + 1) * QUADS // 2 + ROH)
                    sp.sem_inc(sp_waits, 1)
                    dst = scr["table"][:, :, bass.ds(2 * m + i, 1)].rearrange("q p a c -> p q (a c)")
                    sp.dma_start(dst, out[:, i].rearrange("p q e t -> p q (e t)")).then_inc(chunk_out[i], 16)
                for i in range(2):
                    sp.wait_ge(chunk_out[i], 16 * (m + 1))
                    sp.sem_inc(chunk_free[i], 1)

        @block.tensor
        def _(pe):
            pe.sem_inc(quad_done, ROH)
            pe.wait_ge(rows_in, 64)
            for i in range(3):
                for t in range(TT):
                    ins = nc.tensor.transpose(tbank[i][:, t * P:(t + 1) * P], rows[:, i, t], const[:, C_IDENT:C_IDENT + P])
                ins.then_inc(turned, 1)
            with pe.Fori(0, NTC // 2) as m:
                for u in range(QUADS):
                    pe.wait_ge(hot_ready, QUADS * m + u + 1)
                    pe.wait_ge(quad_kept, QUADS * m + u + 1)
                    for t in range(4):
                        ins = nc.tensor.matmul(banks[u % ROH][:, t * P:(t + 1) * P], hot[:, u % ROH, 1, t],
                                               hot[:, u % ROH, 0, t], start=True, stop=True)
                    ins.then_inc(quad_done, 1)

        @block.scalar
        def _(act):
            act.sem_inc(quad_kept, ROH)
            for i in range(3):
                act.wait_ge(turned, i + 1)
                nc.scalar.activation(cols[:, i], tbank[i][:], ACT.Copy).then_inc(cols_ready, 1)
            with act.Fori(0, NTC // 2) as m:
                for u in range(QUADS):
                    i, t = u // (QUADS // 2), u % (QUADS // 2) * 4
                    if t == 0:
                        act.wait_ge(chunk_free[i], m + 1)
                    act.wait_ge(quad_done, QUADS * m + u + 1 + ROH)
                    nc.scalar.activation(out[:, i].rearrange("p q e t -> p t (q e)")[:, t:t + 4],
                                         banks[u % ROH][:].rearrange("p (t i) -> p t i", t=4), ACT.Copy).then_inc(quad_kept, 1)

        @block.vector
        def _(dve):
            for i in range(2):
                dve.sem_inc(chunk_free[i], 1)
            dve.wait_ge(cols_ready, 3)
            with dve.Fori(0, NTC // 2) as m:
                for u in range(QUADS):
                    dve.wait_ge(quad_done, QUADS * m + u + 1)
                    for t in range(4):
                        tok = m * 2 * TC + 4 * u + t
                        first, second, gate = (cols[:, i, bass.ds(tok, 1)] for i in range(3))
                        nc.vector.tensor_scalar(hot[:, u % ROH, 0, t], iota, first, gate, ALU.is_equal, ALU.mult)
                        ins = nc.vector.tensor_scalar(hot[:, u % ROH, 1, t], iota, second, None, ALU.is_equal)
                    ins.then_inc(hot_ready, 1)


RD, RU = 8, 8
CHUNK = 4
NB1 = NBLK // 2
NSTEP = NB1 * PH
assert NSTEP == NQ


def experts(nc, io, scr):
    with ExitStack() as ctx:
        def sb(name, shape, dt=F32):
            return ctx.enter_context(nc.sbuf_tensor(name, shape, dt))

        def sem(name):
            return ctx.enter_context(nc.semaphore(name))

        next_h2, next_gate = sb("next_h2", [P, D]), sb("next_gate", [P, NSEL])
        next_idx = sb("next_idx", [P, NSEL], I32)
        h2, gate = sb("h2", [P, D]), sb("gate_now", [P, NSEL])
        idx_down, idx_up = sb("idx_down", [P, NSEL], I32), sb("idx_up", [P, NSEL], I32)
        down = sb("down", [P, RD, D])
        up = sb("up", [P, RU, D])
        acc, acc_out = sb("acc", [P, D]), sb("acc_out", [P, D])
        dots, gelu = sb("dots", [P, TOPK]), sb("gelu", [P, TOPK])
        wts = sb("wts", [P, 2, TOPK])
        h2T = sb("h2T", [P, KD, TG])
        tdown = sb("tdown", [P, QT, D])
        tup = sb("tup", [P, 2, QT, D])
        gates = sb("gates", [P, 2, NTC, QT, TC])
        gl = sb("gl", [P, 2, TG])
        w = sb("w", [P, 2, QT, TG])
        y = sb("y", [P, TT, D])
        abank = [ctx.enter_context(nc.psum_tensor(f"abank{i}", [P, TG], F32)) for i in range(2)]
        ybank = [ctx.enter_context(nc.psum_tensor(f"ybank{i}", [P, 512], F32)) for i in range(4)]

        idx_in, h2_in = sem("idx_in"), sem("h2_in")
        idx_taken, h2_taken = sem("idx_taken"), sem("h2_taken")
        idx_copied = sem("idx_copied")
        pool_waits, sp_waits = sem("pool_waits"), sem("sp_waits")
        down_in = [sem(f"down_in{i}") for i in range(RD)]
        up_in = [sem(f"up_in{i}") for i in range(RU)]
        dot_done = sem("dot_done")
        up_used = sem("up_used")
        gelu_ready, wts_ready = sem("gelu_ready"), sem("wts_ready")
        acc_ready = sem("acc_ready")
        acc_copied = sem("acc_copied")
        acc_stored = sem("acc_stored")
        acc_free = sem("acc_free")
        h2T_in = sem("h2T_in")
        tdown_in = [sem(f"tdown_in{i}") for i in range(QT)]
        tup_in = [sem(f"tup_in{i}") for i in range(2 * QT)]
        gates_in = [sem(f"gates_in{i}") for i in range(2)]
        a_ready = sem("a_ready")
        gl_ready = sem("gl_ready")
        w_ready = sem("w_ready")
        y_ready = sem("y_ready")
        y_added = sem("y_added")
        y_stored = sem("y_stored")
        y_zero = sem("y_zero")
        dve_own = sem("e_dve_own")

        block = ctx.enter_context(nc.Block())

        def blocks(eng, one):
            with eng.Fori(0, NB1 - 1) as b:
                one(b, False)
            one(NB1 - 1, True)

        def at(dram, i):
            return dram[i] if isinstance(i, int) else dram[bass.ds(i, 1)].rearrange("a p n -> p (a n)")

        @block.sync
        def _(sp):
            def hold(sem, count):
                sp.wait_ge(sem, count)
                sp.sem_inc(sp_waits, 1)

            def load_tdown(n, q):
                sp.dma_start(tdown[:, q], at(io["downT"], 4 * n + q)).then_inc(tdown_in[q], 16)

            def load_tup(n, par, q):
                sp.dma_start(tup[:, par, q], at(up_tiles, 4 * n + q)).then_inc(tup_in[par * QT + q], 16)

            def load_gates(n, par):
                sp.dma_start(gates[:, par].rearrange("p c e t -> p (c e t)"), at(table, n)).then_inc(gates_in[par], 16)

            up_tiles = io["up"].rearrange("(e p) d -> e p d", p=P)
            table = scr["table"].rearrange("q p c n -> q p (c n)")
            sp.dma_start(next_idx[:], scr["eidx"][0]).then_inc(idx_in, 16)
            sp.dma_start(next_h2[:], scr["h2"][0]).then_inc(h2_in, 16)
            sp.dma_start(next_gate[:], scr["gate"][0]).then_inc(h2_in, 16)
            sp.dma_start(h2T[:].rearrange("p k n -> p (k n)"), scr["h2T"][1]).then_inc(h2T_in, 16)
            for q in range(QT):
                load_tdown(0, q)
            load_gates(0, 0)
            for q in range(QT):
                load_tup(0, 0, q)
                hold(a_ready, q + 1)
                load_tdown(1, q)
            load_gates(1, 1)

            def one(b, last):
                for h in range(PH):
                    n = b * PH + h
                    if h == 0 and not last:
                        hold(idx_taken, b + 1)
                        sp.dma_start(next_idx[:], at(scr["eidx"], b + 1)).then_inc(idx_in, 16)
                        hold(h2_taken, b + 1)
                        sp.dma_start(next_h2[:], at(scr["h2"], b + 1)).then_inc(h2_in, 16)
                        sp.dma_start(next_gate[:], at(scr["gate"], b + 1)).then_inc(h2_in, 16)
                    for q in range(QT):
                        if not (last and h == PH - 1):
                            hold(y_ready, 2 * TT * (n + 1))
                            load_tup(n + 1, (h + 1) % 2, q)
                        if not (last and h >= PH - 2):
                            hold(a_ready, QT * (n + 1) + q + 1)
                            load_tdown(n + 2, q)
                    if not (last and h >= PH - 2):
                        hold(w_ready, QT * (n + 1))
                        load_gates(n + 2, h % 2)
                hold(acc_ready, b + 1)
                hold(acc_copied, b + 2)
                sp.dma_start(at(scr["y"], b), acc_out[:]).then_inc(acc_stored, 16)
                hold(acc_stored, 16 * (b + 1))
                sp.sem_inc(acc_free, 1)

            blocks(sp, one)
            sp.wait_ge(y_added, 2 * TT * NSTEP + 4)
            for t in range(TT):
                sp.dma_start(scr["y"][NB1 + t], y[:, t]).then_inc(y_stored, 16)
            sp.wait_ge(y_stored, 16 * TT)

        @block.gpsimd
        def _(pool):
            def gather(dst, table, idx, h, k, arrived):
                nc.gpsimd.indirect_dma_start(dst, None, table, bass.IndirectOffsetOnAxis(
                    idx[:, h * TOPK + k:h * TOPK + k + 1], 0)).then_inc(arrived, 16)

            def free(used, count):
                pool.wait_ge(used, count)
                pool.sem_inc(pool_waits, 1)

            def down_rows(n, h, ks):
                free(dot_done, 16 * n + ks[-1] + 1)
                for k in ks:
                    gather(down[:, k % RD], io["down"], idx_down, h, k, down_in[k % RD])

            nc.gpsimd.memset(y[:], 0.0).then_inc(y_zero, 1)
            pool.wait_ge(idx_in, 16)
            nc.gpsimd.tensor_copy(idx_down[:], next_idx[:]).then_inc(idx_copied, 1)
            pool.wait_ge(idx_copied, 1)
            pool.sem_inc(idx_taken, 1)
            for c in range(0, TOPK, CHUNK):
                down_rows(0, 0, range(c, c + CHUNK))

            def one(b, last):
                for h in range(PH):
                    n = b * PH + h
                    cols = slice(h * TOPK, (h + 1) * TOPK)
                    nc.gpsimd.tensor_copy(idx_up[:, cols], idx_down[:, cols]).then_inc(idx_copied, 1)
                    free(idx_copied, 1 + 2 * n + 1)
                    for c in range(0, TOPK, CHUNK):
                        ks = range(c, c + CHUNK)
                        if not (last and h == PH - 1):
                            down_rows(n + 1, (h + 1) % PH, ks)
                        free(up_used, 16 * n + ks[-1] + 1)
                        for k in ks:
                            gather(up[:, k % RU], io["up"], idx_up, h, k, up_in[k % RU])
                    if h == 0 and not last:
                        pool.wait_ge(idx_in, 16 * (b + 2))
                    free(dot_done, 16 * (n + 1) + RD)
                    nc.gpsimd.tensor_copy(idx_down[:, cols], next_idx[:, cols]).then_inc(idx_copied, 1)
                    if h == PH - 1:
                        pool.wait_ge(idx_copied, 1 + 2 * n + 2)
                        pool.sem_inc(idx_taken, 1)
                pool.sem_clear(pool_waits)

            blocks(pool, one)

        @block.tensor
        def _(pe):
            pe.sem_inc(y_ready, 2 * TT)

            def down_product(n, q):
                pe.wait_ge(tdown_in[q], 16 * (n + 1))
                pe.wait_ge(gl_ready, QT * n + q + 1)
                for k in range(KD):
                    ins = nc.tensor.matmul(abank[q % 2][:], tdown[:, q, k * P:(k + 1) * P], h2T[:, k],
                                           start=k == 0, stop=k == KD - 1)
                ins.then_inc(a_ready, 1)

            def up_product(n, half_n, par, t):
                if t == 0:
                    pe.wait_ge(w_ready, QT * (n + 1))
                    for q in range(QT):
                        pe.wait_ge(tup_in[par * QT + q], 16 * (half_n + 1))
                for i in range(2):
                    out = ybank[t % 2 * 2 + i]
                    pe.wait_ge(y_added, 2 * TT * n + 2 * t + i + 1)
                    for q in range(QT):
                        ins = nc.tensor.matmul(out[:], w[:, par, q, t * P:(t + 1) * P], tup[:, par, q, i * 512:(i + 1) * 512],
                                               start=q == 0, stop=q == QT - 1)
                    ins.then_inc(y_ready, 1)

            pe.wait_ge(h2T_in, 16)
            for q in range(QT):
                down_product(0, q)

            def one(b, last):
                for h in range(PH):
                    n = b * PH + h
                    for q in range(QT):
                        if not (last and h == PH - 1):
                            down_product(n + 1, q)
                        up_product(n, b * (PH // 2) + h // 2, h % 2, q)

            blocks(pe, one)

        @block.scalar
        def _(act):
            act.sem_inc(gl_ready, 2)
            act.sem_inc(acc_free, 1)
            act.sem_inc(acc_copied, 1)

            def expert_gelu(n, q, first=False):
                act.wait_ge(a_ready, QT * n + q + 1)
                if not (first and q < 2):
                    act.wait_ge(w_ready, QT * n + q - 1)
                nc.scalar.activation(gl[:, q % 2], abank[q % 2][:], ACT.Gelu_apprx_tanh).then_inc(gl_ready, 1)

            def dots_gelu(n):
                act.wait_ge(dot_done, 16 * (n + 1) + RD)
                nc.scalar.activation(gelu[:], dots[:], ACT.Gelu_apprx_tanh).then_inc(gelu_ready, 1)

            for q in range(QT):
                expert_gelu(0, q, True)
            dots_gelu(0)

            def one(b, last):
                for h in range(PH):
                    n = b * PH + h
                    if not (last and h == PH - 1):
                        for q in range(QT):
                            expert_gelu(n + 1, q)
                        dots_gelu(n + 1)
                act.wait_ge(acc_ready, b + 1)
                act.wait_ge(acc_free, b + 1)
                nc.scalar.activation(acc_out[:], acc[:], ACT.Copy).then_inc(acc_copied, 1)

            blocks(act, one)

        @block.vector
        def _(dve):
            dve.sem_inc(dot_done, RD)
            dve.sem_inc(up_used, RU)
            dve.sem_inc(y_added, 4)

            def take_block(b):
                dve.wait_ge(h2_in, 32 * (b + 1))
                nc.vector.tensor_copy(h2[:], next_h2[:]).then_inc(dve_own, 1)
                nc.vector.tensor_copy(gate[:], next_gate[:]).then_inc(dve_own, 1)
                dve.wait_ge(dve_own, 2 * (b + 1))
                dve.sem_inc(h2_taken, 1)

            def dot(n, k):
                dve.wait_ge(down_in[k % RD], 16 * (TOPK // RD * n + k // RD + 1))
                row = down[:, k % RD]
                nc.vector.tensor_tensor_reduce(out=row, in0=row, in1=h2[:], scale=1.0, scalar=0.0, op0=ALU.mult,
                                               op1=ALU.add, accum_out=dots[:, k:k + 1]).then_inc(dot_done, 1)

            def weigh(n, h):
                dve.wait_ge(gelu_ready, n + 1)
                nc.vector.tensor_tensor(wts[:, h % 2], gelu[:], gate[:, h * TOPK:(h + 1) * TOPK], ALU.mult).then_inc(wts_ready, 1)

            def add_row(n, b, h, k):
                dve.wait_ge(up_in[k % RU], 16 * (TOPK // RU * n + k // RU + 1))
                wt = wts[:, h % 2, k:k + 1]
                if k == 0:
                    dve.wait_ge(wts_ready, n + 1)
                if h == 0 and k == 0:
                    dve.wait_ge(acc_copied, b + 1)
                    nc.vector.tensor_scalar(acc[:], up[:, k % RU], wt, None, ALU.mult).then_inc(up_used, 1)
                else:
                    dve.wait_ge(up_used, 16 * n + k + RU)
                    nc.vector.scalar_tensor_tensor(out=acc[:], in0=up[:, k % RU], scalar=wt, in1=acc[:],
                                                   op0=ALU.mult, op1=ALU.add).then_inc(up_used, 1)

            def expert_weights(n, half_n, par, q, first=False):
                if q == 0:
                    dve.wait_ge(gates_in[par], 16 * (half_n + 1))
                    if not first:
                        dve.wait_ge(y_ready, 2 * TT * n)
                dve.wait_ge(gl_ready, QT * n + q + 3)
                nc.vector.tensor_tensor(w[:, par, q].rearrange("p (c t) -> p c t", t=TC), gl[:, q % 2]
                                        .rearrange("p (c t) -> p c t", t=TC), gates[:, par, :, q], ALU.mult).then_inc(w_ready, 1)

            def add_y(n, t):
                for i in range(2):
                    dve.wait_ge(y_ready, 2 * TT * (n + 1) + 2 * t + i + 1)
                    part = y[:, t, i * 512:(i + 1) * 512]
                    nc.vector.tensor_tensor(part, part, ybank[t % 2 * 2 + i][:], ALU.add).then_inc(y_added, 1)

            take_block(0)
            for q in range(QT):
                for k in range(4 * q, 4 * q + 4):
                    dot(0, k)
                expert_weights(0, 0, 0, q, True)
            weigh(0, 0)
            dve.wait_ge(y_zero, 1)

            def one(b, last):
                for h in range(PH):
                    n = b * PH + h
                    more = not (last and h == PH - 1)
                    if h == PH - 1 and more:
                        dve.wait_ge(dot_done, 16 * (n + 1) + RD)
                        dve.wait_ge(wts_ready, n + 1)
                        take_block(b + 1)
                    for q in range(QT):
                        for k in range(4 * q, 4 * q + 4):
                            if more:
                                dot(n + 1, k)
                            add_row(n, b, h, k)
                        if more:
                            expert_weights(n + 1, b * (PH // 2) + (h + 1) // 2, (h + 1) % 2, q)
                        add_y(n, q)
                    if h == PH - 1:
                        dve.wait_ge(up_used, 16 * (n + 1) + RU)
                        dve.sem_inc(acc_ready, 1)
                    if more:
                        weigh(n + 1, (h + 1) % PH)

            blocks(dve, one)


def last_norm(nc, io, scr):
    RB = 4
    with ExitStack() as ctx:
        def sb(name, shape, dt=F32):
            return ctx.enter_context(nc.sbuf_tensor(name, shape, dt))

        def sem(name):
            return ctx.enter_context(nc.semaphore(name))

        gfin = sb("gfin", [P, D])
        x, yv, sq = sb("l_x", [P, NBLK, D]), sb("l_y", [P, RB, D]), sb("l_sq", [P, D])
        stat = sb("l_stat", [P, 5, NBLK])
        ssq, var, std, rinv, tmp = (stat[:, i] for i in range(5))
        gfin_in, xy_in = sem("gfin_in"), [sem(f"xy_in{i}") for i in range(NBLK)]
        x3_ready, ssq_ready, var_ready, std_ready = sem("x3_ready"), sem("l_ssq"), sem("l_var"), sem("l_std")
        out_ready, out_done, own = sem("out_ready"), sem("out_done"), sem("l_own")
        block = ctx.enter_context(nc.Block())

        @block.sync
        def _(sp):
            sp.dma_start(gfin[:], io["gfin"]).then_inc(gfin_in, 16)
            for b in range(NBLK):
                sp.dma_start(x[:, b], scr["x2"][b]).then_inc(xy_in[b], 16)
                if b >= RB:
                    sp.wait_ge(x3_ready, b - RB + 1)
                sp.dma_start(yv[:, b % RB], scr["y"][b]).then_inc(xy_in[b], 16)
            for b in range(NBLK):
                sp.wait_ge(out_ready, b + 1)
                sp.dma_start(io["out"][b], x[:, b]).then_inc(out_done, 16)
            sp.wait_ge(out_done, 16 * NBLK)

        @block.scalar
        def _(act):
            for b in range(NBLK):
                act.wait_ge(x3_ready, b + 1)
                if b:
                    act.wait_ge(ssq_ready, b)
                nc.scalar.activation(sq[:], x[:, b], ACT.Square, accum_out=ssq[:, b:b + 1]).then_inc(ssq_ready, 1)
            act.wait_ge(var_ready, 1)
            nc.scalar.activation(std, var, ACT.Sqrt).then_inc(std_ready, 1)

        @block.vector
        def _(dve):
            n = [0]

            def link(ins):
                n[0] += 1
                ins.then_inc(own, 1)
                dve.wait_ge(own, n[0])

            for b in range(NBLK):
                dve.wait_ge(xy_in[b], 32)
                nc.vector.tensor_tensor(x[:, b], x[:, b], yv[:, b % RB], ALU.add).then_inc(x3_ready, 1)
            dve.wait_ge(ssq_ready, NBLK)
            nc.vector.tensor_scalar(var, ssq, 1.0 / D, EPS, ALU.mult, ALU.add).then_inc(var_ready, 1)
            dve.wait_ge(std_ready, 1)
            link(nc.vector.reciprocal(rinv, std))
            link(nc.vector.tensor_tensor(tmp, rinv, rinv, ALU.mult))
            link(nc.vector.tensor_tensor(tmp, tmp, var, ALU.mult))
            link(nc.vector.tensor_scalar(tmp, tmp, -0.5, 1.5, ALU.mult, ALU.add))
            link(nc.vector.tensor_tensor(rinv, rinv, tmp, ALU.mult))
            dve.wait_ge(gfin_in, 16)
            for b in range(NBLK):
                nc.vector.scalar_tensor_tensor(out=x[:, b], in0=x[:, b], scalar=rinv[:, b:b + 1], in1=gfin[:],
                                               op0=ALU.mult, op1=ALU.mult).then_inc(out_ready, 1)


def build(nc, io):
    scr = {n: nc.dram_tensor(f"all_{n}", shape, dt, kind="Internal").ap() for n, shape, dt in (
        ("x2", (NBLK, P, D), F32), ("h2", (NBLK, P, D), F32), ("h2T", (NG, P, KD * TG), F32), ("y", (NBLK, P, D), F32),
        ("eidx", (NBLK, P, NSEL), I32), ("sel1", (NBLK, P, NSEL), F32), ("sel2", (NBLK, P, NSEL), F32),
        ("gate", (NBLK, P, NSEL), F32), ("table", (NQ, P, NTC, QT * TC), F32))}
    mixer(nc, io, scr)
    if STAGES > 1:
        gate_table(nc, io, scr)
        experts(nc, io, scr)
        last_norm(nc, io, scr)


def slots_of(w_in, w_branch_pool, w_branch_attn, w_out, w_peer_q):
    def columns(w):
        k, n = w.shape[0] // P, w.shape[1] // P
        return w.reshape(k, P, n, P).transpose(2, 1, 0, 3).reshape(n, P, k * P)

    pool, q, k, v, gp, ga = np.split(w_in, np.cumsum([POOL_W, NH * HD, P, P, D]), axis=1)
    q = q.reshape(D, 2, 4, HD).transpose(0, 2, 1, 3).reshape(D, NH * HD)
    branches = np.concatenate([columns(w_branch_pool), columns(w_branch_attn)], axis=2)
    merge = np.stack([columns(gp), columns(ga), branches], axis=1).reshape(3 * KD, P, D)
    return np.concatenate([columns(pool), columns(k), columns(v), columns(q), merge,
                           w_out.reshape(KD, P, D), columns(w_peer_q)])


def constants():
    c = np.zeros((P, NCONST), np.float32)
    c[:, C_IDENT:C_IDENT + P] = np.eye(P)
    rot, half = HD // 4, HD // 8
    for base in (0, HD):
        for d in range(rot):
            c[base + (d + half) % rot, C_PERM + base + d] = 1
    c[0, C_ROWS:C_ROWS + CH] = 1
    c[1, C_ROWS + CH:C_ROWS + P] = 1
    mask = c[:, C_MASK:C_MASK + 4 * WK].reshape(P, 4, WK)
    mask[0, :, P:] = -1e30
    mask[1, :, 0:CH] = -1e30
    mask[0, 0:2, 0:CH] = -1e30
    c[:, C_IOTA:C_IOTA + P] = np.arange(P)

    pos = np.arange(T, dtype=np.float32)
    inv = np.float32(500000.0) ** (-np.arange(0, rot, 2, dtype=np.float32) / np.float32(rot))
    ang = pos[:, None] * inv[None, :]
    table = np.zeros((2, P, T), np.float32)
    table[0] = 1
    for base in (0, HD):
        table[0, base:base + rot] = np.tile(np.cos(ang).T, (2, 1))
        table[1, base:base + rot] = np.tile(np.sin(ang).T, (2, 1))
        table[1, base:base + half] *= -1
    r = np.ones((NG, P, NROPE), np.float32)
    r[:, :, R_COS:R_CNT] = table.reshape(2, P, NG, TG).transpose(2, 1, 0, 3).reshape(NG, P, 2 * TG)
    for j in range(NPOOL):
        w = 2 << j
        r[0, :, R_CNT + j * PAD:R_CNT + (j + 1) * PAD] = w / np.minimum(np.arange(PAD) + 1, w)
    return c, r


def arrays_of(x, g_mix, w_in, w_pool_grp, pool_scale, attn_sinks, w_branch_pool, w_branch_attn, w_out, g_ffn,
              w_peer_q, peer_keys_1, peer_keys_2, expert_down, expert_up, g_final):
    c, r = constants()
    vecs = np.concatenate([g_mix[0].reshape(KD, P).T, g_ffn[0].reshape(KD, P).T, pool_scale[0].reshape(NPOOL, P).T,
                           np.broadcast_to(attn_sinks[0], (P, NH))], axis=1)
    return {
        "x": x.reshape(NG, TT, P, D), "const": c, "rope": r, "vecs": vecs,
        "slots": slots_of(w_in[0], w_branch_pool[0], w_branch_attn[0], w_out[0], w_peer_q[0]),
        "keys": np.stack([peer_keys_1[0].T, peer_keys_2[0].T], axis=1),
        "wgrp": w_pool_grp[0].transpose(1, 0, 2),
        "gffn": np.broadcast_to(g_ffn[0], (P, D)), "gfin": np.broadcast_to(g_final, (P, D)),
        "down": expert_down[0], "up": expert_up[0],
        "downT": expert_down[0].reshape(NK, NK, KD, P).transpose(0, 3, 2, 1).reshape(NK, P, D),
    }


def kernel(**inputs):
    import concourse.bacc as bacc
    from concourse.bass_utils import run_bass_kernel_spmd

    nc = bacc.Bacc("TRN2", target_bir_lowering=False, num_devices=1)
    arrays = {n: np.ascontiguousarray(a) for n, a in arrays_of(**{k: np.asarray(a) for k, a in inputs.items()}).items()}
    io = {n: nc.dram_tensor(f"in_{n}", a.shape, F32, kind="ExternalInput").ap() for n, a in arrays.items()}
    io["out"] = nc.dram_tensor("out", (NBLK, P, D), F32, kind="ExternalOutput").ap()
    build(nc, io)
    r = run_bass_kernel_spmd(nc, [{f"in_{n}": a for n, a in arrays.items()}], core_ids=[0])
    return r.results[0]["out"].reshape(1, T, D)
```

```python
from contextlib import ExitStack

import concourse.bass as bass
from concourse import mybir
import numpy as np

P = 128
D = 1024
KD = D // P
T = 1024
TG = 512
NG = T // TG
TT = TG // P
NBLK = T // P
POOL_W = 512
NPOOL = 4
PAD = 16
NH = 8
HD = 64
CH = 64
WK = CH + P
PH = 8
NK = 128
TOPK = 16
NSEL = PH * TOPK
EPS = 1e-6
HALF_ROW = TOPK // 2
NCAND = TOPK + (HALF_ROW - 1) * HALF_ROW + HALF_ROW
NEG_BIG = -3.4028234e38
NBANK = 8
RING = 8
NMIX = 2
DOTS_HEAD = 9
DOTS_TILE = 6
DOTS_MERGE = 10
DOTS_XO = 28
DOTS_NORM = 16
HOIST = 6

F32 = mybir.dt.float32
F32R = mybir.dt.float32r
U32 = mybir.dt.uint32
I32 = mybir.dt.int32
ALU = mybir.AluOpType
ACT = mybir.ActivationFunctionType
AX = mybir.AxisListType

SLOT_P, SLOT_K, SLOT_V, SLOT_Q = 0, 4, 5, 6
SLOT_MERGE = 10
SLOT_OUT = SLOT_MERGE + 3 * KD
SLOT_PQ = SLOT_OUT + KD
NSLOT = SLOT_PQ + 2 * PH

C_IDENT = 0
C_PERM = C_IDENT + P
C_ROWS = C_PERM + P
C_MASK = C_ROWS + P
C_IOTA = C_MASK + 4 * WK
NCONST = C_IOTA + P
V_GMIX, V_GFFN, V_PSCALE = 0, KD, 2 * KD
V_SINK = V_PSCALE + NPOOL
NVEC = V_SINK + NH
R_COS, R_SIN, R_CNT = 0, TG, 2 * TG
NROPE = R_CNT + NPOOL * PAD


EARLY = [("gp", 0), ("ga", 0), ("gp", 1), ("ga", 1)]


def mixer_jobs():
    jobs = [("xT", k) for k in range(KD)]
    jobs += [("p", j) for j in range(NPOOL)] + [("k",), ("v",), ("rot", 0)]
    for j in range(4):
        jobs += [("q", j)]
        if j:
            jobs += [("rot", j)]
    jobs += [("grp", 0), ("rot", 4)] + [("grp", j) for j in range(1, NPOOL)]
    jobs += [("sc", 0, i) for i in range(4)]
    for t in range(TT):
        jobs += [("pT", t, i) for i in range(4)]
        if t + 1 < TT:
            jobs += [("sc", t + 1, i) for i in range(4)]
        jobs += [EARLY[t]]
        jobs += [("pv", t), ("yaT", t)]
    for m in range(KD):
        jobs += [j for j in (("gp", m), ("ga", m)) if j not in EARLY] + [("bp", m), ("ba", m)]
    jobs += [("xo", t, n) for t in range(TT) for n in range(2)]
    jobs += [("xT2", k) for k in range(KD)]
    jobs += [("pq", 0, 0), ("pq", 0, 1)]
    for h in range(PH):
        for i in range(2):
            if h + 1 < PH:
                jobs += [("pq", h + 1, i)]
            jobs += [("ss", h, i)]
    return {job: n for n, job in enumerate(jobs)}


JOBS = mixer_jobs()
NJ = len(JOBS)
NJ += -NJ % NBANK
SLOT_READER = ([("p", j) for j in range(NPOOL)] + [("k",), ("v",)] + [("q", j) for j in range(4)]
               + [(n, m) for m in range(KD) for n in ("gp", "ga", "ba")]
               + [("xo", TT - 1, 1)] * KD + [("pq", h, i) for h in range(PH) for i in range(2)])


def mixer(nc, io, scr):
    with ExitStack() as ctx:
        def sb(name, shape, dt=F32):
            return ctx.enter_context(nc.sbuf_tensor(name, shape, dt))

        def sem(name):
            return ctx.enter_context(nc.semaphore(name))

        banks = [ctx.enter_context(nc.psum_tensor(f"bank{i}", [P, 512], F32)) for i in range(NBANK)]

        const = sb("const", [P, NCONST])
        vecs = sb("vecs", [P, NVEC])
        keys = sb("keys", [P, 2, NK])
        wgrp = sb("wgrp", [P, NPOOL, P])
        gffn = sb("gffn", [P, D])
        rope = sb("rope", [P, NROPE])
        ring = sb("ring", [P, RING, D])
        x = sb("x", [P, TT, D])
        h = sb("h", [P, TT, D])
        hT = sb("hT", [P, KD, TG])
        pT = sb("pT", [P, NPOOL, PAD + TG])
        sums = sb("sums", [P, 2, PAD + TG])
        pooled = sb("pooled", [P, NPOOL, TG])
        ypT = sb("ypT", [P, NPOOL, TG])
        raw = sb("raw", [P, 2, TG])
        rot = sb("rot", [P, 2, TG])
        qz = sb("qz", [P, NH, TG])
        kT = sb("kT", [P, CH + TG])
        v = sb("v", [P, 1 + TT, P])
        pr = sb("pr", [P, NH, 2 * P])
        prT = sb("prT", [P, 2 * NH, P])
        ya = sb("ya", [P, NH * HD])
        yaT = sb("yaT", [P, 4, TG])
        sg = sb("sg", [P, 2, 2, TG])
        smask = sb("smask", [P, 4, NK])
        small = sb("small", [P, 88])
        vtop = sb("vtop", [P, 2, 2, TOPK])
        itop = sb("itop", [P, 2, TT, TOPK], U32)
        itopf = sb("itopf", [P, 2, TT, TOPK])
        cand = sb("cand", [P, 2, NCAND])
        cmask = sb("cmask", [P, 2, NCAND])
        ctop = sb("ctop", [P, TT, TOPK], U32)
        cij = sb("cij", [P, 2, TT, TOPK], U32)
        cijf = sb("cijf", [P, 2, TT, TOPK])
        place = sb("place", [P, 2, TT, TOPK])
        sel = sb("sel", [P, 2, TT, NSEL])
        vals = sb("vals", [P, 2, TT, TOPK])
        gsm = sb("gsm", [P, 2, TT])
        eidx = sb("eidx", [P, TT, NSEL], I32)
        gate = sb("gate", [P, TT, NSEL])
        dots = sb("m_dots", [P, NMIX, NSEL])
        idx = sb("m_idx", [P, NMIX, NSEL], I32)

        mT = h[:].rearrange("p t d -> p (t d)").rearrange("p (k n) -> p k n", k=KD)
        qd = ypT
        s12 = pooled[:].rearrange("p a n -> p (a n)").rearrange("p (h i t c) -> p h i t c", h=2, i=2, t=TT)
        hits = [a[:].rearrange("p a n -> p (a n)")[:, 0:TT * TOPK * TOPK].rearrange("p (n j) -> p n j", j=TOPK)
                for a in (sums, rot)]
        ident = const[:, C_IDENT:C_IDENT + P]
        rows_of = [x, qz[:].rearrange("p a n -> p (a n)").rearrange("p (t d) -> p t d", d=D)]
        h2_of = [gffn[:], rope[:, 0:D]]
        ssq, var, std, rinv, tmp = (small[:, 4 * i:4 * i + 4] for i in range(5))
        mx, negm, sarg, den = (small[:, 24 + 8 * i:32 + 8 * i] for i in range(4))
        es, rs = ([small[:, 56 + 16 * i + 8 * j:64 + 16 * i + 8 * j] for j in range(2)] for i in range(2))

        consts_in = sem("consts_in")
        x_in = [sem(f"x_in{t}") for t in range(TT)]
        rope_in = sem("rope_in")
        slot_in = [sem(f"slot_in{i}") for i in range(RING)]
        job_full = sem("job_full")
        ssq_ready = sem("ssq_ready")
        var_ready = sem("var_ready")
        std_ready = sem("std_ready")
        rinv_ready = sem("rinv_ready")
        h_ready = sem("h_ready")
        hT_ready = sem("hT_ready")
        p_ready = sem("p_ready")
        raw_ready = sem("raw_ready")
        roped = sem("roped")
        v_ready = sem("v_ready")
        pooled_ready = sem("pooled_ready")
        yp_ready = sem("yp_ready")
        m_ready = sem("m_ready")
        exp_ready = sem("exp_ready")
        prT_ready = sem("prT_ready")
        ya_ready = sem("ya_ready")
        yaT_ready = sem("yaT_ready")
        early_kept = sem("early_kept")
        sig_ready = sem("sig_ready")
        merged = sem("merged")
        x2_ready = sem("x2_ready")
        x2_out = sem("x2_out")
        h2_ready = sem("h2_ready")
        h2_out = sem("h2_out")
        h2T_out = sem("h2T_out")
        qd_ready = sem("qd_ready")
        ss_ready = sem("ss_ready")
        garg_ready = sem("garg_ready")
        gexp_ready = sem("gexp_ready")
        topk_done = sem("topk_done")
        hit_ready = sem("hit_ready")
        chosen = sem("chosen")
        choice_out = sem("choice_out")
        zeroed = sem("zeroed")
        h2_in = [sem(f"m_h2_in{i}") for i in range(NMIX)]
        idx_copied = sem("m_idx_copied")
        down_in = [sem(f"m_down_in{i}") for i in range(TT)]
        dot_done = sem("m_dot_done")
        gffn_in = sem("gffn_in")
        act_ready = sem("m_act_ready")
        act_out = sem("m_act_out")
        carried = sem("carried")
        dve_own = sem("dve_own")
        pool_own = sem("pool_own")

        def rows_by_head(hd):
            first = NSEL + TT + DOTS_XO + DOTS_NORM
            return min(NMIX * NSEL, first + DOTS_HEAD * (hd + 1))

        frees = {}
        for k in range(KD):
            frees["xT", k] = (hT_ready, k + 1, 2 * KD)
            frees["xT2", k] = (hT_ready, KD + k + 1, 2 * KD)
        for j in range(NPOOL):
            frees["p", j] = (p_ready, j + 1, NPOOL)
            frees["grp", j] = (yp_ready, j + 1, NPOOL)
            frees["q", j] = (raw_ready, j + 2, 5)
        frees["k",] = (raw_ready, 1, 5)
        frees["v",] = (v_ready, 1, 1)
        for i in range(5):
            frees["rot", i] = (roped, i + 1, 5)
        for t in range(TT):
            for i in range(4):
                frees["sc", t, i] = (exp_ready, 9 * t + 2 * i + 2, 9 * TT)
                frees["pT", t, i] = (prT_ready, 4 * t + i + 1, 4 * TT)
            frees["pv", t] = (ya_ready, t + 1, TT)
            frees["yaT", t] = (yaT_ready, t + 1, TT)
            for n in range(2):
                frees["xo", t, n] = (x2_ready, 2 * t + n + 1, 2 * TT)
        for m in range(KD):
            for i, name in enumerate(("gp", "ga")):
                frees[name, m] = (sig_ready, 2 * m + 1 + i, 2 * KD) if m > 1 else (early_kept, 2 * m + 1 + i, TT)
            frees["bp", m] = frees["ba", m] = (merged, m + 1, KD)
        for hd in range(PH):
            for i in range(2):
                frees["pq", hd, i] = (qd_ready, 2 * hd + i + 1, 2 * PH)
                frees["ss", hd, i] = (ss_ready, 2 * hd + i + 1, 2 * PH)
        by_number = {n: job for job, n in JOBS.items()}

        def bank(*job):
            return banks[JOBS[job] % NBANK]

        def wait_job(eng, g, *job):
            eng.wait_ge(job_full, (g + 1) * NJ + JOBS[job] + 1)

        block = ctx.enter_context(nc.Block())

        @block.sync
        def _(sp):
            def load_x(g):
                for t in range(TT):
                    sp.dma_start(x[:, t], io["x"][g, t]).then_inc(x_in[t], 16)

            load_x(0)
            for dst, src in ((const, io["const"]), (vecs, io["vecs"]), (keys, io["keys"]),
                             (wgrp, io["wgrp"]), (gffn, io["gffn"])):
                sp.dma_start(dst[:], src).then_inc(consts_in, 16)

            def load_group(g):
                if g:
                    load_x(g)
                sp.dma_start(rope[:], io["rope"][g]).then_inc(rope_in, 16)

            for g in range(NG):
                if g == 0:
                    load_group(0)
                for s in range(NSLOT):
                    before = [r for r in range(s % RING, NSLOT, RING) if r < s] or [
                        r - NSLOT for r in range(s % RING, NSLOT, RING)]
                    r = before[-1]
                    if g or r >= 0:
                        sp.wait_ge(job_full, (g + (1 if r >= 0 else 0)) * NJ + JOBS[SLOT_READER[r % NSLOT]] + 1)
                    sp.dma_start(ring[:, s % RING], io["slots"][s]).then_inc(slot_in[s % RING], 16)
                    if g and s == SLOT_OUT + KD - 1:
                        sp.wait_ge(dot_done, NSEL)
                        load_x(g)
                        sp.dma_start(gffn[:], io["gffn"]).then_inc(gffn_in, 16)
                    if g and s == SLOT_MERGE:
                        sp.wait_ge(pooled_ready, (g + 1) * NPOOL)
                        sp.wait_ge(roped, (g + 1) * 5)
                        sp.dma_start(h2_of[1], scr["h2"][1]).then_inc(h2_in[1], 16)
                    if s == SLOT_PQ + 5:
                        for t in range(TT):
                            sp.wait_ge(x2_ready, g * 2 * TT + 2 * t + 2)
                            sp.dma_start(scr["x2"][g * TT + t],
                                         x[:, t]).then_inc(x2_out, 16)
                    if s == SLOT_PQ + 9:
                        for t in range(TT):
                            sp.wait_ge(h2_ready, g * TT + t + 1)
                            sp.dma_start(scr["h2"][g * TT + t], x[:, t]).then_inc(h2_out, 16)
                        sp.wait_ge(hT_ready, g * 2 * KD + 2 * KD)
                        sp.dma_start(scr["h2T"][g], hT[:].rearrange("p k n -> p (k n)")).then_inc(h2T_out, 16)
                    if s == SLOT_PQ + 11 and g + 1 < NG:
                        sp.wait_ge(h2_out, 16 * (g + 1) * TT)
                        sp.wait_ge(pooled_ready, (g + 1) * NPOOL)
                        sp.wait_ge(roped, (g + 1) * 5)
                        load_group(g + 1)
                        sp.dma_start(h2_of[0], scr["h2"][0]).then_inc(h2_in[0], 16)
            for b in range(NMIX):
                sp.wait_ge(act_ready, b + 1)
                sp.dma_start(scr["act"][b], dots[:, b]).then_inc(act_out, 16)
            sp.wait_ge(act_out, 16 * NMIX)
            sp.wait_ge(x2_out, 16 * NBLK)
            sp.wait_ge(h2_out, 16 * NBLK)
            sp.wait_ge(choice_out, 64 * NG - 16)
            sp.wait_ge(h2T_out, 16 * NG)

        def slot_uses(q):
            return len(range(q, NSLOT, RING))

        @block.tensor
        def _(pe):
            pe.sem_inc(job_full, NJ)
            pe.wait_ge(consts_in, 16 * 5)
            for g in range(NG):
                def begin(*job):
                    n = JOBS[job]
                    if n >= NBANK:
                        s, c, per = frees[by_number[n - NBANK]]
                        pe.wait_ge(s, g * per + c)
                    return banks[n % NBANK]

                def weights(s):
                    pe.wait_ge(slot_in[s % RING], 16 * (g * slot_uses(s % RING) + s // RING + 1))
                    return ring[:, s % RING]

                def product(out, w, act, ks):
                    for i, k in enumerate(ks):
                        ins = nc.tensor.matmul(out[:], w[:, k * P:(k + 1) * P], act[:, i],
                                               start=i == 0, stop=i == len(ks) - 1)
                    ins.then_inc(job_full, 1)

                def project(job, s, act=hT, ks=range(KD)):
                    out = begin(*job)
                    w = weights(s)
                    product(out, w, act, ks)

                def turn(job, src):
                    out = begin(*job)
                    for i, a in enumerate(src):
                        ins = nc.tensor.transpose(out[:, i * P:(i + 1) * P], a, ident)
                    ins.then_inc(job_full, 1)

                pe.wait_ge(h_ready, g * 2 * TT + TT)
                for k in range(KD):
                    turn(("xT", k), [h[:, t, k * P:(k + 1) * P] for t in range(TT)])
                pe.wait_ge(hT_ready, g * 2 * KD + KD)
                for j in range(NPOOL):
                    project(("p", j), SLOT_P + j)
                project(("k",), SLOT_K)
                out = begin("v")
                w = weights(SLOT_V)
                for t in range(TT):
                    for k in range(KD):
                        ins = nc.tensor.matmul(out[:, t * P:(t + 1) * P], hT[:, k, t * P:(t + 1) * P],
                                               w[:, k * P:(k + 1) * P], start=k == 0, stop=k == KD - 1)
                ins.then_inc(job_full, 1)

                def partner(i):
                    out = begin("rot", i)
                    pe.wait_ge(raw_ready, g * 5 + i + 1)
                    nc.tensor.matmul(out[:], const[:, C_PERM:C_PERM + P], raw[:, i % 2],
                                     start=True, stop=True).then_inc(job_full, 1)

                def group(j):
                    out = begin("grp", j)
                    pe.wait_ge(pooled_ready, g * NPOOL + j + 1)
                    nc.tensor.matmul(out[:], wgrp[:, j], pooled[:, j], start=True, stop=True).then_inc(job_full, 1)

                partner(0)
                for j in range(4):
                    project(("q", j), SLOT_Q + j)
                    if j:
                        partner(j)
                group(0)
                partner(4)
                for j in range(1, NPOOL):
                    group(j)

                def scores(t):
                    if t == 0:
                        pe.wait_ge(roped, g * 5 + 5)
                        if g:
                            pe.wait_ge(carried, 3 * g)
                        else:
                            pe.wait_ge(zeroed, 1)
                    mask = const[:, C_MASK:C_MASK + 2 * WK] if t == 0 and g == 0 else const[:, C_MASK + 2 * WK:C_MASK + 4 * WK]
                    for i in range(4):
                        out = begin("sc", t, i)
                        nc.tensor.matmul(out[:, 0:2 * WK], const[:, C_ROWS:C_ROWS + P], mask, start=True, stop=False)
                        for e in range(2):
                            ins = nc.tensor.matmul(out[:, e * WK:(e + 1) * WK], qz[:, 2 * i + e, t * P:(t + 1) * P],
                                                   kT[:, t * P:t * P + WK], start=False, stop=e == 1)
                        ins.then_inc(job_full, 1)

                scores(0)
                for t in range(TT):
                    for i in range(4):
                        pe.wait_ge(exp_ready, g * 9 * TT + 9 * t + 2 * i + 2)
                        turn(("pT", t, i), [pr[:, 2 * i + e // 2, (e % 2) * P:(e % 2 + 1) * P] for e in range(4)])
                    if t + 1 < TT:
                        scores(t + 1)
                    project(EARLY[t], SLOT_MERGE + 3 * (t // 2) + t % 2)
                    out = begin("pv", t)
                    pe.wait_ge(prT_ready, g * 4 * TT + 4 * t + 4)
                    if t == 0:
                        pe.wait_ge(v_ready, g + 1)
                    for hd in range(NH):
                        kv = slice(hd // 4 * HD, (hd // 4 + 1) * HD)
                        nc.tensor.matmul(out[:, hd * HD:(hd + 1) * HD], prT[:, 2 * hd], v[:, t, kv], start=True, stop=False)
                        ins = nc.tensor.matmul(out[:, hd * HD:(hd + 1) * HD], prT[:, 2 * hd + 1], v[:, t + 1, kv],
                                               start=False, stop=True)
                    ins.then_inc(job_full, 1)
                    pe.wait_ge(ya_ready, g * TT + t + 1)
                    turn(("yaT", t), [ya[:, j * P:(j + 1) * P] for j in range(4)])

                for m in range(KD):
                    s = SLOT_MERGE + 3 * m
                    if m > 1:
                        project(("gp", m), s)
                        project(("ga", m), s + 1)
                    w = weights(s + 2)
                    if m == 0:
                        pe.wait_ge(yp_ready, g * NPOOL + NPOOL)
                        pe.wait_ge(yaT_ready, g * TT + TT)
                    product(begin("bp", m), w, ypT, range(4))
                    product(begin("ba", m), w, yaT, range(4, 8))

                wo = [weights(SLOT_OUT + k) for k in range(KD)]
                pe.wait_ge(merged, g * KD + KD)
                for t in range(TT):
                    for n in range(2):
                        out = begin("xo", t, n)
                        for k in range(KD):
                            ins = nc.tensor.matmul(out[:], mT[:, k, t * P:(t + 1) * P], wo[k][:, n * 512:(n + 1) * 512],
                                                   start=k == 0, stop=k == KD - 1)
                        ins.then_inc(job_full, 1)

                pe.wait_ge(h_ready, g * 2 * TT + 2 * TT)
                for k in range(KD):
                    turn(("xT2", k), [h[:, t, k * P:(k + 1) * P] for t in range(TT)])
                pe.wait_ge(hT_ready, g * 2 * KD + 2 * KD)
                project(("pq", 0, 0), SLOT_PQ)
                project(("pq", 0, 1), SLOT_PQ + 1)
                for hd in range(PH):
                    for i in range(2):
                        if hd + 1 < PH:
                            project(("pq", hd + 1, i), SLOT_PQ + 2 * hd + 2 + i)
                        out = begin("ss", hd, i)
                        pe.wait_ge(qd_ready, g * 2 * PH + 2 * hd + i + 1)
                        for t in range(TT):
                            ins = nc.tensor.matmul(out[:, t * P:(t + 1) * P], qd[:, (2 * hd + i) % 4, t * P:(t + 1) * P],
                                                   keys[:, i], start=True, stop=True)
                        ins.then_inc(job_full, 1)
                pe.wait_ge(ss_ready, g * 2 * PH + 2 * PH)
                pe.wait_ge(qd_ready, g * 2 * PH + 2 * PH)
                pe.sem_inc(job_full, NJ - len(JOBS))

        @block.scalar
        def _(act):

            def norm(g, n):
                if n == 1:
                    act.wait_ge(x2_ready, g * 2 * TT + 2 * TT)
                else:
                    if g:
                        act.wait_ge(h2_ready, g * TT)
                for t in range(TT):
                    if n == 0:
                        act.wait_ge(x_in[t], 16 * (g + 1))
                    ins = nc.scalar.activation(h[:, t], x[:, t], ACT.Square, accum_out=ssq[:, t:t + 1])
                ins.then_inc(ssq_ready, 1)
                act.wait_ge(var_ready, 2 * g + n + 1)
                nc.scalar.activation(std, var, ACT.Sqrt).then_inc(std_ready, 1)
                act.wait_ge(rinv_ready, 2 * g + n + 1)
                for t in range(TT):
                    nc.scalar.activation(h[:, t], x[:, t], ACT.Copy, scale=rinv[:, t:t + 1]).then_inc(h_ready, 1)

            def norm_turned(g, n):
                if g + n == 0:
                    act.wait_ge(consts_in, 16 * 5)
                for k in range(KD):
                    job = ("xT2" if n else "xT", k)
                    wait_job(act, g, *job)
                    if g and n == 0:
                        wait_job(act, g - 1, "pq", PH - 1, 1)
                        act.wait_ge(h2T_out, 16 * g)
                    gain = vecs[:, (V_GFFN if n else V_GMIX) + k:(V_GFFN if n else V_GMIX) + k + 1]
                    nc.scalar.activation(hT[:, k], bank(*job)[:], ACT.Copy, scale=gain).then_inc(hT_ready, 1)

            for g in range(NG):
                if g == 0:
                    norm(0, 0)
                    norm_turned(0, 0)
                    act.wait_ge(zeroed, 1)
                else:
                    act.wait_ge(carried, 3 * g)
                for j in range(NPOOL):
                    wait_job(act, g, "p", j)
                    nc.scalar.activation(pT[:, j, PAD:], bank("p", j)[:], ACT.Copy).then_inc(p_ready, 1)

                def keep_raw(i, *job):
                    wait_job(act, g, *job)
                    if i >= 2:
                        act.wait_ge(roped, g * 5 + i - 1)
                    nc.scalar.activation(raw[:, i % 2], bank(*job)[:], ACT.Copy).then_inc(raw_ready, 1)

                keep_raw(0, "k")
                wait_job(act, g, "v")
                nc.scalar.activation(v[:, 1:1 + TT].rearrange("p t c -> p (t c)"), bank("v")[:], ACT.Copy).then_inc(v_ready, 1)
                for j in range(4):
                    keep_raw(1 + j, "q", j)
                for j in range(NPOOL):
                    wait_job(act, g, "grp", j)
                    nc.scalar.activation(ypT[:, j], bank("grp", j)[:], ACT.Copy,
                                         scale=vecs[:, V_PSCALE + j:V_PSCALE + j + 1]).then_inc(yp_ready, 1)

                def expon(t):
                    act.wait_ge(m_ready, g * TT + t + 1)
                    if t:
                        wait_job(act, g, "pT", t - 1, 3)
                    if t > 1:
                        act.wait_ge(ya_ready, g * TT + t - 1)
                    for hd in range(NH):
                        src = bank("sc", t, hd // 2)[:, hd % 2 * WK:(hd % 2 + 1) * WK]
                        nc.scalar.activation(pr[:, hd, CH:], src, ACT.Exp, bias=negm[:, hd:hd + 1], scale=HD ** -0.5,
                                             accum_out=rs[t % 2][:, hd:hd + 1]).then_inc(exp_ready, 1)
                    nc.scalar.activation(es[t % 2], sarg, ACT.Exp).then_inc(exp_ready, 1)

                expon(0)
                for t in range(TT):
                    if t + 1 < TT:
                        expon(t + 1)
                    if g and t == 0:
                        act.wait_ge(merged, g * KD)
                    wait_job(act, g, *EARLY[t])
                    nc.scalar.activation(sg[:, t // 2, t % 2], bank(*EARLY[t])[:], ACT.Copy).then_inc(early_kept, 1)
                    wait_job(act, g, "yaT", t)
                    nc.scalar.activation(yaT[:, :, t * P:(t + 1) * P],
                                         bank("yaT", t)[:].rearrange("p (j c) -> p j c", j=4), ACT.Copy).then_inc(yaT_ready, 1)

                for m in range(KD):
                    if m >= 2:
                        act.wait_ge(merged, g * KD + m - 1)
                    else:
                        act.wait_ge(early_kept, g * TT + 2 * m + 2)
                    for i, n in enumerate(("gp", "ga")):
                        src = sg[:, m, i] if m < 2 else bank(n, m)[:]
                        if m >= 2:
                            wait_job(act, g, n, m)
                        nc.scalar.activation(sg[:, m % 2, i], src, ACT.Sigmoid).then_inc(sig_ready, 1)

                norm(g, 1)
                norm_turned(g, 1)

                def keep_q(hd, i):
                    n = 2 * hd + i
                    wait_job(act, g, "pq", hd, i)
                    if n >= 4:
                        wait_job(act, g, "ss", (n - 4) // 2, i)
                    nc.scalar.activation(qd[:, n % 4], bank("pq", hd, i)[:], ACT.Copy).then_inc(qd_ready, 1)

                def gate_exp(hd):
                    act.wait_ge(garg_ready, g * PH + hd + 1)
                    nc.scalar.activation(vals[:, hd % 2], vals[:, hd % 2], ACT.Exp).then_inc(gexp_ready, 1)

                keep_q(0, 0)
                keep_q(0, 1)
                for hd in range(PH):
                    if hd == HOIST and g + 1 < NG:
                        norm(g + 1, 0)
                    for i in range(2):
                        if hd + 1 < PH:
                            keep_q(hd + 1, i)
                        wait_job(act, g, "ss", hd, i)
                        if hd >= 2:
                            act.wait_ge(garg_ready, g * PH + hd - 1)
                        nc.scalar.activation(s12[:, hd % 2, i].rearrange("p t c -> p (t c)"), bank("ss", hd, i)[:],
                                             ACT.Copy).then_inc(ss_ready, 1)
                    if 0 < hd < PH - 1:
                        gate_exp(hd - 1)
                if g + 1 < NG:
                    norm_turned(g + 1, 0)
                gate_exp(PH - 2)
                gate_exp(PH - 1)
                if g:
                    for b in range(NMIX):
                        act.wait_ge(dot_done, (b + 1) * NSEL)
                        nc.scalar.activation(dots[:, b], dots[:, b], ACT.Gelu_apprx_tanh).then_inc(act_ready, 1)

        @block.gpsimd
        def _(pool):
            nc.gpsimd.memset(qz[:], 0.0)
            nc.gpsimd.memset(pr[:], 0.0)
            nc.gpsimd.memset(pT[:, :, 0:PAD], 0.0)
            nc.gpsimd.memset(kT[:, 0:CH], 0.0)
            nc.gpsimd.memset(v[:, 0], 0.0).then_inc(zeroed, 1)
            pool.wait_ge(consts_in, 16 * 5)
            own = [0]

            def gather_rows(first, end):
                for c in range(first, end):
                    if c >= TT:
                        pool.wait_ge(dot_done, c - TT + 1)
                    b, k = divmod(c, NSEL)
                    nc.gpsimd.indirect_dma_start(rows_of[b][:, c % TT], None, io["down"], bass.IndirectOffsetOnAxis(
                        idx[:, b, k:k + 1], 0)).then_inc(down_in[c % TT], 16)

            for g in range(NG):
                def link(ins):
                    own[0] += 1
                    ins.then_inc(pool_own, 1)
                    pool.wait_ge(pool_own, own[0])

                if g:
                    wait_job(pool, g - 1, "grp", NPOOL - 1)
                pool.wait_ge(rope_in, 16 * (g + 1))
                for j in range(NPOOL):
                    pool.wait_ge(p_ready, g * NPOOL + j + 1)
                    src, lo = pT[:, j], 0
                    for i in range(j + 1):
                        lo += 1 << i
                        dst = sums[:, i % 2]
                        link(nc.gpsimd.tensor_tensor(dst[:, lo:], src[:, lo:], src[:, lo - (1 << i):PAD + TG - (1 << i)], ALU.add))
                        src = dst
                    head = src[:, PAD:2 * PAD]
                    link(nc.gpsimd.tensor_tensor(head, head, rope[:, R_CNT + j * PAD:R_CNT + (j + 1) * PAD], ALU.mult))
                    link(nc.gpsimd.tensor_scalar(src[:, PAD:], src[:, PAD:], 1.0 / (2 << j), None, ALU.mult))
                    nc.gpsimd.tensor_tensor(pooled[:, j], src[:, PAD:], pT[:, j, PAD:], ALU.subtract).then_inc(pooled_ready, 1)
                    pool.wait_ge(pooled_ready, g * NPOOL + j + 1)

                if g:
                    nc.gpsimd.tensor_copy(idx[:], eidx[:, 0:NMIX]).then_inc(idx_copied, 1)
                    pool.wait_ge(idx_copied, 1)
                    pool.wait_ge(h_ready, g * 2 * TT + TT)
                    gather_rows(0, NSEL)
                    wait_job(pool, g, "sc", TT - 1, 3)
                    gather_rows(NSEL, NSEL + TT + DOTS_XO + DOTS_NORM)

                if g:
                    pool.wait_ge(gffn_in, 16)
                for t in range(TT):
                    pool.wait_ge(h_ready, g * 2 * TT + TT + t + 1)
                    pool.wait_ge(x2_out, 16 * (g * TT + TT))
                    nc.gpsimd.tensor_tensor(x[:, t], h[:, t], gffn[:], ALU.mult).then_inc(h2_ready, 1)

                if g + 1 < NG:
                    wait_job(pool, g, "pv", TT - 1)
                    nc.gpsimd.tensor_copy(pT[:, :, 0:PAD], pT[:, :, TG:TG + PAD]).then_inc(carried, 1)
                    nc.gpsimd.tensor_copy(kT[:, 0:CH], kT[:, TG:TG + CH]).then_inc(carried, 1)
                    nc.gpsimd.tensor_copy(v[:, 0], v[:, TT]).then_inc(carried, 1)

                for hd in range(PH):
                    if g:
                        gather_rows(rows_by_head(hd - 1), rows_by_head(hd))
                    cols = slice(hd * TOPK, (hd + 1) * TOPK)
                    for i in range(2):
                        pool.wait_ge(hit_ready, g * 2 * PH + 2 * hd + i + 1)
                        hit = hits[i].rearrange("p (t k) j -> p t k j", t=TT)
                        link(nc.gpsimd.tensor_tensor(hit, hit, itopf[:, i].unsqueeze(2)
                                                     .to_broadcast([P, TT, TOPK, TOPK]), ALU.mult))
                        for n in (8, 4, 2, 1):
                            dst = hit[:, :, :, 0:n] if n > 1 else sel[:, i, :, cols].unsqueeze(3)
                            link(nc.gpsimd.tensor_tensor(dst, hit[:, :, :, 0:n], hit[:, :, :, n:2 * n], ALU.add))
                    if g + 1 == NG:
                        pool.sem_inc(chosen, 1)
                        continue
                    scaled = hits[0].rearrange("p n j -> p (n j)")[:, 0:TT * TOPK].rearrange("p (t k) -> p t k", t=TT)
                    link(nc.gpsimd.tensor_scalar(scaled, sel[:, 0, :, cols], float(NK), None, ALU.mult))
                    link(nc.gpsimd.tensor_tensor(scaled, scaled, sel[:, 1, :, cols], ALU.add))
                    nc.gpsimd.tensor_copy(eidx[:, :, cols], scaled).then_inc(chosen, 1)
                    pool.wait_ge(chosen, g * PH + hd + 1)

                if g:
                    gather_rows(rows_by_head(PH - 1), NMIX * NSEL)

                pool.wait_ge(topk_done, g * PH + PH)
                of = slice(g * TT, (g + 1) * TT)
                for name, src in (("sel1", sel[:, 0]), ("sel2", sel[:, 1]), ("eidx", eidx[:]), ("gate", gate[:])):
                    if name != "eidx" or g + 1 < NG:
                        pool.dma_start(scr[name][of].rearrange("t p n -> p t n"), src).then_inc(choice_out, 16)

        @block.vector
        def _(dve):
            own = [0]
            for g in range(NG):
                def link(ins):
                    own[0] += 1
                    ins.then_inc(dve_own, 1)
                    dve.wait_ge(dve_own, own[0])

                def mark(ins):
                    own[0] += 1
                    ins.then_inc(dve_own, 1)

                def linked():
                    dve.wait_ge(dve_own, own[0])

                def norm(g, n):
                    dve.wait_ge(ssq_ready, 2 * g + n + 1)
                    nc.vector.tensor_scalar(var, ssq, 1.0 / D, EPS, ALU.mult, ALU.add).then_inc(var_ready, 1)
                    dve.wait_ge(std_ready, 2 * g + n + 1)
                    link(nc.vector.reciprocal(rinv, std))
                    link(nc.vector.tensor_tensor(tmp, rinv, rinv, ALU.mult))
                    link(nc.vector.tensor_tensor(tmp, tmp, var, ALU.mult))
                    link(nc.vector.tensor_scalar(tmp, tmp, -0.5, 1.5, ALU.mult, ALU.add))
                    nc.vector.tensor_tensor(rinv, rinv, tmp, ALU.mult).then_inc(rinv_ready, 1)

                if g == 0:
                    norm(0, 0)
                    dve.wait_ge(consts_in, 16 * 5)

                def some_dots(n):
                    for c in range(dots_made[0], dots_made[0] + n if g else 0):
                        b, k = divmod(c, NSEL)
                        dve.wait_ge(down_in[c % TT], 16 * (c // TT + 1))
                        if k == 0:
                            dve.wait_ge(h2_in[b], 16)
                        row = rows_of[b][:, c % TT]
                        nc.vector.tensor_tensor_reduce(out=row, in0=row, in1=h2_of[b], scale=1.0, scalar=0.0, op0=ALU.mult,
                                                       op1=ALU.add, accum_out=dots[:, b, k:k + 1]).then_inc(dot_done, 1)
                    dots_made[0] += n if g else 0

                dots_made = [0]

                dve.wait_ge(rope_in, 16 * (g + 1))
                if g:
                    dve.wait_ge(chosen, g * PH)
                    dve.wait_ge(carried, 3 * g)
                    wait_job(dve, g - 1, "sc", TT - 1, 3)
                else:
                    dve.wait_ge(zeroed, 1)
                for i in range(5):
                    dve.wait_ge(raw_ready, g * 5 + i + 1)
                    mark(nc.vector.tensor_tensor(rot[:, 0], raw[:, i % 2], rope[:, R_COS:R_COS + TG], ALU.mult))
                    wait_job(dve, g, "rot", i)
                    link(nc.vector.tensor_tensor(rot[:, 1], bank("rot", i)[:], rope[:, R_SIN:R_SIN + TG], ALU.mult))
                    if i == 0:
                        nc.vector.tensor_tensor(kT[:, CH:], rot[:, 0], rot[:, 1], ALU.add).then_inc(roped, 1)
                    else:
                        mark(nc.vector.tensor_tensor(qz[0:HD, i - 1], rot[0:HD, 0], rot[0:HD, 1], ALU.add))
                        nc.vector.tensor_tensor(qz[HD:P, i + 3], rot[HD:P, 0], rot[HD:P, 1], ALU.add).then_inc(roped, 1)
                    dve.wait_ge(roped, g * 5 + i + 1)

                sink = vecs[:, V_SINK:V_SINK + NH]

                def maxima(t):
                    for i in range(4):
                        wait_job(dve, g, "sc", t, i)
                        mark(nc.vector.tensor_reduce(mx[:, 2 * i:2 * i + 2],
                                                     bank("sc", t, i)[:, 0:2 * WK].rearrange("p (e c) -> p e c", e=2),
                                                     AX.X, ALU.max))
                    linked()
                    if t:
                        dve.wait_ge(exp_ready, g * 9 * TT + 9 * t)
                    link(nc.vector.scalar_tensor_tensor(out=mx, in0=mx, scalar=HD ** -0.5, in1=sink, op0=ALU.mult, op1=ALU.max))
                    mark(nc.vector.tensor_scalar(negm, mx, -1.0, None, ALU.mult))
                    nc.vector.tensor_tensor(sarg, sink, mx, ALU.subtract).then_inc(m_ready, 1)
                    dve.wait_ge(m_ready, g * TT + t + 1)

                maxima(0)
                for t in range(TT):
                    some_dots(DOTS_TILE)
                    for i in range(4):
                        wait_job(dve, g, "pT", t, i)
                        nc.vector.tensor_copy(prT[:, 4 * i:4 * i + 4].rearrange("p a c -> p (a c)"),
                                              bank("pT", t, i)[:]).then_inc(prT_ready, 1)
                    if t + 1 < TT:
                        maxima(t + 1)
                    dve.wait_ge(exp_ready, g * 9 * TT + 9 * t + 9)
                    link(nc.vector.tensor_tensor(den, rs[t % 2], es[t % 2], ALU.add))
                    link(nc.vector.reciprocal(den, den))
                    wait_job(dve, g, "pv", t)
                    nc.vector.tensor_tensor(ya[:].rearrange("p (a c) -> p a c", a=NH),
                                            bank("pv", t)[:].rearrange("p (a c) -> p a c", a=NH),
                                            den.unsqueeze(2).to_broadcast([P, NH, HD]), ALU.mult).then_inc(ya_ready, 1)
                    some_dots(DOTS_TILE)

                for m in range(KD):
                    for i, n in enumerate(("bp", "ba")):
                        wait_job(dve, g, n, m)
                        dve.wait_ge(sig_ready, g * 2 * KD + 2 * m + 1 + i)
                        mark(nc.vector.tensor_tensor(sg[:, m % 2, i], bank(n, m)[:], sg[:, m % 2, i], ALU.mult))
                    linked()
                    nc.vector.tensor_tensor(mT[:, m], sg[:, m % 2, 0], sg[:, m % 2, 1], ALU.add).then_inc(merged, 1)
                    some_dots(DOTS_MERGE if m < KD - 1 else NSEL - dots_made[0])

                if g:
                    for t in range(TT):
                        dve.wait_ge(x_in[t], 16 * (NG + 1))
                for t in range(TT):
                    for n in range(2):
                        wait_job(dve, g, "xo", t, n)
                        part = x[:, t, n * 512:(n + 1) * 512]
                        nc.vector.tensor_tensor(part, part, bank("xo", t, n)[:], ALU.add).then_inc(x2_ready, 1)
                        if t * 2 + n < 2 * TT - 1:
                            some_dots(DOTS_XO // (2 * TT - 1))

                norm(g, 1)

                def top16(hd, chains):
                    def step(op, first):
                        if g and not first:
                            some_dots(min(1, rows_by_head(hd) - TT - dots_made[0]))
                        for c, (scores, masked, values, places) in enumerate(chains):
                            if not first:
                                dve.wait_ge(dve_own, done[c])
                            mark(op(scores, masked, values, places))
                            done[c] = own[0]

                    done = [0] * len(chains)
                    step(lambda s, m, v, p: nc.vector.max(v[:, 0:8], s), True)
                    step(lambda s, m, v, p: nc.vector.match_replace(m, v[:, 0:8], s, NEG_BIG), False)
                    step(lambda s, m, v, p: nc.vector.max(v[:, 8:16], m), False)
                    step(lambda s, m, v, p: nc.vector.max_index(p[:, 0:8], v[:, 0:8], s), True)
                    step(lambda s, m, v, p: nc.vector.max_index(p[:, 8:16], v[:, 8:16], m), False)
                    linked()

                iota = const[:, C_IOTA:C_IOTA + TOPK]
                dve.wait_ge(pooled_ready, (g + 1) * NPOOL)

                def norm_gates(hd):
                    dve.wait_ge(gexp_ready, g * PH + hd + 1)
                    cols = slice(hd * TOPK, (hd + 1) * TOPK)
                    link(nc.vector.tensor_reduce(gsm[:, 1], vals[:, hd % 2], AX.X, ALU.add))
                    link(nc.vector.reciprocal(gsm[:, 1], gsm[:, 1]))
                    nc.vector.tensor_tensor(gate[:, :, cols], vals[:, hd % 2], gsm[:, 1].unsqueeze(2).to_broadcast([P, TT, TOPK]),
                                            ALU.mult).then_inc(topk_done, 1)
                    dve.wait_ge(topk_done, g * PH + hd + 1)

                some_dots(DOTS_NORM)
                if g:
                    dve.wait_ge(choice_out, 64 * g)
                for hd in range(PH):
                    if hd == HOIST and g + 1 < NG:
                        norm(g + 1, 0)
                    dve.wait_ge(ss_ready, g * 2 * PH + 2 * hd + 2)
                    def halves(ts):
                        return [(s12[:, hd % 2, i, t], smask[:, 2 * (t % 2) + i], vtop[:, t % 2, i], itop[:, i, t])
                                for t in ts for i in range(2)]

                    def pair_sums(ts):
                        a, b = vtop[:, :, 0], vtop[:, :, 1]
                        last = NCAND - HALF_ROW
                        mark(nc.vector.tensor_tensor(cand[:, :, 0:TOPK], a[:, :, 0:1].to_broadcast([P, 2, TOPK]), b, ALU.add))
                        mark(nc.vector.tensor_tensor(
                            cand[:, :, TOPK:last].rearrange("p t (i j) -> p t i j", j=HALF_ROW),
                            a[:, :, 1:HALF_ROW].unsqueeze(3).to_broadcast([P, 2, HALF_ROW - 1, HALF_ROW]),
                            b[:, :, 0:HALF_ROW].unsqueeze(2).to_broadcast([P, 2, HALF_ROW - 1, HALF_ROW]), ALU.add))
                        mark(nc.vector.tensor_tensor(cand[:, :, last:], a[:, :, HALF_ROW:],
                                                     b[:, :, 0:1].to_broadcast([P, 2, HALF_ROW]), ALU.add))
                        linked()
                        return [(cand[:, t % 2], cmask[:, t % 2], vals[:, hd % 2, t], ctop[:, t]) for t in ts]

                    top16(hd, halves((0, 1)))
                    top16(hd, pair_sums((0, 1)) + halves((2, 3)))
                    top16(hd, pair_sums((2, 3)))
                    mark(nc.vector.tensor_scalar(cij[:, 0], ctop[:], 3, None, ALU.logical_shift_right))
                    mark(nc.vector.tensor_scalar(cij[:, 1], ctop[:], HALF_ROW - 1, None, ALU.bitwise_and))
                    mark(nc.vector.tensor_copy(place[:, 0], ctop[:]))
                    mark(nc.vector.tensor_copy(gsm[:, 0], vals[:, hd % 2, :, 0]))
                    linked()
                    if g * PH + hd:
                        dve.wait_ge(chosen, g * PH + hd)
                    mark(nc.vector.tensor_copy(itopf[:], itop[:]))
                    row, low, is_last = cijf[:, 0], cijf[:, 1], place[:, 1]
                    mark(nc.vector.tensor_copy(cijf[:], cij[:]))
                    mark(nc.vector.tensor_tensor(vals[:, hd % 2], vals[:, hd % 2],
                                                 gsm[:, 0].unsqueeze(2).to_broadcast([P, TT, TOPK]), ALU.subtract))
                    linked()
                    dve.sem_inc(garg_ready, 1)
                    link(nc.vector.scalar_tensor_tensor(out=is_last, in0=place[:, 0], scalar=float(NCAND - HALF_ROW), in1=low,
                                                        op0=ALU.is_ge, op1=ALU.mult))
                    link(nc.vector.tensor_tensor(low, low, is_last, ALU.subtract))
                    mark(nc.vector.tensor_scalar(place[:, 0], row, 1.0, float(HALF_ROW), ALU.is_equal, ALU.mult))
                    linked()
                    mark(nc.vector.tensor_tensor(low, low, place[:, 0], ALU.add))
                    link(nc.vector.tensor_scalar(row, row, -1.0, 0.0, ALU.add, ALU.max))
                    link(nc.vector.tensor_tensor(row, row, is_last, ALU.add))
                    for i in range(2):
                        nc.vector.tensor_tensor(hits[i], cijf[:, i].rearrange("p t k -> p (t k)").unsqueeze(2)
                                                .to_broadcast([P, TT * TOPK, TOPK]),
                                                iota.unsqueeze(1).to_broadcast([P, TT * TOPK, TOPK]),
                                                ALU.is_equal).then_inc(hit_ready, 1)
                    if hd:
                        norm_gates(hd - 1)
                norm_gates(PH - 1)
                if g:
                    some_dots(NMIX * NSEL - dots_made[0])


NQ = NK // 4
QT = 4
TC = 32
NTC = TG // TC
NB1 = NBLK // 2


def gate_table(nc, io, scr):
    QUADS = 2 * TC // 4
    ROH = 4
    LEAD = 10
    NB = NB1 - NMIX
    RD = 16
    NDOT = NB * TOPK
    assert NTC // 2 == PH
    with ExitStack() as ctx:
        def sb(name, shape, dt=F32):
            return ctx.enter_context(nc.sbuf_tensor(name, shape, dt))

        def sem(name):
            return ctx.enter_context(nc.semaphore(name))

        const = sb("t_const", [P, NCONST])
        rows = sb("t_rows", [P, 3, TT, NSEL])
        cols = sb("t_cols", [P, 3, TG])
        hot = sb("hot", [P, ROH, 2, 4, P])
        out = sb("t_out", [P, 2, NQ, QT, TC])
        banks = [ctx.enter_context(nc.psum_tensor(f"tbank{i}", [P, 512], F32)) for i in range(ROH)]
        h2 = sb("t_h2", [P, NB, D])
        idx_all, idx = sb("idx_all", [P, NB, NSEL], I32), sb("t_idx", [P, NB, TOPK], I32)
        down = sb("down", [P, RD, D])
        dots, act_all = sb("t_dots", [P, NB, TOPK]), sb("act_all", [P, NB, NSEL])
        tbank = [ctx.enter_context(nc.psum_tensor(f"tturn{i}", [P, TG], F32)) for i in range(3)]

        rows_in, turned, cols_ready = sem("rows_in"), sem("turned"), sem("cols_ready")
        hot_ready = sem("hot_ready")
        hot_weighed = sem("hot_weighed")
        quad_done = sem("quad_done")
        quad_kept = sem("quad_kept")
        chunk_out = [sem(f"chunk_out{i}") for i in range(2)]
        sp_waits = sem("t_sp_waits")
        chunk_free = [sem(f"chunk_free{i}") for i in range(2)]
        idx_in, h2_in = sem("t_idx_in"), sem("t_h2_in")
        idx_copied = sem("t_idx_copied")
        down_in = [sem(f"t_down_in{i}") for i in range(RD)]
        dot_done = sem("t_dot_done")
        gelu_done = sem("gelu_done")
        act_out = sem("t_act_out")
        pool_waits = sem("t_pool_waits")

        block = ctx.enter_context(nc.Block())
        iota = const[:, C_IOTA:C_IOTA + P]

        @block.sync
        def _(sp):
            sp.dma_start(idx_all[:], scr["eidx"][NMIX:NB1].rearrange("t p n -> p t n")).then_inc(idx_in, 16)
            sp.dma_start(const[:], io["const"]).then_inc(rows_in, 16)
            for i, name in enumerate(("sel1", "sel2", "gate")):
                sp.dma_start(rows[:, i], scr[name][TT:2 * TT].rearrange("t p n -> p t n")).then_inc(rows_in, 16)
            sp.dma_start(h2[:], scr["h2"][NMIX:NB1].rearrange("t p n -> p t n")).then_inc(h2_in, 16)
            with sp.Fori(0, NTC // 2) as m:
                for i in range(2):
                    sp.wait_ge(quad_kept, QUADS * m + (i + 1) * QUADS // 2 + ROH)
                    sp.sem_inc(sp_waits, 1)
                    dst = scr["table"][:, :, bass.ds(2 * m + i, 1)].rearrange("q p a c -> p q (a c)")
                    sp.dma_start(dst, out[:, i].rearrange("p q e t -> p q (e t)")).then_inc(chunk_out[i], 16)
                for i in range(2):
                    sp.wait_ge(chunk_out[i], 16 * (m + 1))
                    sp.sem_inc(chunk_free[i], 1)
            sp.wait_ge(gelu_done, NB * PH + NB)
            sp.dma_start(scr["act"][NMIX:NB1].rearrange("t p n -> p t n"), act_all[:]).then_inc(act_out, 16)
            sp.wait_ge(act_out, 16)

        @block.gpsimd
        def _(pool):
            pool.wait_ge(idx_in, 16)

            def gather_pair(m, n):
                i, k = divmod(n, TOPK)
                if k == 0:
                    pool.wait_ge(dot_done, NDOT * m + TOPK * (i + 1))
                    pool.sem_inc(pool_waits, 1)
                    of = slice(0, TOPK) if isinstance(m, int) and m == 0 else bass.ds(m * TOPK, TOPK)
                    nc.gpsimd.tensor_copy(idx[:, i], idx_all[:, i, of]).then_inc(idx_copied, 1)
                    pool.wait_ge(idx_copied, NB * m + i + 1)
                pool.wait_ge(dot_done, NDOT * m + n + 2 + NDOT - RD)
                pool.sem_inc(pool_waits, 1)
                for c in range(n, n + 2):
                    nc.gpsimd.indirect_dma_start(down[:, c % RD], None, io["down"], bass.IndirectOffsetOnAxis(
                        idx[:, i, c % TOPK:c % TOPK + 1], 0)).then_inc(down_in[c % RD], 16)

            def turn(m, last):
                for u in range(QUADS):
                    for n in range(NDOT * u // QUADS + LEAD, NDOT * (u + 1) // QUADS + LEAD, 2):
                        if n < NDOT:
                            gather_pair(m, n)
                        elif not last:
                            gather_pair(m + 1, n - NDOT)
                    if u == 0:
                        pool.wait_ge(cols_ready, 3)
                    pool.wait_ge(hot_ready, QUADS * m + u + 1)
                    pool.sem_inc(pool_waits, 1)
                    of = cols[:, 2, bass.ds(m * 2 * TC + 4 * u, 4)]
                    nc.gpsimd.tensor_tensor(hot[:, u % ROH, 0], hot[:, u % ROH, 0], of.unsqueeze(2).to_broadcast([P, 4, P]),
                                            ALU.mult).then_inc(hot_weighed, 1)

            for n in range(0, LEAD, 2):
                gather_pair(0, n)
            with pool.Fori(0, PH - 1) as m:
                turn(m, False)
            turn(PH - 1, True)

        @block.tensor
        def _(pe):
            pe.sem_inc(quad_done, ROH)
            pe.wait_ge(rows_in, 64)
            for i in range(3):
                for t in range(TT):
                    ins = nc.tensor.transpose(tbank[i][:, t * P:(t + 1) * P], rows[:, i, t], const[:, C_IDENT:C_IDENT + P])
                ins.then_inc(turned, 1)
            with pe.Fori(0, NTC // 2) as m:
                for u in range(QUADS):
                    pe.wait_ge(hot_weighed, QUADS * m + u + 1)
                    pe.wait_ge(quad_kept, QUADS * m + u + 1)
                    for t in range(4):
                        ins = nc.tensor.matmul(banks[u % ROH][:, t * P:(t + 1) * P], hot[:, u % ROH, 1, t],
                                               hot[:, u % ROH, 0, t], start=True, stop=True)
                    ins.then_inc(quad_done, 1)

        @block.scalar
        def _(act):
            act.sem_inc(quad_kept, ROH)
            for i in range(3):
                act.wait_ge(turned, i + 1)
                nc.scalar.activation(cols[:, i], tbank[i][:], ACT.Copy).then_inc(cols_ready, 1)
            with act.Fori(0, NTC // 2) as m:
                for u in range(QUADS):
                    i, t = u // (QUADS // 2), u % (QUADS // 2) * 4
                    if t == 0:
                        act.wait_ge(chunk_free[i], m + 1)
                    act.wait_ge(quad_done, QUADS * m + u + 1 + ROH)
                    nc.scalar.activation(out[:, i].rearrange("p q e t -> p t (q e)")[:, t:t + 4],
                                         banks[u % ROH][:].rearrange("p (t i) -> p t i", t=4), ACT.Copy).then_inc(quad_kept, 1)
                    for b in range(NB):
                        if u == (QUADS * (b + 1) - 1) // NB:
                            act.wait_ge(dot_done, NDOT * m + TOPK * (b + 1) + NDOT)
                            nc.scalar.activation(act_all[:, b, bass.ds(m * TOPK, TOPK)], dots[:, b],
                                                 ACT.Gelu_apprx_tanh).then_inc(gelu_done, 1)

        @block.vector
        def _(dve):
            for i in range(2):
                dve.sem_inc(chunk_free[i], 1)
            dve.sem_inc(dot_done, NDOT)
            dve.sem_inc(gelu_done, NB)
            dve.wait_ge(cols_ready, 3)
            dve.wait_ge(h2_in, 16)
            with dve.Fori(0, NTC // 2) as m:
                for u in range(QUADS):
                    dve.wait_ge(quad_done, QUADS * m + u + 1)
                    of = cols[:, 0:2, bass.ds(m * 2 * TC + 4 * u, 4)]
                    nc.vector.tensor_tensor(hot[:, u % ROH], iota.unsqueeze(1).unsqueeze(1).to_broadcast([P, 2, 4, P]),
                                            of.unsqueeze(3).to_broadcast([P, 2, 4, P]), ALU.is_equal).then_inc(hot_ready, 1)
                    for n in range(NDOT * u // QUADS, NDOT * (u + 1) // QUADS):
                        b, k = n // TOPK, n % TOPK
                        if k == 0:
                            dve.wait_ge(gelu_done, NB * m + b + 1)
                        dve.wait_ge(down_in[n % RD], 16 * (NDOT // RD * m + n // RD + 1))
                        row = down[:, n % RD]
                        nc.vector.tensor_tensor_reduce(out=row, in0=row, in1=h2[:, b], scale=1.0, scalar=0.0, op0=ALU.mult,
                                                       op1=ALU.add, accum_out=dots[:, b, k:k + 1]).then_inc(dot_done, 1)


RU = 8
CHUNK = 4
NSTEP = NB1 * PH
assert NSTEP == NQ


def experts(nc, io, scr):
    NPAIR = 2 * NSTEP
    NOP = 8
    with ExitStack() as ctx:
        def sb(name, shape, dt=F32):
            return ctx.enter_context(nc.sbuf_tensor(name, shape, dt))

        def sem(name):
            return ctx.enter_context(nc.semaphore(name))

        next_act, next_gate = sb("next_act", [P, NSEL]), sb("next_gate", [P, NSEL])
        next_idx, idx_up = sb("next_idx", [P, NSEL], I32), sb("idx_up", [P, NSEL], I32)
        wts = sb("wts", [P, NSEL])
        up = sb("up", [P, RU, D])
        acc, x3 = sb("acc", [P, D]), sb("x3", [P, D])
        x2, gfin = sb("e_x2", [P, D]), sb("gfin", [P, D])
        stat = sb("e_stat", [P, 5, TT])
        h2T_hi, h2T_lo = sb("h2T_hi", [P, KD, TG], F32R), sb("h2T_lo", [P, KD, TG], F32R)
        tdown = sb("tdown", [P, 2, D])
        tdown_hi, tdown_lo = sb("tdown_hi", [P, 2, D], F32R), sb("tdown_lo", [P, 2, D], F32R)
        tup = sb("tup", [P, 2, D])
        tup_hi, tup_lo = sb("tup_hi", [P, 2, 2, D], F32R), sb("tup_lo", [P, 2, 2, D], F32R)
        gates = sb("gates", [P, 2, NTC, QT, TC])
        gl = sb("gl", [P, 2, TG])
        w, w_hi, w_lo = sb("w", [P, 2, TG]), sb("w_hi", [P, 2, 2, TG], F32R), sb("w_lo", [P, 2, 2, TG], F32R)
        y = sb("y", [P, TT, D])
        h2T = up[:, 0:KD * TG // D].rearrange("p a d -> p (a d)").rearrange("p (k n) -> p k n", k=KD)
        abank = [ctx.enter_context(nc.psum_tensor(f"abank{i}", [P, TG], F32)) for i in range(2)]
        ybank = [ctx.enter_context(nc.psum_tensor(f"ybank{i}", [P, 512], F32)) for i in range(4)]

        idx_in, act_in = sem("idx_in"), sem("act_in")
        idx_taken, wts_ready = sem("idx_taken"), sem("wts_ready")
        idx_copied = sem("idx_copied")
        pool_waits, sp_waits = sem("pool_waits"), sem("sp_waits")
        up_in = [sem(f"up_in{i}") for i in range(RU)]
        up_used = sem("up_used")
        gfin_in, x2_in = sem("gfin_in"), sem("e_x2_in")
        x2_used = sem("x2_used")
        ssq_ready = sem("e_ssq_ready")
        norm_own = sem("norm_own")
        var_ready, std_ready = sem("e_var_ready"), sem("e_std_ready")
        normed = sem("normed")
        out_done = sem("out_done")
        h2T_in, h2T_halved, h2T_low = sem("h2T_in"), sem("h2T_halved"), sem("h2T_low")
        tdown_in = [sem(f"tdown_in{i}") for i in range(2)]
        tup_in = [sem(f"tup_in{i}") for i in range(2)]
        down_high, down_low = sem("down_high"), sem("down_low")
        up_high, up_low = sem("up_high"), sem("up_low")
        gates_in = [sem(f"gates_in{i}") for i in range(2)]
        a_ready = sem("a_ready")
        gl_ready = sem("gl_ready")
        w_ready, w_high, w_low = sem("w_ready"), sem("w_high"), sem("w_low")
        y_ready = sem("y_ready")
        y_added = sem("y_added")
        y_in = sem("y_in")

        block = ctx.enter_context(nc.Block())

        def blocks(eng, one):
            with eng.Fori(0, NB1 - 1) as b:
                one(b, False)
            one(NB1 - 1, True)

        def pairs(b, last):
            for h in range(PH):
                for r in range(2):
                    end = last and h == PH - 1
                    yield b * PH + h, h, r, 2 * (b * PH + h) + r, not (end and r), not end

        def at(dram, i):
            return dram[i] if isinstance(i, int) else dram[bass.ds(i, 1)].rearrange("a p n -> p (a n)")

        @block.sync
        def _(sp):
            def load_tdown(p, q):
                sp.dma_start(tdown[:, q], at(io["downT"], 2 * p + q)).then_inc(tdown_in[q], 16)

            def load_tup(p, q):
                sp.dma_start(tup[:, q], at(up_tiles, 2 * p + q)).then_inc(tup_in[q], 16)

            def load_gates(n, par):
                sp.dma_start(gates[:, par].rearrange("p c e t -> p (c e t)"), at(table, n)).then_inc(gates_in[par], 16)

            def hold(sem, count):
                sp.wait_ge(sem, count)
                sp.sem_inc(sp_waits, 1)

            up_tiles = io["up"].rearrange("(e p) d -> e p d", p=P)
            table = scr["table"].rearrange("q p c n -> q p (c n)")
            load_tdown(0, 0)
            sp.dma_start(h2T.rearrange("p k n -> p (k n)"), scr["h2T"][1]).then_inc(h2T_in, 16)
            load_tdown(0, 1)
            for q in range(2):
                load_tup(0, q)
            sp.dma_start(next_idx[:], scr["eidx"][0]).then_inc(idx_in, 16)
            load_gates(0, 0)
            sp.dma_start(next_act[:], scr["act"][0]).then_inc(act_in, 16)
            sp.dma_start(next_gate[:], scr["gate"][0]).then_inc(act_in, 16)
            sp.dma_start(y[:], scr["x2"][NB1:NBLK].rearrange("t p d -> p t d")).then_inc(y_in, 16)
            for q in range(2):
                sp.wait_ge(down_low, q + 1)
                load_tdown(1, q)
            for q in range(2):
                sp.wait_ge(up_low, q + 1)
                load_tup(1, q)
            load_gates(1, 1)
            sp.dma_start(gfin[:], io["gfin"]).then_inc(gfin_in, 16)

            def one(b, last):
                for n, h, r, p, more, more2 in pairs(b, last):
                    if more2:
                        for q in range(2):
                            hold(down_low, 2 * (p + 1) + q + 1)
                            load_tdown(p + 2, q)
                        for q in range(2):
                            hold(up_low, 2 * (p + 1) + q + 1)
                            load_tup(p + 2, q)
                    if h == 1 and r == 0 and not last:
                        hold(idx_taken, b + 1)
                        sp.dma_start(next_idx[:], at(scr["eidx"], b + 1)).then_inc(idx_in, 16)
                        hold(wts_ready, b + 1)
                        sp.dma_start(next_act[:], at(scr["act"], b + 1)).then_inc(act_in, 16)
                        sp.dma_start(next_gate[:], at(scr["gate"], b + 1)).then_inc(act_in, 16)
                    if h == 2 and r == 0:
                        hold(x2_used, b + 1)
                        sp.dma_start(x2[:], at(scr["x2"], b)).then_inc(x2_in, 16)
                    if r == 1 and not (last and h >= PH - 2):
                        hold(w_ready, QT * (n + 1))
                        load_gates(n + 2, h % 2)
                hold(normed, b + 1)
                sp.dma_start(at(io["out"], b), x3[:]).then_inc(out_done, 16)

            blocks(sp, one)
            for t in range(TT):
                sp.wait_ge(normed, NB1 + t + 1)
                sp.dma_start(io["out"][NB1 + t], y[:, t]).then_inc(out_done, 16)
            sp.wait_ge(out_done, 16 * (NBLK + 1))

        @block.gpsimd
        def _(pool):
            def gather(dst, table, idx, h, k, arrived):
                nc.gpsimd.indirect_dma_start(dst, None, table, bass.IndirectOffsetOnAxis(
                    idx[:, h * TOPK + k:h * TOPK + k + 1], 0)).then_inc(arrived, 16)

            def free(used, count):
                pool.wait_ge(used, count)
                pool.sem_inc(pool_waits, 1)

            def down_rest(p, q):
                pool.wait_ge(down_high, 2 * p + q + 1)
                nc.gpsimd.tensor_tensor(tdown_lo[:, q], tdown[:, q], tdown_hi[:, q].bitcast(F32), ALU.subtract).then_inc(down_low, 1)

            def up_rest(p, r, q):
                pool.wait_ge(up_high, 2 * p + q + 1)
                nc.gpsimd.tensor_tensor(tup_lo[:, r, q], tup[:, q], tup_hi[:, r, q].bitcast(F32), ALU.subtract).then_inc(up_low, 1)

            for q in range(2):
                down_rest(0, q)
            for q in range(2):
                up_rest(0, 0, q)
            for q in range(2):
                down_rest(1, q)
            pool.wait_ge(idx_in, 16)
            nc.gpsimd.tensor_copy(idx_up[:], next_idx[:]).then_inc(idx_copied, 1)
            pool.wait_ge(h2T_low, KD)

            def one(b, last):
                for n, h, r, p, more, more2 in pairs(b, last):
                    if r == 0:
                        free(idx_copied, n + 1)
                    for q in range(2):
                        c = r * TOPK // 2 + q * CHUNK
                        free(up_used, 16 * n + c + CHUNK)
                        for k in range(c, c + CHUNK):
                            gather(up[:, k % RU], io["up"], idx_up, h, k, up_in[k % RU])
                        if more:
                            up_rest(p + 1, 1 - r, q)
                        if more2:
                            down_rest(p + 2, q)
                    if r == 0:
                        continue
                    cols = slice((h - 1) % PH * TOPK, ((h - 1) % PH + 1) * TOPK)
                    if h == 1 and not last:
                        pool.wait_ge(idx_in, 16 * (b + 2))
                    free(up_used, 16 * n + RU)
                    nc.gpsimd.tensor_copy(idx_up[:, cols], next_idx[:, cols]).then_inc(idx_copied, 1)
                    if h == 0:
                        pool.wait_ge(idx_copied, n + 2)
                        pool.sem_inc(idx_taken, 1)
                pool.sem_clear(pool_waits)

            blocks(pool, one)

        @block.tensor
        def _(pe):
            pe.sem_inc(y_ready, 2 * TT)

            def product(out, terms, done, first=False):
                for i, (a_hi, a_lo, b_hi, b_lo) in enumerate(terms):
                    if first:
                        pe.wait_ge(h2T_low, i + 1)
                    nc.tensor.matmul(out, a_hi, b_hi, start=i == 0, stop=False)
                    nc.tensor.matmul(out, a_hi, b_lo, start=False, stop=False)
                    ins = nc.tensor.matmul(out, a_lo, b_hi, start=False, stop=i == len(terms) - 1)
                ins.then_inc(done, 1)

            def down_product(p, q, first=False):
                pe.wait_ge(down_low, 2 * p + q + 1)
                pe.wait_ge(gl_ready, 2 * p + q + 1)
                at = [slice(k * P, (k + 1) * P) for k in range(KD)]
                product(abank[q][:], [(tdown_hi[:, q, at[k]], tdown_lo[:, q, at[k]], h2T_hi[:, k], h2T_lo[:, k])
                                      for k in range(KD)], a_ready, first)

            def up_product(p, r, t):
                if t == 0:
                    pe.wait_ge(w_low, 2 * (p + 1))
                    pe.wait_ge(up_low, 2 * (p + 1))
                for i in range(2):
                    pe.wait_ge(y_added, 2 * TT * p + 2 * t + i + 1)
                    ts, ds = slice(t * P, (t + 1) * P), slice(i * 512, (i + 1) * 512)
                    product(ybank[t % 2 * 2 + i][:], [(w_hi[:, r, q, ts], w_lo[:, r, q, ts], tup_hi[:, r, q, ds], tup_lo[:, r, q, ds])
                                                      for q in range(2)], y_ready)

            for q in range(2):
                down_product(0, q, first=q == 0)

            def one(b, last):
                for n, h, r, p, more, more2 in pairs(b, last):
                    for t in range(TT):
                        if more and t % 2 == 0:
                            down_product(p + 1, t // 2)
                        up_product(p, r, t)

            blocks(pe, one)

        @block.scalar
        def _(act):
            act.sem_inc(gl_ready, 2)
            act.sem_inc(x2_used, 1)
            act.sem_inc(out_done, 16)

            def high(dst, src, done):
                nc.scalar.activation(dst, src, ACT.Copy).then_inc(done, 1)

            def down_high_of(p, q):
                act.wait_ge(tdown_in[q], 16 * (p + 1))
                high(tdown_hi[:, q], tdown[:, q], down_high)

            def up_high_of(p, r, q):
                act.wait_ge(tup_in[q], 16 * (p + 1))
                act.wait_ge(y_ready, 2 * TT * p)
                high(tup_hi[:, r, q], tup[:, q], up_high)

            def expert_gelu(p, q, first=False):
                act.wait_ge(a_ready, 2 * p + q + 1)
                if not first:
                    act.wait_ge(w_ready, 2 * p + q - 1)
                nc.scalar.activation(gl[:, q], abank[q][:], ACT.Gelu_apprx_tanh).then_inc(gl_ready, 1)

            def weights_high(p, r, q):
                act.wait_ge(w_ready, 2 * p + q + 1)
                high(w_hi[:, r, q], w[:, q], w_high)

            def root(c, n):
                act.wait_ge(var_ready, c + 1)
                nc.scalar.activation(stat[:, 2, 0:n], stat[:, 1, 0:n], ACT.Sqrt).then_inc(std_ready, 1)

            down_high_of(0, 0)
            act.wait_ge(h2T_in, 16)
            for k in range(KD):
                high(h2T_hi[:, k], h2T[:, k], h2T_halved)
            down_high_of(0, 1)
            for q in range(2):
                act.wait_ge(tup_in[q], 16)
                high(tup_hi[:, 0, q], tup[:, q], up_high)
            for q in range(2):
                expert_gelu(0, q, True)
                down_high_of(1, q)
            for q in range(2):
                weights_high(0, 0, q)

            def one(b, last):
                for n, h, r, p, more, more2 in pairs(b, last):
                    for q in range(2):
                        if more:
                            up_high_of(p + 1, 1 - r, q)
                            if q == 1:
                                weights_high(p + 1, 1 - r, 0)
                            expert_gelu(p + 1, q)
                        if more2:
                            down_high_of(p + 2, q)
                    if more:
                        weights_high(p + 1, 1 - r, 1)
                root(b, 1)

            blocks(act, one)
            act.wait_ge(normed, NB1)
            act.wait_ge(up_used, 16 * NSTEP + RU)
            for t in range(TT):
                act.wait_ge(y_added, 2 * TT * (NPAIR - 1) + 2 * t + 2 + 4)
                nc.scalar.activation(up[:, t], y[:, t], ACT.Square, accum_out=stat[:, 0, t:t + 1]).then_inc(ssq_ready, 1)
            root(NB1, TT)

        @block.vector
        def _(dve):
            dve.sem_inc(up_used, RU)
            dve.sem_inc(y_added, 4)

            def weigh(b):
                dve.wait_ge(act_in, 32 * (b + 1))
                nc.vector.tensor_tensor(wts[:], next_act[:], next_gate[:], ALU.mult).then_inc(wts_ready, 1)

            def add_row(n, b, h, k):
                dve.wait_ge(up_in[k % RU], 16 * (TOPK // RU * n + k // RU + 1))
                wt = wts[:, h * TOPK + k:h * TOPK + k + 1]
                if h == 0 and k == 0:
                    dve.wait_ge(wts_ready, b + 1)
                    nc.vector.tensor_scalar(acc[:], up[:, k % RU], wt, None, ALU.mult).then_inc(up_used, 1)
                else:
                    dve.wait_ge(up_used, 16 * n + k + RU)
                    nc.vector.scalar_tensor_tensor(out=acc[:], in0=up[:, k % RU], scalar=wt, in1=acc[:],
                                                   op0=ALU.mult, op1=ALU.add).then_inc(up_used, 1)

            def by_chunk(ap):
                return ap.rearrange("p (c t) -> p c t", t=TC)

            def weights(p, n, par, r, q, first=False):
                if q == 0:
                    if r == 0:
                        dve.wait_ge(gates_in[par], 16 * n + 16)
                    if not first:
                        dve.wait_ge(y_ready, 2 * TT * p)
                    if not first:
                        dve.wait_ge(w_low, 2 * p)
                dve.wait_ge(gl_ready, 2 * p + q + 3)
                nc.vector.tensor_tensor(by_chunk(w[:, q]), by_chunk(gl[:, q]), gates[:, par, :, 2 * r + q],
                                        ALU.mult).then_inc(w_ready, 1)

            def weights_rest(p, r, q):
                dve.wait_ge(w_high, 2 * p + q + 1)
                nc.vector.tensor_tensor(w_lo[:, r, q], w[:, q], w_hi[:, r, q].bitcast(F32), ALU.subtract).then_inc(w_low, 1)

            def add_y(p, t):
                for i in range(2):
                    dve.wait_ge(y_ready, 2 * TT * (p + 1) + 2 * t + i + 1)
                    part = y[:, t, i * 512:(i + 1) * 512]
                    nc.vector.tensor_tensor(part, part, ybank[t % 2 * 2 + i][:], ALU.add).then_inc(y_added, 1)

            def finish(c, rows):
                n, step = len(rows), [NOP * c + (2 if len(rows) == 1 else 0)]
                ssq, var, std, rinv, tmp = (stat[:, i, 0:n] for i in range(5))

                def link(ins):
                    step[0] += 1
                    ins.then_inc(norm_own, 1)
                    dve.wait_ge(norm_own, step[0])

                link(nc.vector.tensor_scalar(var, ssq, 1.0 / D, EPS, ALU.mult, ALU.add))
                dve.sem_inc(var_ready, 1)
                dve.wait_ge(std_ready, c + 1)
                link(nc.vector.reciprocal(rinv, std))
                link(nc.vector.tensor_tensor(tmp, rinv, rinv, ALU.mult))
                link(nc.vector.tensor_tensor(tmp, tmp, var, ALU.mult))
                link(nc.vector.tensor_scalar(tmp, tmp, -0.5, 1.5, ALU.mult, ALU.add))
                link(nc.vector.tensor_tensor(rinv, rinv, tmp, ALU.mult))
                for i, row in enumerate(rows):
                    nc.vector.scalar_tensor_tensor(out=row, in0=row, scalar=rinv[:, i:i + 1], in1=gfin[:],
                                                   op0=ALU.mult, op1=ALU.mult).then_inc(normed, 1)

            def finish_block(b):
                nc.vector.tensor_tensor(x3[:], acc[:], x2[:], ALU.add).then_inc(norm_own, 1)
                dve.wait_ge(norm_own, NOP * b + 1)
                dve.sem_inc(x2_used, 1)
                nc.vector.tensor_tensor_reduce(out=acc[:], in0=x3[:], in1=x3[:], scale=1.0, scalar=0.0, op0=ALU.mult,
                                               op1=ALU.add, accum_out=stat[:, 0, 0:1]).then_inc(norm_own, 1)
                dve.wait_ge(norm_own, NOP * b + 2)
                finish(b, [x3[:]])

            for k in range(KD):
                dve.wait_ge(h2T_halved, k + 1)
                nc.vector.tensor_tensor(h2T_lo[:, k], h2T[:, k], h2T_hi[:, k].bitcast(F32), ALU.subtract).then_inc(h2T_low, 1)
            weigh(0)
            for q in range(2):
                weights(0, 0, 0, 0, q, True)
            for q in range(2):
                weights_rest(0, 0, q)
            dve.wait_ge(y_in, 16)

            def one(b, last):
                for n, h, r, p, more, more2 in pairs(b, last):
                    par = (h + r) % 2
                    loads = b * (PH // 2) + (h + r) // 2
                    for t in range(TT):
                        for k in range(2):
                            add_row(n, b, h, r * TOPK // 2 + 2 * t + k)
                        if more and t == 2:
                            weights_rest(p + 1, 1 - r, 0)
                        add_y(p, t)
                        if more and t % 2 == 1:
                            weights(p + 1, loads, par, 1 - r, t // 2)
                    if more:
                        weights_rest(p + 1, 1 - r, 1)
                    if r == 1 and h == PH - 1:
                        if more:
                            weigh(b + 1)
                        dve.wait_ge(up_used, 16 * (n + 1) + RU)
                        dve.wait_ge(x2_in, 16 * (b + 1))
                        dve.wait_ge(out_done, 16 * (b + 1))
                        finish_block(b)

            dve.wait_ge(gfin_in, 16)
            blocks(dve, one)
            dve.wait_ge(ssq_ready, TT)
            finish(NB1, [y[:, t] for t in range(TT)])


def build(nc, io):
    scr = {n: nc.dram_tensor(f"all_{n}", shape, dt, kind="Internal").ap() for n, shape, dt in (
        ("x2", (NBLK, P, D), F32), ("h2", (NBLK, P, D), F32), ("h2T", (NG, P, KD * TG), F32),
        ("act", (NB1, P, NSEL), F32),
        ("eidx", (NBLK, P, NSEL), I32), ("sel1", (NBLK, P, NSEL), F32), ("sel2", (NBLK, P, NSEL), F32),
        ("gate", (NBLK, P, NSEL), F32), ("table", (NQ, P, NTC, QT * TC), F32))}
    mixer(nc, io, scr)
    gate_table(nc, io, scr)
    experts(nc, io, scr)


def slots_of(w_in, w_branch_pool, w_branch_attn, w_out, w_peer_q):
    def columns(w):
        k, n = w.shape[0] // P, w.shape[1] // P
        return w.reshape(k, P, n, P).transpose(2, 1, 0, 3).reshape(n, P, k * P)

    pool, q, k, v, gp, ga = np.split(w_in, np.cumsum([POOL_W, NH * HD, P, P, D]), axis=1)
    q = q.reshape(D, 2, 4, HD).transpose(0, 2, 1, 3).reshape(D, NH * HD)
    branches = np.concatenate([columns(w_branch_pool), columns(w_branch_attn)], axis=2)
    merge = np.stack([columns(gp), columns(ga), branches], axis=1).reshape(3 * KD, P, D)
    return np.concatenate([columns(pool), columns(k), columns(v), columns(q), merge,
                           w_out.reshape(KD, P, D), columns(w_peer_q)])


def constants():
    c = np.zeros((P, NCONST), np.float32)
    c[:, C_IDENT:C_IDENT + P] = np.eye(P)
    rot, half = HD // 4, HD // 8
    for base in (0, HD):
        for d in range(rot):
            c[base + (d + half) % rot, C_PERM + base + d] = 1
    c[0, C_ROWS:C_ROWS + CH] = 1
    c[1, C_ROWS + CH:C_ROWS + P] = 1
    mask = c[:, C_MASK:C_MASK + 4 * WK].reshape(P, 4, WK)
    mask[0, :, P:] = -1e30
    mask[1, :, 0:CH] = -1e30
    mask[0, 0:2, 0:CH] = -1e30
    c[:, C_IOTA:C_IOTA + P] = np.arange(P)

    pos = np.arange(T, dtype=np.float32)
    inv = np.float32(500000.0) ** (-np.arange(0, rot, 2, dtype=np.float32) / np.float32(rot))
    ang = pos[:, None] * inv[None, :]
    table = np.zeros((2, P, T), np.float32)
    table[0] = 1
    for base in (0, HD):
        table[0, base:base + rot] = np.tile(np.cos(ang).T, (2, 1))
        table[1, base:base + rot] = np.tile(np.sin(ang).T, (2, 1))
        table[1, base:base + half] *= -1
    r = np.ones((NG, P, NROPE), np.float32)
    r[:, :, R_COS:R_CNT] = table.reshape(2, P, NG, TG).transpose(2, 1, 0, 3).reshape(NG, P, 2 * TG)
    for j in range(NPOOL):
        w = 2 << j
        r[0, :, R_CNT + j * PAD:R_CNT + (j + 1) * PAD] = w / np.minimum(np.arange(PAD) + 1, w)
    return c, r


def arrays_of(x, g_mix, w_in, w_pool_grp, pool_scale, attn_sinks, w_branch_pool, w_branch_attn, w_out, g_ffn,
              w_peer_q, peer_keys_1, peer_keys_2, expert_down, expert_up, g_final):
    c, r = constants()
    vecs = np.concatenate([g_mix[0].reshape(KD, P).T, g_ffn[0].reshape(KD, P).T, pool_scale[0].reshape(NPOOL, P).T,
                           np.broadcast_to(attn_sinks[0], (P, NH))], axis=1)
    return {
        "x": x.reshape(NG, TT, P, D), "const": c, "rope": r, "vecs": vecs,
        "slots": slots_of(w_in[0], w_branch_pool[0], w_branch_attn[0], w_out[0], w_peer_q[0]),
        "keys": np.stack([peer_keys_1[0].T, peer_keys_2[0].T], axis=1),
        "wgrp": w_pool_grp[0].transpose(1, 0, 2),
        "gffn": np.broadcast_to(g_ffn[0], (P, D)), "gfin": np.broadcast_to(g_final, (P, D)),
        "down": expert_down[0], "up": expert_up[0],
        "downT": expert_down[0].reshape(NK, NK, KD, P).transpose(0, 3, 2, 1).reshape(NK, P, D),
    }


def kernel(**inputs):
    import concourse.bacc as bacc
    from concourse.bass_utils import run_bass_kernel_spmd

    nc = bacc.Bacc("TRN2", target_bir_lowering=False, num_devices=1)
    arrays = {n: np.ascontiguousarray(a) for n, a in arrays_of(**{k: np.asarray(a) for k, a in inputs.items()}).items()}
    io = {n: nc.dram_tensor(f"in_{n}", a.shape, F32, kind="ExternalInput").ap() for n, a in arrays.items()}
    io["out"] = nc.dram_tensor("out", (NBLK, P, D), F32, kind="ExternalOutput").ap()
    build(nc, io)
    r = run_bass_kernel_spmd(nc, [{f"in_{n}": a for n, a in arrays.items()}], core_ids=[0])
    return r.results[0]["out"].reshape(1, T, D)
```
